# Optimizing a Trainium2 kernel written in Bass

```python
import math
import jax, jax.numpy as jnp
from jax import lax
import numpy as np
import jax
import jax.numpy as jnp

D_MODEL = 1024
BATCH = 1
SEQ = 512
DEPTH = 1

GRID_W = 64
ATT_HEADS = 8
ATT_KV_HEADS = 2
ATT_HEAD_DIM = 64
ATT_WIDTH = ATT_HEADS * ATT_HEAD_DIM
ATT_KV_WIDTH = ATT_KV_HEADS * ATT_HEAD_DIM
Q_BLOCK = 128
ROPE_THETA = 10000.0
HG_HEADS = 4
HG_DK = 128
HG_DV = 128
HG_WIDTH_K = HG_HEADS * HG_DK
HG_WIDTH_V = HG_HEADS * HG_DV
HG_CHUNK = 64
N_BRANCH = 2
IN_SPLITS = (ATT_WIDTH, ATT_KV_WIDTH, ATT_KV_WIDTH,
             HG_WIDTH_K, HG_WIDTH_K, HG_WIDTH_K, HG_WIDTH_V, HG_WIDTH_V,
             N_BRANCH * D_MODEL)
IN_WIDTH = sum(IN_SPLITS)
PEER_HEADS = 8
PEER_NKEYS = 128
PEER_N_EXPERTS = PEER_NKEYS * PEER_NKEYS
PEER_DKEY = 256
PEER_TOPK = 16
PEER_TOKEN_BLOCK = 128
PLE_DIM = 256
EPS = 1e-6


def rmsnorm(x, g):
    xf = x.astype(jnp.float32)
    y = xf * lax.rsqrt(jnp.mean(xf * xf, axis=-1, keepdims=True) + EPS)
    return (y * g.astype(jnp.float32)).astype(x.dtype)

def axial_rope_tables(seq_len):
    rows = seq_len // GRID_W
    row = jnp.repeat(jnp.arange(rows), GRID_W).astype(jnp.float32)
    col = jnp.tile(jnp.arange(GRID_W), rows).astype(jnp.float32)
    axis_dim = ATT_HEAD_DIM // 2
    rot_half = axis_dim // 2
    inv = ROPE_THETA ** (-jnp.arange(rot_half, dtype=jnp.float32) / rot_half)
    ang = jnp.stack([row[:, None] * inv, col[:, None] * inv], axis=1)
    return jnp.cos(ang), jnp.sin(ang)

def apply_axial_rope(x, cos, sin):
    B, S, H, hd = x.shape
    xr = x.reshape(B, S, H, 2, 2, hd // 4).astype(jnp.float32)
    x1, x2 = xr[..., 0, :], xr[..., 1, :]
    c = cos[None, :, None]
    s = sin[None, :, None]
    out = jnp.stack([x1 * c - x2 * s, x1 * s + x2 * c], axis=-2)
    return out.reshape(B, S, H, hd).astype(x.dtype)

def gqa_attention(q, k, v):
    B, S = q.shape[:2]
    G = ATT_HEADS // ATT_KV_HEADS
    nb = S // Q_BLOCK
    scale = ATT_HEAD_DIM ** -0.5
    qb = q.reshape(B, nb, Q_BLOCK, ATT_KV_HEADS, G, ATT_HEAD_DIM).transpose(1, 0, 2, 3, 4, 5)

    def one_block(qblk):
        s = jnp.einsum('bqkgd,bskd->bkgqs', qblk, k, preferred_element_type=jnp.float32) * scale
        pr = jax.nn.softmax(s, axis=-1)
        return jnp.einsum('bkgqs,bskd->bqkgd', pr.astype(v.dtype), v)

    o = lax.map(one_block, qb)
    return o.transpose(1, 0, 2, 3, 4, 5).reshape(B, S, ATT_WIDTH)

def gla_chunk_scan(q, k, v, log_f):
    B, S, H, dk = q.shape
    dv = v.shape[-1]
    C = HG_CHUNK
    nc = S // C

    def to_chunks(a):
        return a.reshape(B, nc, C, H, a.shape[-1]).transpose(1, 0, 3, 2, 4)

    qc, kc, vc, gc = to_chunks(q), to_chunks(k), to_chunks(v), to_chunks(log_f)
    lower = jnp.tril(jnp.ones((C, C), dtype=bool))[:, :, None]

    def step(state, inp):
        qi, ki, vi, gi = inp
        b = jnp.cumsum(gi.astype(jnp.float32), axis=2)
        diff = b[:, :, :, None, :] - b[:, :, None, :, :]
        decay = jnp.exp(jnp.where(lower, diff, -jnp.inf))
        A = jnp.einsum('bhtd,bhsd,bhtsd->bhts', qi.astype(jnp.float32), ki.astype(jnp.float32), decay)
        o_intra = jnp.einsum('bhts,bhse->bhte', A, vi.astype(jnp.float32))
        o_inter = jnp.einsum('bhtd,bhde->bhte', qi.astype(jnp.float32) * jnp.exp(b), state)
        b_last = b[:, :, -1:, :]
        k_dec = ki.astype(jnp.float32) * jnp.exp(b_last - b)
        new_state = state * jnp.exp(b_last[:, :, 0, :])[..., None] + \
            jnp.einsum('bhsd,bhse->bhde', k_dec, vi.astype(jnp.float32))
        return new_state, o_intra + o_inter

    state0 = jnp.zeros((B, H, dk, dv), jnp.float32)
    _, o = lax.scan(step, state0, (qc, kc, vc, gc))
    return o.transpose(1, 0, 3, 2, 4).reshape(B, S, H, dv)

def hgrn2_bidirectional(hq, hf_f, hf_b, hi, hg, lb, out_norm):
    B, S = hq.shape[:2]
    q = jax.nn.silu(hq).reshape(B, S, HG_HEADS, HG_DK)
    i_in = hi.reshape(B, S, HG_HEADS, HG_DV)

    def gates(fpre, lbd):
        f = lbd + (1.0 - lbd) * jax.nn.sigmoid(fpre.astype(jnp.float32))
        f = f.reshape(B, S, HG_HEADS, HG_DK)
        return 1.0 - f, jnp.log(f)

    k_f, lf_f = gates(hf_f, lb[0])
    k_b, lf_b = gates(hf_b, lb[1])
    o_fwd = gla_chunk_scan(q, k_f, i_in, lf_f)
    flip = lambda a: jnp.flip(a, axis=1)
    o_bwd = flip(gla_chunk_scan(flip(q), flip(k_b), flip(i_in), flip(lf_b)))
    o = rmsnorm(o_fwd + o_bwd, out_norm)
    o = o * jax.nn.silu(hg.astype(jnp.float32).reshape(B, S, HG_HEADS, HG_DV))
    return o.reshape(B, S, HG_WIDTH_V).astype(hq.dtype)

def peer_ffn(h, w_q, sub_keys, u, v):
    B, S, D = h.shape
    T = B * S
    K = PEER_TOPK
    ht = h.reshape(T, D)
    q = (ht @ w_q).reshape(T, PEER_HEADS, 2, PEER_DKEY // 2)
    s = jnp.einsum('thpc,hpnc->thpn', q, sub_keys, preferred_element_type=jnp.float32)
    v1, i1 = lax.top_k(s[:, :, 0], K)
    v2, i2 = lax.top_k(s[:, :, 1], K)
    cand = (v1[..., :, None] + v2[..., None, :]).reshape(T, PEER_HEADS, K * K)
    cand_idx = (i1[..., :, None] * PEER_NKEYS + i2[..., None, :]).reshape(T, PEER_HEADS, K * K)
    top_s, pos = lax.top_k(cand, K)
    idx = jnp.take_along_axis(cand_idx, pos, axis=-1)
    g = jax.nn.softmax(top_s, axis=-1)
    nb = T // PEER_TOKEN_BLOCK

    def one_block(args):
        xb, ib, gb = args
        ue = jnp.take(u, ib, axis=0)
        a = jnp.einsum('thkd,td->thk', ue, xb, preferred_element_type=jnp.float32)
        w = jax.nn.gelu(a) * gb
        ve = jnp.take(v, ib, axis=0)
        return jnp.einsum('thk,thkd->td', w.astype(ve.dtype), ve)

    out = lax.map(one_block, (ht.reshape(nb, PEER_TOKEN_BLOCK, D),
                              idx.reshape(nb, PEER_TOKEN_BLOCK, PEER_HEADS, K),
                              g.reshape(nb, PEER_TOKEN_BLOCK, PEER_HEADS, K)))
    return out.reshape(B, S, D).astype(h.dtype)

def first_inputs(seed: int = 0) -> dict:
    key = jax.random.key(seed)
    ks = jax.random.split(key, 24)
    f32 = jnp.float32
    nrm = lambda k, shape, scale: jax.random.normal(k, shape, f32) * scale
    gain = lambda k, shape: 1.0 + 0.02 * jax.random.normal(k, shape, f32)
    return {
        "x": nrm(ks[0], (BATCH, SEQ, D_MODEL), 1.0),
        "p": nrm(ks[1], (DEPTH, BATCH, SEQ, PLE_DIM), 1.0),
        "norm_mix": gain(ks[2], (DEPTH, D_MODEL)),
        "w_in": nrm(ks[3], (DEPTH, D_MODEL, IN_WIDTH), D_MODEL ** -0.5),
        "q_norm": gain(ks[4], (DEPTH, ATT_HEAD_DIM)),
        "k_norm": gain(ks[5], (DEPTH, ATT_HEAD_DIM)),
        "hg_lb_raw": nrm(ks[6], (DEPTH + 1, 2, HG_WIDTH_K), 0.1),
        "hg_out_norm": gain(ks[7], (DEPTH, HG_DV)),
        "w_up_att": nrm(ks[8], (DEPTH, ATT_WIDTH, D_MODEL), ATT_WIDTH ** -0.5),
        "w_up_hg": nrm(ks[9], (DEPTH, HG_WIDTH_V, D_MODEL), HG_WIDTH_V ** -0.5),
        "w_out": nrm(ks[10], (DEPTH, D_MODEL, D_MODEL), D_MODEL ** -0.5),
        "norm_ffn": gain(ks[11], (DEPTH, D_MODEL)),
        "peer_wq": nrm(ks[12], (DEPTH, D_MODEL, PEER_HEADS * PEER_DKEY), D_MODEL ** -0.5),
        "peer_subkeys": nrm(ks[13], (DEPTH, PEER_HEADS, 2, PEER_NKEYS, PEER_DKEY // 2), (PEER_DKEY // 2) ** -0.5),
        "peer_u": nrm(ks[14], (DEPTH, PEER_N_EXPERTS, D_MODEL), D_MODEL ** -0.5),
        "peer_v": nrm(ks[15], (DEPTH, PEER_N_EXPERTS, D_MODEL), 0.3),
        "norm_ple": gain(ks[16], (DEPTH, D_MODEL)),
        "ple_gate": nrm(ks[17], (DEPTH, D_MODEL, D_MODEL), D_MODEL ** -0.5),
        "ple_proj": nrm(ks[18], (DEPTH, PLE_DIM, D_MODEL), PLE_DIM ** -0.5),
    }

def first_block(x, p, norm_mix, w_in, q_norm, k_norm, hg_lb_raw, hg_out_norm, w_up_att, w_up_hg,
              w_out, norm_ffn, peer_wq, peer_subkeys, peer_u, peer_v, norm_ple, ple_gate, ple_proj):
    B, S, D = x.shape
    cos, sin = axial_rope_tables(S)
    lb_all = jnp.cumsum(jax.nn.softmax(hg_lb_raw.astype(jnp.float32), axis=0), axis=0)
    offsets = [int(o) for o in np.cumsum(IN_SPLITS)[:-1]]
    for i in range(DEPTH):
        h = rmsnorm(x, norm_mix[i])
        proj = h @ w_in[i]
        aq, ak, av, hq, hf_f, hf_b, hi, hg, gate_pre = jnp.split(proj, offsets, axis=-1)
        q = rmsnorm(aq.reshape(B, S, ATT_HEADS, ATT_HEAD_DIM), q_norm[i])
        k = rmsnorm(ak.reshape(B, S, ATT_KV_HEADS, ATT_HEAD_DIM), k_norm[i])
        v = av.reshape(B, S, ATT_KV_HEADS, ATT_HEAD_DIM)
        q = apply_axial_rope(q, cos, sin)
        k = apply_axial_rope(k, cos, sin)
        y_att = gqa_attention(q, k, v) @ w_up_att[i]
        y_hg = hgrn2_bidirectional(hq, hf_f, hf_b, hi, hg, lb_all[i], hg_out_norm[i]) @ w_up_hg[i]
        gts = jax.nn.sigmoid(gate_pre.astype(jnp.float32)).reshape(B, S, N_BRANCH, D)
        merged = (gts[:, :, 0] * y_att + gts[:, :, 1] * y_hg).astype(x.dtype)
        x = x + merged @ w_out[i]
        x = x + peer_ffn(rmsnorm(x, norm_ffn[i]), peer_wq[i], peer_subkeys[i], peer_u[i], peer_v[i])
        g_ple = jax.nn.sigmoid(rmsnorm(x, norm_ple[i]) @ ple_gate[i])
        x = x + g_ple * (p[i] @ ple_proj[i])
    return x


DEPTH_2 = 2

MIX_A = D_MODEL // 2
RET_HEADS = 4
RET_HEAD_DIM = (D_MODEL - MIX_A) // RET_HEADS
RET_WIDTH = RET_HEADS * RET_HEAD_DIM
IN_COLS = 2 * MIX_A + 4 * RET_WIDTH
CONV_WIDTH = 31
RET_CHUNK = 128
ROPE_BASE = 10000.0
S5_GROUP = 16
S5_GROUPS = D_MODEL // S5_GROUP
S5_STATE = 64
D_FF = 4 * D_MODEL
N_EVEN = (DEPTH_2 + 1) // 2
N_ODD = DEPTH_2 // 2


def _rmsnorm(x, g):
    xf = x.astype(jnp.float32)
    y = xf * lax.rsqrt(jnp.mean(xf * xf, axis=-1, keepdims=True) + EPS)
    return (y * g.astype(jnp.float32)).astype(x.dtype)

def _head_rmsnorm(x):
    xf = x.astype(jnp.float32)
    y = xf * lax.rsqrt(jnp.mean(xf * xf, axis=-1, keepdims=True) + EPS)
    return y.astype(x.dtype)

def _layernorm(x, g, b):
    xf = x.astype(jnp.float32)
    mu = jnp.mean(xf, axis=-1, keepdims=True)
    xc = xf - mu
    var = jnp.mean(xc * xc, axis=-1, keepdims=True)
    y = xc * lax.rsqrt(var + EPS) * g.astype(jnp.float32) + b.astype(jnp.float32)
    return y.astype(x.dtype)

def _rotary(t, cos, sin):
    half = t.shape[-1] // 2
    t1, t2 = t[..., :half], t[..., half:]
    cos = cos.astype(t.dtype)
    sin = sin.astype(t.dtype)
    return jnp.concatenate([t1 * cos - t2 * sin, t1 * sin + t2 * cos], axis=-1)

def _retention_bidir(q, k, v):
    bsz, seq, nh, dh = q.shape
    L = RET_CHUNK
    n = seq // L
    dt = q.dtype
    q = q.reshape(bsz, n, L, nh, dh)
    k = k.reshape(bsz, n, L, nh, dh)
    v = v.reshape(bsz, n, L, nh, dh)
    log_g = jnp.log1p(-jnp.exp2(-5.0 - jnp.arange(nh, dtype=jnp.float32)))
    idx = jnp.arange(L, dtype=jnp.float32)
    dist = jnp.abs(idx[:, None] - idx[None, :])
    dmat = jnp.exp(log_g[:, None, None] * dist).astype(dt)
    scores = jnp.einsum('bnihd,bnjhd->bnhij', q, k) * dmat[None, None]
    intra = jnp.einsum('bnhij,bnjhe->bnihe', scores, v)
    w_kf = jnp.exp(log_g[None, :] * (L - 1.0 - idx)[:, None]).astype(dt)
    w_kb = jnp.exp(log_g[None, :] * idx[:, None]).astype(dt)
    kv_f = jnp.einsum('bnjhd,jh,bnjhe->nbhde', k, w_kf, v)
    kv_b = jnp.einsum('bnjhd,jh,bnjhe->nbhde', k, w_kb, v)
    g_L = jnp.exp(log_g * L).astype(dt)[None, :, None, None]

    def step(state, kv):
        return g_L * state + kv, state

    init = jnp.zeros((bsz, nh, dh, dh), dtype=kv_f.dtype)
    _, s_f = lax.scan(step, init, kv_f)
    _, s_b = lax.scan(step, init, kv_b, reverse=True)
    w_qf = jnp.exp(log_g[None, :] * (idx + 1.0)[:, None]).astype(dt)
    w_qb = jnp.exp(log_g[None, :] * (L - idx)[:, None]).astype(dt)
    inter = (jnp.einsum('bnihd,ih,nbhde->bnihe', q, w_qf, s_f)
             + jnp.einsum('bnihd,ih,nbhde->bnihe', q, w_qb, s_b))
    return (intra + inter).reshape(bsz, seq, nh, dh)

def _mixer_conv_retention(h, w_in, conv_w, conv_b, cln_g, cln_b, w_out):
    bsz, seq, _ = h.shape
    proj = h @ w_in
    splits = [MIX_A, 2 * MIX_A, 2 * MIX_A + RET_WIDTH,
              2 * MIX_A + 2 * RET_WIDTH, 2 * MIX_A + 3 * RET_WIDTH]
    a_val, a_gate, q, k, v, g = jnp.split(proj, splits, axis=-1)
    a = a_val * jax.nn.sigmoid(a_gate)
    a = lax.conv_general_dilated(
        a, conv_w[:, None, :].astype(a.dtype), window_strides=(1,), padding='SAME',
        dimension_numbers=('NWC', 'WIO', 'NWC'), feature_group_count=MIX_A)
    a = jax.nn.silu(_layernorm(a + conv_b, cln_g, cln_b))
    q = q.reshape(bsz, seq, RET_HEADS, RET_HEAD_DIM)
    k = k.reshape(bsz, seq, RET_HEADS, RET_HEAD_DIM)
    v = v.reshape(bsz, seq, RET_HEADS, RET_HEAD_DIM)
    inv = ROPE_BASE ** (-jnp.arange(0, RET_HEAD_DIM, 2, dtype=jnp.float32) / RET_HEAD_DIM)
    ang = jnp.arange(seq, dtype=jnp.float32)[:, None] * inv[None, :]
    cos, sin = jnp.cos(ang)[:, None, :], jnp.sin(ang)[:, None, :]
    q = _rotary(q, cos, sin) * (RET_HEAD_DIM ** -0.5)
    k = _rotary(k, cos, sin)
    r = _head_rmsnorm(_retention_bidir(q, k, v)).reshape(bsz, seq, RET_WIDTH)
    r = jax.nn.silu(g) * r
    return jnp.concatenate([a, r], axis=-1) @ w_out

def _s5_combine(e1, e2):
    a1r, a1i, b1r, b1i = e1
    a2r, a2i, b2r, b2i = e2
    ar = a2r * a1r - a2i * a1i
    ai = a2r * a1i + a2i * a1r
    br = a2r * b1r - a2i * b1i + b2r
    bi = a2r * b1i + a2i * b1r + b2i
    return ar, ai, br, bi

def _mixer_s5(h, lam_re, lam_im, log_step, b_re, b_im, c_re, c_im, d_skip, w_glu_a, w_glu_b):
    bsz, seq, dm = h.shape
    f32 = jnp.float32
    u = h.astype(f32)
    ug = u.reshape(bsz, seq, S5_GROUPS, S5_GROUP)
    lr = jnp.minimum(lam_re.astype(f32), -1e-4)
    li = lam_im.astype(f32)
    dt = jnp.exp(log_step.astype(f32))[..., None]
    mag = jnp.exp(lr * dt)
    ab_re, ab_im = mag * jnp.cos(li * dt), mag * jnp.sin(li * dt)
    den = lr * lr + li * li
    nr, ni = ab_re - 1.0, ab_im
    f_re = (nr * lr + ni * li) / den
    f_im = (ni * lr - nr * li) / den
    br_, bi_ = b_re.astype(f32), b_im.astype(f32)
    bb_re = f_re[..., None] * br_ - f_im[..., None] * bi_
    bb_im = f_re[..., None] * bi_ + f_im[..., None] * br_
    cr, ci = c_re.astype(f32), c_im.astype(f32)

    def one_sequence(us):
        y = jnp.zeros_like(us)
        for direction in (0, 1):
            bu_re = jnp.einsum('sgc,gpc->sgp', us, bb_re[direction])
            bu_im = jnp.einsum('sgc,gpc->sgp', us, bb_im[direction])
            a_re = jnp.broadcast_to(ab_re[direction], bu_re.shape)
            a_im = jnp.broadcast_to(ab_im[direction], bu_re.shape)
            _, _, h_re, h_im = lax.associative_scan(
                _s5_combine, (a_re, a_im, bu_re, bu_im), reverse=(direction == 1), axis=0)
            y = y + (jnp.einsum('sgp,gcp->sgc', h_re, cr[direction])
                     - jnp.einsum('sgp,gcp->sgc', h_im, ci[direction]))
        return y

    y = lax.map(one_sequence, ug).reshape(bsz, seq, dm)
    y = (y + d_skip.astype(f32) * u).astype(h.dtype)
    z = jax.nn.gelu(y)
    return (z @ w_glu_a) * jax.nn.sigmoid(z @ w_glu_b)

def second_inputs(seed: int = 0) -> dict:
    key = jax.random.key(seed)
    ks = jax.random.split(key, 32)
    f32 = jnp.float32

    def nrm(k, shape, scale):
        return jax.random.normal(k, shape, f32) * scale

    P, G, Cg = S5_STATE, S5_GROUPS, S5_GROUP
    return {
        "x": nrm(ks[0], (BATCH, SEQ, D_MODEL), 1.0),
        "c": nrm(ks[1], (BATCH, D_MODEL), 1.0),
        "norm_g": 1.0 + nrm(ks[2], (DEPTH_2, 2, D_MODEL), 0.05),
        "ada_w": nrm(ks[3], (DEPTH_2, D_MODEL, 6 * D_MODEL), 0.5 * D_MODEL ** -0.5),
        "ada_b": nrm(ks[4], (DEPTH_2, 6 * D_MODEL), 0.02),
        "w_in": nrm(ks[5], (N_EVEN, D_MODEL, IN_COLS), D_MODEL ** -0.5),
        "conv_w": nrm(ks[6], (N_EVEN, CONV_WIDTH, MIX_A), CONV_WIDTH ** -0.5),
        "conv_b": nrm(ks[7], (N_EVEN, MIX_A), 0.02),
        "cln_g": 1.0 + nrm(ks[8], (N_EVEN, MIX_A), 0.05),
        "cln_b": nrm(ks[9], (N_EVEN, MIX_A), 0.02),
        "w_out": nrm(ks[10], (N_EVEN, MIX_A + RET_WIDTH, D_MODEL), (MIX_A + RET_WIDTH) ** -0.5),
        "s5_lam_re": -0.5 + nrm(ks[11], (N_ODD, 2, G, P), 0.01),
        "s5_lam_im": math.pi * jnp.arange(P, dtype=f32) + nrm(ks[12], (N_ODD, 2, G, P), 0.01),
        "s5_log_step": jax.random.uniform(ks[13], (N_ODD, 2, G), f32,
                                          math.log(1e-3), math.log(1e-1)),
        "s5_b_re": nrm(ks[14], (N_ODD, 2, G, P, Cg), (2 * Cg) ** -0.5),
        "s5_b_im": nrm(ks[15], (N_ODD, 2, G, P, Cg), (2 * Cg) ** -0.5),
        "s5_c_re": nrm(ks[16], (N_ODD, 2, G, Cg, P), 0.5),
        "s5_c_im": nrm(ks[17], (N_ODD, 2, G, Cg, P), 0.5),
        "s5_d": nrm(ks[18], (N_ODD, D_MODEL), 1.0),
        "w_glu_a": nrm(ks[19], (N_ODD, D_MODEL, D_MODEL), D_MODEL ** -0.5),
        "w_glu_b": nrm(ks[20], (N_ODD, D_MODEL, D_MODEL), D_MODEL ** -0.5),
        "w_fc1": nrm(ks[21], (DEPTH_2, D_MODEL, D_FF), D_MODEL ** -0.5),
        "w_fc2": nrm(ks[22], (DEPTH_2, D_FF, D_MODEL), D_FF ** -0.5),
        "norm_f": 1.0 + nrm(ks[23], (D_MODEL,), 0.05),
    }

def second_block(x, c, norm_g, ada_w, ada_b, w_in, conv_w, conv_b, cln_g, cln_b, w_out,
              s5_lam_re, s5_lam_im, s5_log_step, s5_b_re, s5_b_im, s5_c_re, s5_c_im, s5_d,
              w_glu_a, w_glu_b, w_fc1, w_fc2, norm_f):
    c_act = jax.nn.silu(c)
    for layer in range(DEPTH_2):
        mod = (c_act @ ada_w[layer] + ada_b[layer])[:, None, :]
        shift_m, scale_m, gate_m, shift_f, scale_f, gate_f = jnp.split(mod, 6, axis=-1)
        h = _rmsnorm(x, norm_g[layer, 0]) * (1.0 + scale_m) + shift_m
        if layer % 2 == 0:
            i = layer // 2
            mix = _mixer_conv_retention(h, w_in[i], conv_w[i], conv_b[i], cln_g[i],
                                        cln_b[i], w_out[i])
        else:
            i = layer // 2
            mix = _mixer_s5(h, s5_lam_re[i], s5_lam_im[i], s5_log_step[i], s5_b_re[i],
                            s5_b_im[i], s5_c_re[i], s5_c_im[i], s5_d[i],
                            w_glu_a[i], w_glu_b[i])
        x = x + gate_m * mix
        h = _rmsnorm(x, norm_g[layer, 1]) * (1.0 + scale_f) + shift_f
        x = x + gate_f * (jnp.square(jax.nn.relu(h @ w_fc1[layer])) @ w_fc2[layer])
    return _rmsnorm(x, norm_f)


def setup_inputs(seed=0):
    out = dict(first_inputs(seed))
    for name, value in second_inputs(seed + 1).items():
        if name != "x":
            out[name + "_2"] = value
    return out


def reference(
    x, p, norm_mix, w_in, q_norm, k_norm, hg_lb_raw, hg_out_norm, w_up_att, w_up_hg, w_out,
    norm_ffn, peer_wq, peer_subkeys, peer_u, peer_v, norm_ple, ple_gate, ple_proj, c_2,
    norm_g_2, ada_w_2, ada_b_2, w_in_2, conv_w_2, conv_b_2, cln_g_2, cln_b_2, w_out_2,
    s5_lam_re_2, s5_lam_im_2, s5_log_step_2, s5_b_re_2, s5_b_im_2, s5_c_re_2, s5_c_im_2, s5_d_2,
    w_glu_a_2, w_glu_b_2, w_fc1_2, w_fc2_2, norm_f_2,
):
    x = first_block(
        x, p, norm_mix, w_in, q_norm, k_norm, hg_lb_raw, hg_out_norm, w_up_att, w_up_hg, w_out,
        norm_ffn, peer_wq, peer_subkeys, peer_u, peer_v, norm_ple, ple_gate, ple_proj,
    )
    return second_block(
        x, c_2, norm_g_2, ada_w_2, ada_b_2, w_in_2, conv_w_2, conv_b_2, cln_g_2, cln_b_2,
        w_out_2, s5_lam_re_2, s5_lam_im_2, s5_log_step_2, s5_b_re_2, s5_b_im_2, s5_c_re_2,
        s5_c_im_2, s5_d_2, w_glu_a_2, w_glu_b_2, w_fc1_2, w_fc2_2, norm_f_2,
    )


_drawn_inputs = setup_inputs


def setup_inputs(seed=0):
    import zlib

    import numpy as np

    out = dict(_drawn_inputs(seed))
    spreads = {}
    factors = {'norm_mix': 3.305,
     'q_norm': 8.0,
     'k_norm': 8.0,
     'hg_lb_raw': 6.599,
     'hg_out_norm': 11.364,
     'norm_ffn': 20.522,
     'norm_ple': 200.0,
     'conv_b_2': 8.0,
     'cln_g_2': 48.471,
     'cln_b_2': 200.0,
     's5_lam_re_2': 200.0,
     'norm_g_2': 4.999,
     'ada_b_2': 3.746,
     's5_lam_im_2': 64.0,
     's5_log_step_2': 64.0,
     's5_b_re_2': 64.0,
     's5_b_im_2': 64.0,
     's5_c_re_2': 64.0,
     's5_c_im_2': 64.0,
     's5_d_2': 3.492,
     'w_glu_a_2': 3.038,
     'w_glu_b_2': 8.0}
    for name, (base, spread) in spreads.items():
        noise = np.random.default_rng([zlib.crc32(name.encode()), seed]).standard_normal(out[name].shape)
        drawn = base * np.exp(spread * noise) if base else spread * noise
        out[name] = jnp.asarray(drawn.astype(out[name].dtype))
    for name, factor in factors.items():
        out[name] = (out[name] * factor).astype(out[name].dtype)
    return out
```

```python
from contextlib import ExitStack

import numpy as np

import concourse.bass as bass
from concourse import mybir

F32 = mybir.dt.float32
U32 = mybir.dt.uint32
ALU = mybir.AluOpType
ACT = mybir.ActivationFunctionType
AX = mybir.AxisListType

P = 128
S = 512
D = 1024
KT = D // P
TT = S // P
EPS = 1e-6

AH, AKV, AD = 8, 2, 64
GH, GD = 4, 128
GC, GB = 64, 16
NCH, NBL = S // GC, GC // GB
PH, PK, PN, PX = 8, 16, 128, 128 * 128
RH = 4
MA = D // 2
CW = 31
FF = 4 * D
SG, SC, SP = 64, 16, 64
ST = 8
SN = S // ST
SB = 8
NEG = -3.0e38
ROUND = 12582912.0

COLS = [("norm_mix", KT), ("norm_ffn", KT), ("norm_ple", KT), ("q_norm", 1), ("k_norm", 1),
        ("hg_out_norm", 1), ("lb_raw", 16), ("norm_g", 4 * KT), ("ada_b", 12 * KT), ("conv_b", 4),
        ("cln_g", 4), ("cln_b", 4), ("conv_w", 4 * CW), ("norm_f", KT), ("c", KT),
        ("s5_lr", 2 * SG), ("s5_li", 2 * SG), ("s5_step", 2 * SG)]
COL_AT = {}
_n = 0
for _name, _k in COLS:
    COL_AT[_name] = (_n, _k)
    _n += _k
N_COLS = _n

CONSTS = [("ident", P), ("ones", P), ("ones64", P), ("rot_att", P), ("rot_ret", P), ("swap_s5", P),
          ("sign", 2), ("reset", 2 * S), ("causal", 2 * TT * GC), ("cos_att", S), ("sin_att", S),
          ("cos_ret", S), ("sin_ret", S), ("decay", RH * TT * S), ("iota16", PK),
          ("chunk_no", 2 * SB * SN), ("chunk_keep", 2 * SB * SN), ("power_b", 2 * SG * ST),
          ("power_c", 2 * SG * ST)]
CONST_AT = {}
_n = 0
for _name, _k in CONSTS:
    CONST_AT[_name] = (_n, _k)
    _n += _k
N_CONSTS = _n


def constants():
    t = {}
    t["ident"] = np.eye(P)
    t["ones"] = np.ones((P, P))
    t["ones64"] = np.kron(np.eye(2), np.ones((64, 64)))
    pos = np.arange(S)
    inv = (np.float32(10000.0) ** (-np.arange(16, dtype=np.float32) / np.float32(16))).astype(np.float32)
    axis = np.stack([pos // 64, pos % 64]).astype(np.float32)
    ang = (axis[:, None, :] * inv[None, :, None]).astype(np.float32).astype(np.float64)
    ang = np.broadcast_to(ang[:, None], (2, 2, 16, S)).reshape(64, S)
    t["cos_att"], t["sin_att"] = (np.tile(f(ang), (2, 1)) for f in (np.cos, np.sin))
    rot = np.zeros((P, P))
    for c in range(P):
        if (c // 16) % 2 == 0:
            rot[c + 16, c] = -1.0
        else:
            rot[c - 16, c] = 1.0
    t["rot_att"] = rot
    inv = (np.float32(10000.0) ** (-np.arange(0, P, 2, dtype=np.float32) / np.float32(P))).astype(np.float32)
    ang = (pos[None, :].astype(np.float32) * inv[:, None]).astype(np.float32).astype(np.float64)
    t["cos_ret"], t["sin_ret"] = (np.tile(f(ang), (2, 1)) for f in (np.cos, np.sin))
    rot = np.zeros((P, P))
    swap = np.zeros((P, P))
    for c in range(64):
        rot[c + 64, c], rot[c, c + 64] = -1.0, 1.0
        swap[c + 64, c], swap[c, c + 64] = 1.0, -1.0
    t["rot_ret"], t["swap_s5"] = rot, swap
    sign = np.ones((P, 2))
    sign[:64, 0] = -1.0
    sign[64:, 1] = -1.0
    t["sign"] = sign
    reset = np.ones((2, S))
    reset[0, 0::GC] = 0.0
    reset[1, GC - 1::GC] = 0.0
    t["reset"] = np.broadcast_to(reset.reshape(-1), (P, 2 * S))
    s = np.arange(P) % GC
    c = np.arange(GC)
    mask = np.stack([s[:, None] <= c[None], s[:, None] >= c[None]], 1).astype(float)
    t["causal"] = np.broadcast_to(mask[:, :, None], (P, 2, TT, GC)).reshape(P, -1)
    lg = np.log1p(-np.exp2(-5.0 - np.arange(RH)))
    m = np.arange(P)[:, None] + P * np.arange(TT)[None]
    t["decay"] = np.exp(lg[None, :, None, None] * np.abs(m[:, None, :, None] - pos)).reshape(P, -1)
    t["iota16"] = np.broadcast_to(np.arange(PK), (P, PK))
    no = np.arange(SN)
    t["chunk_no"] = np.broadcast_to(np.stack([no, SN - 1 - no])[:, None], (2, SB, SN)).reshape(1, -1)
    keep = np.ones((2, SN))
    keep[0, 0] = keep[1, -1] = 0.0
    t["chunk_keep"] = np.broadcast_to(keep[:, None], (2, SB, SN)).reshape(1, -1)
    d = np.arange(ST)
    t["power_b"] = np.broadcast_to(np.stack([ST - 1 - d, d])[:, None], (2, SG, ST)).reshape(1, -1)
    t["power_c"] = np.broadcast_to(np.stack([d + 1, ST - d])[:, None], (2, SG, ST)).reshape(1, -1)
    out = np.concatenate([np.broadcast_to(t[n], (P, k)) for n, k in CONSTS], 1)
    return np.ascontiguousarray(out, dtype=np.float32)


def wait_apart(eng, sem, value, passed):
    eng.wait_ge(sem, value)
    eng.sem_inc(passed, 1)


class Steps:

    def __init__(self, eng, sem):
        self.eng, self.sem, self.base, self.n = eng, sem, 0, 0

    def mark(self, ins):
        self.n += 1
        ins.then_inc(self.sem, 1)

    def wait(self, lag=0):
        self.eng.wait_ge(self.sem, self.base + (self.n - lag))

    def __call__(self, ins):
        self.mark(ins)
        self.wait()

    def enter(self, i, per):
        self.start, self.per = self.base + self.n, per
        self.base, self.n = i * per + self.start, 0

    def leave(self, count):
        assert self.n == self.per, (self.n, self.per)
        self.base, self.n = self.start + count * self.per, 0


class Core:

    def __init__(self, nc, dram):
        self.nc, self.dram, self.stages, self.spent = nc, dram, 0, []

    def const(self, name):
        at, n = CONST_AT[name]
        return self.dram["consts"][:, at:at + n]

    def col(self, name, at=0, n=None):
        a, k = COL_AT[name]
        return self.cols[:, a + at:a + at + (k - at if n is None else n)]


class Stage:

    def __init__(self, core):
        core.stages += 1
        self.nc, self.ctx, self.tag = core.nc, ExitStack(), f"_{core.stages}"
        self.sems, self.core = [], core

    def __enter__(self):
        if len(self.nc.free_semaphores) < 60 and self.core.spent:
            self.nc.clear_and_free_semaphores(self.core.spent)
            self.nc.all_engine_barrier()
            self.core.spent = []
        self.ctx.__enter__()
        return self

    def __exit__(self, *a):
        self.ctx.__exit__(*a)
        self.core.spent += self.sems

    def sb(self, name, shape, dt=F32):
        return self.ctx.enter_context(self.nc.sbuf_tensor(name + self.tag, shape, dt))

    def ps(self, name, shape):
        return self.ctx.enter_context(self.nc.psum_tensor(name + self.tag, shape, F32))

    def sem(self, name):
        self.sems.append(self.nc.alloc_semaphore(name + self.tag))
        return self.sems[-1]

    def block(self):
        return self.ctx.enter_context(self.nc.Block())


def load_stage(core):
    with Stage(core) as st:
        landed = st.sem("landed")
        block = st.block()

        @block.sync
        def _(sp):
            loads = [(core.xT[:, :, :], core.dram["xT"].rearrange("p (k s) -> p k s", k=KT)),
                     (core.cols[:, :], core.dram["cols"][:, :])]
            for name, tile in core.mats.items():
                loads.append((tile[:, :], core.const(name)))
            for dst, src in loads:
                sp.dma_start(dst, src).then_inc(landed, 16)
            sp.wait_ge(landed, 16 * len(loads))


def linear(core, w, kt, width, chunks, src, evac, token_major=False, engine="scalar", after=None):
    banks = TT if token_major else width // P
    n = width if token_major else S
    with Stage(core) as st:
        ring = st.sb("ring", [P, 2, kt * width])
        acc = st.ps("acc", [P, 2, 4, 512])
        landed = [st.sem("landed0"), st.sem("landed1")]
        multiplied, slot_free = st.sem("multiplied"), st.sem("slot_free")
        block = st.block()

        @block.sync
        def _(sp):
            for s in range(2):
                sp.dma_start(ring[:, s, :], w[s * P:(s + 1) * P, :]).then_inc(landed[s], 16)
            if chunks > 2:
                with sp.Fori(1, chunks // 2) as i:
                    for s in range(2):
                        sp.wait_ge(multiplied, i * 2 - 1 + s)
                        sp.dma_start(ring[:, s, :], w[bass.ds((i * 2 + s) * P, P), :]).then_inc(landed[s], 16)

        def multiply(pe, s):
            for j in range(banks):
                for k in range(kt):
                    wk = ring[:, s, k * width:(k + 1) * width]
                    if token_major:
                        lhsT, rhs = src[:, k, j * P:(j + 1) * P], wk
                    else:
                        lhsT, rhs = wk[:, j * P:(j + 1) * P], src[:, k, :]
                    last = pe.matmul(acc[:, s, j, 0:n], lhsT, rhs, start=(k == 0), stop=(k == kt - 1))
            last.then_inc(multiplied, 1)

        @block.tensor
        def _(pe):
            for s in range(2):
                pe.wait_ge(landed[s], 16)
                multiply(pe, s)
            if chunks > 2:
                with pe.Fori(1, chunks // 2) as i:
                    for s in range(2):
                        pe.wait_ge(landed[s], i * 16 + 16)
                        pe.wait_ge(slot_free, i * 2 - 1 + s)
                        multiply(pe, s)

        def take_out(eng):
            with eng.Fori(0, chunks // 2) as i:
                for s in range(2):
                    eng.wait_ge(multiplied, i * 2 + 1 + s)
                    for j in range(banks):
                        last = evac(eng, i * 2 + s, j, acc[:, s, j, 0:n])
                    last.then_inc(slot_free, 1)

        if after is not None:
            @block.vector
            def _(dve):
                with dve.Fori(0, chunks // 2) as i:
                    for s in range(2):
                        dve.wait_ge(slot_free, i * 2 + 1 + s)
                        after(dve, i * 2 + s)

        if engine == "scalar":
            @block.scalar
            def _(act):
                take_out(act)
        else:
            @block.vector
            def _(dve):
                take_out(dve)


def tiles_to(dst, per, func=None, scale=1.0):
    def evac(act, c, j, bank):
        out = dst[:, bass.ds(c * per + j, 1), :].rearrange("p a s -> p (a s)")
        return act.activation(out, bank, func or ACT.Copy, scale=scale)
    return evac


def tokens_to(dst, width):
    def evac(act, c, j, bank):
        return act.activation(dst[:, j, bass.ds(c * width, width)], bank, ACT.Copy)
    return evac


def add_to_x(core, per, gate=None, gate_at=0):
    def evac(dve, c, j, bank):
        x = core.xT[:, bass.ds(c * per + j, 1), :].rearrange("p a s -> p (a s)")
        if gate is None:
            return dve.tensor_tensor(x, bank, x, ALU.add)
        return dve.scalar_tensor_tensor(x, bank, gate[:, bass.ds(c * per + j + gate_at, 1)], x,
                                        ALU.mult, ALU.add)
    return evac


def norm(core, gain, bias=None, out=None):
    out = core.hT if out is None else out
    with Stage(core) as st:
        sq = st.sb("sq", [P, KT, S])
        rstd = st.sb("rstd", [P, S])
        ms = st.ps("ms", [P, S])
        squared, summed, v_step, rooted = (st.sem(n) for n in ("squared", "summed", "v_step", "rooted"))
        scaled = st.sem("scaled")
        block = st.block()

        @block.scalar
        def _(act):
            for k in range(KT):
                act.activation(sq[:, k, :], core.xT[:, k, :], ACT.Square).then_inc(squared, 1)
            act.wait_ge(v_step, 1)
            act.activation(rstd[:, :], rstd[:, :], ACT.Sqrt).then_inc(rooted, 1)
            if bias is not None:
                for k in range(KT):
                    act.wait_ge(scaled, k + 1)
                    act.activation(out[:, k, :], out[:, k, :], ACT.Identity, bias=bias[:, k:k + 1])

        @block.tensor
        def _(pe):
            for k in range(KT):
                pe.wait_ge(squared, k + 1)
                last = pe.matmul(ms[:, :], core.mats["ones"][:, :], sq[:, k, :], start=(k == 0), stop=(k == KT - 1))
            last.then_inc(summed, 1)

        @block.vector
        def _(dve):
            step = Steps(dve, v_step)
            dve.wait_ge(summed, 1)
            step(dve.tensor_scalar(rstd[:, :], ms[:, :], 1.0 / D, EPS, ALU.mult, ALU.add))
            dve.wait_ge(rooted, 1)
            step(dve.reciprocal(rstd[:, :], rstd[:, :]))
            for k in range(KT):
                dve.scalar_tensor_tensor(out[:, k, :], core.xT[:, k, :], gain[:, k:k + 1], rstd[:, :],
                                         ALU.mult, ALU.mult).then_inc(scaled, 1)


def attention(core, qT, kT, v, yT):
    UNITS = [(a, t) for a in range(2) for t in range(TT)]
    with Stage(core) as st:
        cs = st.sb("cs", [P, 2, S])
        kr = st.sb("kr", [P, S])
        qr = st.sb("qr", [P, S])
        sq, xn, a1, a2, rstd = (st.sb(n, [P, S]) for n in ("sq", "xn", "a1", "a2", "rstd"))
        prob = st.sb("prob", [P, 2, S])
        probT = st.sb("probT", [P, TT, 2, S])
        stat = st.sb("stat", [P, 3, 8])
        pn = st.ps("pn", [P, S])
        pr = st.ps("pr", [P, S])
        sc = st.ps("sc", [P, 2, S])
        pt = st.ps("pt", [P, 2, S])
        po = st.ps("po", [P, 2, S])
        landed, squared, summed, v_step, rooted, normed, turned, rotated = (
            st.sem(n) for n in ("landed", "squared", "summed", "v_step", "rooted", "normed", "turned", "rotated"))
        st_unit = st.sem("unit_step")
        scored, maxed, expd, scaled, transposed, copied, mixed, out_done = (
            st.sem(n) for n in ("scored", "maxed", "expd", "scaled", "transposed", "copied", "mixed", "out_done"))
        block = st.block()

        @block.sync
        def _(sp):
            sp.dma_start(cs[:, 0, :], core.const("cos_att")).then_inc(landed, 16)
            sp.dma_start(cs[:, 1, :], core.const("sin_att")).then_inc(landed, 16)

        def turn_tensor(pe, n):
            pe.wait_ge(squared, n)
            pe.matmul(pn[:, :], core.mats["ones64"][:, :], sq[:, :], start=True, stop=True).then_inc(summed, 1)
            pe.wait_ge(normed, n)
            pe.matmul(pr[:, :], core.mats["rot_att"][:, :], xn[:, :], start=True, stop=True).then_inc(turned, 1)

        def turn_scalar(act, n, src):
            act.activation(sq[:, :], src, ACT.Square).then_inc(squared, 1)
            act.wait_ge(v_step, (n - 1) * 4 + 1)
            act.activation(rstd[:, :], rstd[:, :], ACT.Sqrt).then_inc(rooted, 1)

        def turn_vector(dve, step, n, src, gain, dst):
            dve.wait_ge(summed, n)
            step(dve.tensor_scalar(rstd[:, :], pn[:, :], 1.0 / AD, EPS, ALU.mult, ALU.add))
            dve.wait_ge(rooted, n)
            step(dve.reciprocal(rstd[:, :], rstd[:, :]))
            dve.scalar_tensor_tensor(xn[:, :], src, gain, rstd[:, :], ALU.mult, ALU.mult).then_inc(normed, 1)
            dve.wait_ge(normed, n)
            step(dve.tensor_tensor(a1[:, :], xn[:, :], cs[:, 0, :], ALU.mult))
            dve.wait_ge(turned, n)
            step(dve.tensor_tensor(a2[:, :], pr[:, :], cs[:, 1, :], ALU.mult))
            dve.tensor_tensor(dst, a1[:, :], a2[:, :], ALU.add).then_inc(rotated, 1)

        def q_tile(j):
            return qT[:, bass.ds(j, 1), :].rearrange("p a s -> p (a s)")

        @block.tensor
        def _(pe):
            turn_tensor(pe, 1)
            with pe.Fori(0, 4) as j:
                turn_tensor(pe, j + 2)
                pe.wait_ge(rotated, j + 2)

                def transposes(u):
                    a, t = UNITS[u]
                    pe.wait_ge(scaled, j * 8 + (u + 1))
                    if u >= 2:
                        pe.wait_ge(copied, j * 8 + (u - 1))
                    for b in range(TT):
                        last = pe.transpose(pt[:, u % 2, b * P:(b + 1) * P], prob[:, u % 2, b * P:(b + 1) * P],
                                            core.mats["ident"][:, :])
                    last.then_inc(transposed, 1)

                def mix(a):
                    pe.wait_ge(copied, j * 8 + (4 * a + 4))
                    for b in range(TT):
                        last = pe.matmul(po[64 * a:64 * a + 64, a, :], v[:, b, 64 * a:64 * a + 64],
                                         probT[:, b, a, :], start=(b == 0), stop=(b == TT - 1))
                    last.then_inc(mixed, 1)

                for u, (a, t) in enumerate(UNITS):
                    if u >= 2:
                        pe.wait_ge(expd, j * 8 + (u - 1))
                    pe.matmul(sc[:, u % 2, :], qr[64 * a:64 * a + 64, t * P:(t + 1) * P],
                              kr[64 * a:64 * a + 64, :], start=True, stop=True).then_inc(scored, 1)
                    if u >= 1:
                        transposes(u - 1)
                    if u == 5:
                        mix(0)
                transposes(7)
                mix(1)
                pe.wait_ge(out_done, j * 2 + 2)

        @block.scalar
        def _(act):
            turn_scalar(act, 1, kT[:, 0, :])
            with act.Fori(0, 4) as j:
                act.wait_ge(rotated, j + 1)
                turn_scalar(act, j + 2, q_tile(j))

                def copy(u):
                    a, t = UNITS[u]
                    act.wait_ge(transposed, j * 8 + (u + 1))
                    act.activation(probT[:, :, a, t * P:(t + 1) * P],
                                   pt[:, u % 2, :].rearrange("p (b q) -> p b q", b=TT),
                                   ACT.Copy).then_inc(copied, 1)

                for u in range(8):
                    act.wait_ge(maxed, j * 8 + (u + 1))
                    if u >= 2:
                        act.wait_ge(transposed, j * 8 + (u - 1))
                    act.activation(prob[:, u % 2, :], sc[:, u % 2, :], ACT.Exp, bias=stat[:, 0, u:u + 1],
                                   scale=AD ** -0.5, accum_out=stat[:, 1, u:u + 1]).then_inc(expd, 1)
                    if u >= 1:
                        copy(u - 1)
                copy(7)
                for a in range(2):
                    act.wait_ge(mixed, j * 2 + (a + 1))
                    act.activation(yT[64 * a:64 * a + 64, bass.ds(j, 1), :].rearrange("p a s -> p (a s)"),
                                   po[64 * a:64 * a + 64, a, :], ACT.Copy).then_inc(out_done, 1)

        @block.vector
        def _(dve):
            step = Steps(dve, v_step)
            dve.wait_ge(landed, 32)
            turn_vector(dve, step, 1, kT[:, 0, :], core.col("k_norm"), kr[:, :])
            unit = Steps(dve, st_unit)
            with dve.Fori(0, 4) as j:
                step.enter(j, 4)
                unit.enter(j, 16)
                turn_vector(dve, step, j + 2, q_tile(j), core.col("q_norm"), qr[:, :])

                def scale(u):
                    dve.wait_ge(expd, j * 8 + (u + 1))
                    unit(dve.reciprocal(stat[:, 2, u:u + 1], stat[:, 1, u:u + 1]))
                    dve.tensor_scalar(prob[:, u % 2, :], prob[:, u % 2, :], stat[:, 2, u:u + 1], None,
                                      ALU.mult).then_inc(scaled, 1)

                for u in range(8):
                    dve.wait_ge(scored, j * 8 + (u + 1))
                    unit(dve.tensor_reduce(stat[:, 0, u:u + 1], sc[:, u % 2, :], AX.X, ALU.max))
                    dve.tensor_scalar(stat[:, 0, u:u + 1], stat[:, 0, u:u + 1], -AD ** -0.5, None,
                                      ALU.mult).then_inc(maxed, 1)
                    if u >= 1:
                        scale(u - 1)
                scale(7)
                unit.leave(4)
                step.leave(4)


def hgrn_gates(core, qT, fT, kT, lT):
    n = 2 * GH
    with Stage(core) as st:
        r = st.sb("r", [P, 6, n])
        v_step, maxed, expd, sig, kept, gated = (st.sem(x) for x in ("v_step", "maxed", "expd", "sig", "kept", "gated"))
        block = st.block()

        @block.scalar
        def _(act):
            act.wait_ge(maxed, 2)
            act.activation(r[:, 0:2, :], r[:, 0:2, :], ACT.Exp).then_inc(expd, 1)
            for d in range(2):
                act.activation(kT[:, d, :, :], fT[:, d, :, :], ACT.Sigmoid).then_inc(sig, 1)
            for d in range(2):
                act.wait_ge(kept, d + 1)
                act.activation(lT[:, d, :, :], lT[:, d, :, :], ACT.Ln)

        @block.vector
        def _(dve):
            step = Steps(dve, v_step)
            raw = [core.col("lb_raw", i * n, n) for i in range(2)]
            step(dve.tensor_tensor(r[:, 2, :], raw[0], raw[1], ALU.max))
            for i in range(2):
                dve.tensor_tensor(r[:, i, :], raw[i], r[:, 2, :], ALU.subtract).then_inc(maxed, 1)
            dve.wait_ge(expd, 1)
            step(dve.tensor_tensor(r[:, 3, :], r[:, 0, :], r[:, 1, :], ALU.add))
            step(dve.reciprocal(r[:, 3, :], r[:, 3, :]))
            step(dve.tensor_tensor(r[:, 4, :], r[:, 0, :], r[:, 3, :], ALU.mult))
            step(dve.tensor_scalar(r[:, 5, :], r[:, 4, :], -1.0, 1.0, ALU.mult, ALU.add))
            for d in range(2):
                dve.wait_ge(sig, d + 1)
                for h in range(GH):
                    i = d * GH + h
                    dve.tensor_scalar(lT[:, d, h, :], kT[:, d, h, :], r[:, 5, i:i + 1], r[:, 4, i:i + 1],
                                      ALU.mult, ALU.add).then_inc(gated, 1)
            for d in range(2):
                dve.wait_ge(gated, GH * (d + 1))
                dve.tensor_scalar(fT[:, d, :, :], lT[:, d, :, :], -1.0, 1.0, ALU.mult, ALU.add).then_inc(kept, 1)


def hgrn(core, qT, kT, lT, v, gT, oT):
    W = NCH * NBL
    with Stage(core) as st:
        reset = st.sb("reset", [P, 2, S])
        causal = st.sb("causal", [P, 2, TT, GC])
        ql, vl, gl = (st.sb(n, [P, S]) for n in ("ql", "vl", "gl"))
        kl, b = (st.sb(n, [P, 2, S]) for n in ("kl", "b"))
        qd, qe, kd = (st.sb(n, [P, 2, S]) for n in ("qd", "qe", "kd"))
        kk = st.sb("kk", [P, 2, NCH, NBL, GC])
        ebl = st.sb("ebl", [P, 2, NCH])
        kdT = st.sb("kdT", [P, 2, TT, P])
        at = st.sb("at", [P, 2, TT, GC])
        state = st.sb("state", [P, 2, P])
        sq, rstd, on = (st.sb(n, [P, S]) for n in ("sq", "rstd", "on"))
        pa = st.ps("pa", [P, 2, TT, GC])
        pk = st.ps("pk", [P, 2, TT, P])
        pst = st.ps("pst", [P, 2, 512])
        po = st.ps("po", [P, 2, 512])
        pn = st.ps("pn", [P, S])
        (landed, v_step, a_step, a_ready, k_ready, kdT_ready, a_scores, a_masked, state_add, state_new,
         o_done, squared, summed, rooted, kdt_p) = (st.sem(n) for n in (
             "landed", "v_step", "a_step", "a_ready", "k_ready", "kdT_ready", "a_scores", "a_masked",
             "state_add", "state_new", "o_done", "squared", "summed", "rooted", "kdt_p"))
        block = st.block()
        ident = core.mats["ident"]

        @block.sync
        def _(sp):
            sp.dma_start(reset[:, :, :], core.const("reset").rearrange("p (d s) -> p d s", d=2)).then_inc(landed, 16)
            sp.dma_start(causal[:, :, :, :], core.const("causal").rearrange("p (d t c) -> p d t c", d=2, t=TT)).then_inc(landed, 16)

        def one(x, h):
            return x[:, bass.ds(h, 1), :].rearrange("p a s -> p (a s)")

        def rows(d, i):
            return (0, GB * (i + 1)) if d == 0 else (GB * i, GC)

        @block.vector
        def _(dve):
            step = Steps(dve, v_step)
            dve.wait_ge(landed, 32)
            step(dve.memset(kk[:, :, :, :, :], 0.0))
            with dve.Fori(0, GH) as h:
                step.enter(h, 26)
                step.mark(dve.tensor_copy(ql[:, :], one(qT, h)))
                for d in range(2):
                    step.mark(dve.tensor_copy(kl[:, d, :], kT[:, d, bass.ds(h, 1), :].rearrange("p a s -> p (a s)")))
                step.mark(dve.tensor_copy(vl[:, :].rearrange("p (t e) -> p t e", t=TT), v[:, :, bass.ds(h * P, P)]))
                step.mark(dve.memset(state[:, :, :], 0.0))
                for d in range(2):
                    way = slice(None, None, 1) if d == 0 else slice(None, None, -1)
                    lg = lT[:, d, bass.ds(h, 1), :].rearrange("p a s -> p (a s)")
                    if d == 1:
                        step(dve.tensor_copy(qe[:, 1, :], lg))
                        lg = qe[:, 1, :]
                    step(dve.tensor_tensor_scan(b[:, d, way], reset[:, d, way], lg[:, way], 0.0, ALU.mult, ALU.add))
                bb = [b[:, d, :].rearrange("p (w g) -> p w g", g=GB) for d in range(2)]
                bc = [b[:, d, :].rearrange("p (n c) -> p n c", c=GC) for d in range(2)]
                mid = [GB // 2 - 1, GB // 2]
                last = [GC - 1, 0]
                for d in range(2):
                    m = bb[d][:, :, mid[d]:mid[d] + 1].to_broadcast([P, W, GB])
                    step.mark(dve.tensor_tensor(qd[:, d, :].rearrange("p (w g) -> p w g", g=GB), bb[d], m, ALU.subtract))
                    e = bc[d][:, :, last[d]:last[d] + 1].to_broadcast([P, NCH, GC])
                    step.mark(dve.tensor_tensor(kd[:, d, :].rearrange("p (n c) -> p n c", c=GC), e, bc[d], ALU.subtract))
                step.wait()
                dve.tensor_scalar(qd[:, :, :], qd[:, :, :], 80.0, None, ALU.min).then_inc(a_ready, 1)
                for d in range(2):
                    for i in range(NBL):
                        lo, hi = rows(d, i)
                        m = bc[d][:, :, GB * i + mid[d]:GB * i + mid[d] + 1].to_broadcast([P, NCH, hi - lo])
                        step.mark(dve.tensor_tensor(kk[:, d, :, i, lo:hi], m, bc[d][:, :, lo:hi], ALU.subtract))
                step.wait()
                for d in range(2):
                    for i in range(NBL):
                        own = kk[:, d, :, i, GB * i:GB * (i + 1)]
                        last_ = dve.tensor_scalar(own, own, 80.0, None, ALU.min)
                last_.then_inc(a_ready, 1)
                dve.wait_ge(a_step, h * 2 + 1)
                step.mark(dve.tensor_tensor(qd[:, :, :], qd[:, :, :], ql[:, :].unsqueeze(1).to_broadcast([P, 2, S]), ALU.mult))
                step.mark(dve.tensor_tensor(qe[:, :, :], qe[:, :, :], ql[:, :].unsqueeze(1).to_broadcast([P, 2, S]), ALU.mult))
                dve.tensor_tensor(kd[:, :, :], kd[:, :, :], kl[:, :, :], ALU.mult).then_inc(k_ready, 1)
                dve.wait_ge(a_step, h * 2 + 2)
                for d in range(2):
                    kc = kl[:, d, :].rearrange("p (n c) -> p n c", c=GC)
                    for i in range(NBL):
                        lo, hi = rows(d, i)
                        x = kk[:, d, :, i, lo:hi]
                        last_ = dve.tensor_tensor(x, x, kc[:, :, lo:hi], ALU.mult)
                last_.then_inc(k_ready, 1)
                dve.wait_ge(a_scores, h + 1)
                dve.tensor_tensor(at[:, :, :, :], pa[:, :, :, :], causal[:, :, :, :], ALU.mult).then_inc(a_masked, 1)
                for n in range(NCH):
                    for d in range(2):
                        c = n if d == 0 else NCH - 1 - n
                        dve.wait_ge(state_add, h * 16 + (2 * n + d + 1))
                        dve.scalar_tensor_tensor(state[:, d, :], state[:, d, :], ebl[:, d, c:c + 1],
                                                 pst[:, d, 0:P], ALU.mult, ALU.add).then_inc(state_new, 1)
                dve.wait_ge(summed, h + 1)
                step(dve.tensor_scalar(rstd[:, :], pn[:, :], 1.0 / GD, EPS, ALU.mult, ALU.add))
                dve.wait_ge(rooted, h + 1)
                step(dve.reciprocal(rstd[:, :], rstd[:, :]))
                step(dve.scalar_tensor_tensor(on[:, :], on[:, :], core.col("hg_out_norm"), rstd[:, :], ALU.mult, ALU.mult))
                step(dve.tensor_tensor(one(oT, h), on[:, :], one(gT, h), ALU.mult))
                step.leave(GH)

        @block.scalar
        def _(act):
            with act.Fori(0, GH) as h:
                act.wait_ge(a_ready, h * 2 + 1)
                act.activation(qd[:, :, :], qd[:, :, :], ACT.Exp)
                act.activation(kd[:, :, :], kd[:, :, :], ACT.Exp)
                act.activation(qe[:, :, :], b[:, :, :], ACT.Exp)
                act.activation(ebl[:, 0, :], b[:, 0, GC - 1::GC], ACT.Exp)
                act.activation(ebl[:, 1, :], b[:, 1, 0::GC], ACT.Exp).then_inc(a_step, 1)
                act.wait_ge(a_ready, h * 2 + 2)
                for d in range(2):
                    for i in range(NBL):
                        lo, hi = rows(d, i)
                        x = kk[:, d, :, i, lo:hi]
                        last_ = act.activation(x, x, ACT.Exp)
                last_.then_inc(a_step, 1)
                for d in range(2):
                    act.wait_ge(kdt_p, h * 2 + (d + 1))
                    act.activation(kdT[:, d, :, :], pk[:, d, :, :], ACT.Copy).then_inc(kdT_ready, 1)
                act.wait_ge(o_done, h + 1)
                o = po[:, :, 0:S // 2].rearrange("p a (t c) -> p a t c", c=GC)
                for dst, func in ((sq, ACT.Square), (on, ACT.Copy)):
                    act.activation(dst[:, :].rearrange("p (t a c) -> p a t c", a=2, c=GC), o, func).then_inc(squared, 1)
                act.wait_ge(v_step, h * 26 + 24)
                act.activation(rstd[:, :], rstd[:, :], ACT.Sqrt).then_inc(rooted, 1)

        @block.tensor
        def _(pe):
            with pe.Fori(0, GH) as h:
                pe.wait_ge(k_ready, h * 2 + 1)
                for d in range(2):
                    for t in range(TT):
                        last = pe.transpose(pk[:, d, t, :], kd[:, d, t * P:(t + 1) * P], ident[:, :])
                    last.then_inc(kdt_p, 1)
                pe.wait_ge(k_ready, h * 2 + 2)
                for d in range(2):
                    for c in range(NCH):
                        r = GC * (c % 2)
                        for i in range(NBL):
                            last = pe.matmul(pa[r:r + GC, d, c // 2, GB * i:GB * (i + 1)], kk[:, d, c, i, :],
                                             qd[:, d, c * GC + GB * i:c * GC + GB * (i + 1)], start=True, stop=True,
                                             skip_group_check=True)
                last.then_inc(a_scores, 1)
                pe.wait_ge(a_masked, h + 1)
                for n in range(NCH):
                    for d in range(2):
                        c = n if d == 0 else NCH - 1 - n
                        r = GC * (c % 2)
                        vc = vl[r:r + GC, (c // 2) * P:(c // 2 + 1) * P]
                        o = po[:, c % 2, GC * (c // 2):GC * (c // 2 + 1)]
                        pe.matmul(o, vc, at[r:r + GC, d, c // 2, :], start=(n == 0), stop=False, skip_group_check=True)
                        if n == 0 and d == 0:
                            pe.wait_ge(kdT_ready, h * 2 + 2)
                        if n >= 1:
                            pe.wait_ge(state_new, h * 16 + (2 * (n - 1) + d + 1))
                        last = pe.matmul(o, state[:, d, :], qe[:, d, c * GC:(c + 1) * GC], start=False, stop=False,
                                         skip_group_check=True)
                        pe.matmul(pst[:, d, 0:P], kdT[r:r + GC, d, c // 2, :], vc, start=True, stop=True).then_inc(state_add, 1)
                last.then_inc(o_done, 1)
                pe.wait_ge(squared, h * 2 + 2)
                pe.matmul(pn[:, :], core.mats["ones"][:, :], sq[:, :], start=True, stop=True).then_inc(summed, 1)


def merge(core, gates, y_att, y_hg, m):
    with Stage(core) as st:
        v_step = st.sem("v_step")
        block = st.block()

        @block.vector
        def _(dve):
            step = Steps(dve, v_step)
            step(dve.tensor_tensor(y_att[:, :, :], y_att[:, :, :], gates[:, 0:KT, :], ALU.mult))
            step(dve.tensor_tensor(y_hg[:, :, :], y_hg[:, :, :], gates[:, KT:2 * KT, :], ALU.mult))
            dve.tensor_tensor(m[:, :, :], y_att[:, :, :], y_hg[:, :, :], ALU.add)


def first_mixer(core):
    norm(core, core.col("norm_mix"))
    d = core.dram
    with Stage(core) as st:
        ya = st.sb("ya", [P, 4, S])
        yh = st.sb("yh", [P, GH, S])
        with Stage(core) as st2:
            qkT = st2.sb("qkT", [P, 6, S])
            v = st2.sb("v", [P, TT, AKV * AD])
            linear(core, d["w_qk"], KT, 384, 2, core.hT, tiles_to(qkT, 3))
            linear(core, d["w_v"], KT, 64, 2, core.hT, tokens_to(v, 64), token_major=True)
            attention(core, qkT, qkT[:, 4:5, :], v, ya)
        with Stage(core) as st2:
            pT = st2.sb("pT", [P, 4, GH, S])
            hv = st2.sb("hv", [P, TT, GH * GD])
            kT = st2.sb("kT", [P, 2, GH, S])
            flat = pT[:, :, :, :].rearrange("p a h s -> p (a h) s")
            linear(core, d["w_hg_silu"], KT, 512, 2, core.hT, tiles_to(flat[:, 0:8, :], 4, ACT.Silu))
            linear(core, d["w_hg_f"], KT, 512, 2, core.hT, tiles_to(flat[:, 8:16, :], 4))
            linear(core, d["w_hg_v"], KT, 256, 2, core.hT, tokens_to(hv, 256), token_major=True)
            fT = pT[:, 2:4, :, :]
            lT = kT
            hgrn_gates(core, pT, fT, kT, lT)
            hgrn(core, pT[:, 0, :, :], fT, lT, hv, pT[:, 1, :, :], yh)
        with Stage(core) as st2:
            y_att, y_hg = st2.sb("y_att", [P, KT, S]), st2.sb("y_hg", [P, KT, S])
            gates = st2.sb("gates", [P, 2 * KT, S])
            linear(core, d["w_up_att"], 4, 512, 2, ya, tiles_to(y_att, 4))
            linear(core, d["w_up_hg"], 4, 512, 2, yh, tiles_to(y_hg, 4))
            linear(core, d["w_gates"], KT, 512, 4, core.hT, tiles_to(gates, 4, ACT.Sigmoid))
            merge(core, gates, y_att, y_hg, core.hT)
            linear(core, d["w_out"], KT, 512, 2, core.hT, add_to_x(core, 4), engine="vector")


def peer_scores(core, qT, h_tm, scores):
    with Stage(core) as st:
        keys = st.sb("keys", [P, 2 * PH, PN])
        pt = st.ps("pt", [P, 4, 512])
        pq = st.ps("pq", [P, 4, 512])
        landed, transposed, copied, scored, taken = (st.sem(n) for n in ("landed", "transposed", "copied", "scored", "taken"))
        block = st.block()

        @block.sync
        def _(sp):
            sp.dma_start(keys[:, :, :], core.dram["sub_keys"].rearrange("p (h n) -> p h n", n=PN)).then_inc(landed, 16)

        @block.tensor
        def _(pe):
            n = 0
            for t in range(TT):
                for half in range(2):
                    if n >= 4:
                        pe.wait_ge(copied, n - 3)
                    for k in range(4):
                        last = pe.transpose(pt[:, n % 4, k * P:(k + 1) * P],
                                            core.hT[:, half * 4 + k, t * P:(t + 1) * P], core.mats["ident"][:, :])
                    last.then_inc(transposed, 1)
                    n += 1
            pe.wait_ge(landed, 16)
            n = 0
            for t in range(TT):
                for quarter in range(4):
                    if n >= 4:
                        pe.wait_ge(taken, n - 3)
                    for k in range(4):
                        i = quarter * 4 + k
                        last = pe.matmul(pq[:, n % 4, k * PN:(k + 1) * PN], qT[:, i, t * P:(t + 1) * P],
                                         keys[:, i, :], start=True, stop=True)
                    last.then_inc(scored, 1)
                    n += 1

        @block.scalar
        def _(act):
            for n in range(2 * TT):
                act.wait_ge(transposed, n + 1)
                act.activation(h_tm[:, n // 2, (n % 2) * 512:(n % 2 + 1) * 512], pt[:, n % 4, :], ACT.Copy).then_inc(copied, 1)

        @block.vector
        def _(dve):
            for n in range(4 * TT):
                dve.wait_ge(scored, n + 1)
                dve.tensor_copy(scores[:, n // 4, (n % 4) * 4:(n % 4) * 4 + 4, :],
                                pq[:, n % 4, :].rearrange("p (k n) -> p k n", n=PN)).then_inc(taken, 1)


def peer_pick(core, scores, expert, weight):
    HK = PH * PK
    with Stage(core) as st:
        iota = st.sb("iota", [P, PK])
        sc = st.sb("sc", [P, 2 * PH, PN])
        rest = st.sb("rest", [P, 2 * PH, PN])
        v = st.sb("v", [P, 2 * PH, PK])
        ix = st.sb("ix", [P, 2 * PH, PK], U32)
        ixf = st.sb("ixf", [P, 2 * PH, PK])
        cand = st.sb("cand", [P, PH, PK, PK])
        best = st.sb("best", [P, PH, PK])
        pos = st.sb("pos", [P, PH, PK], U32)
        part = st.sb("part", [P, 2, HK], U32)
        partf = st.sb("partf", [P, 2, HK])
        hit = st.sb("hit", [P, PH, PK, PK])
        name = st.sb("name", [P, 2, HK])
        ex = st.sb("ex", [P, PH, PK])
        tot = st.sb("tot", [P, PH])
        landed, v_step, ready, expd, passed = (st.sem(n) for n in ("landed", "v_step", "ready", "expd", "passed"))
        block = st.block()

        @block.sync
        def _(sp):
            sp.dma_start(iota[:, :], core.const("iota16")).then_inc(landed, 16)

        @block.scalar
        def _(act):
            with act.Fori(0, TT) as t:
                act.wait_ge(ready, t + 1)
                act.activation(ex[:, :, :], ex[:, :, :], ACT.Exp).then_inc(expd, 1)

        @block.vector
        def _(dve):
            step = Steps(dve, v_step)

            def best16(values, spare, n, top, where):
                rows = range(n)
                for i in rows:
                    last = dve.max(top[:, i, 0:8], values(i))
                step.mark(last)
                wait_apart(dve, v_step, step.base + step.n, passed)
                for i in rows:
                    dve.max_index(where[:, i, 0:8], top[:, i, 0:8], values(i))
                    last = dve.match_replace(spare(i), top[:, i, 0:8], values(i), NEG)
                step.mark(last)
                wait_apart(dve, v_step, step.base + step.n, passed)
                for i in rows:
                    last = dve.max(top[:, i, 8:16], spare(i))
                step.mark(last)
                wait_apart(dve, v_step, step.base + step.n, passed)
                for i in rows:
                    last = dve.max_index(where[:, i, 8:16], top[:, i, 8:16], spare(i))
                step.mark(last)
                wait_apart(dve, v_step, step.base + step.n, passed)

            dve.wait_ge(landed, 16)
            with dve.Fori(0, TT) as t:
                step.enter(t, 24)
                step.mark(dve.tensor_copy(sc[:, :, :], scores[:, bass.ds(t, 1), :, :].rearrange("p a h n -> p (a h) n")))
                wait_apart(dve, v_step, step.base + step.n, passed)
                best16(lambda i: sc[:, i, :], lambda i: rest[:, i, :], 2 * PH, v, ix)
                step(dve.tensor_copy(ixf[:, :, :], ix[:, :, :]))
                v2 = v[:, :, :].rearrange("p (h q) k -> p h q k", q=2)
                step.mark(dve.tensor_tensor(cand[:, :, :, :], v2[:, :, 0, :].unsqueeze(3).to_broadcast([P, PH, PK, PK]),
                                       v2[:, :, 1, :].unsqueeze(2).to_broadcast([P, PH, PK, PK]), ALU.add))
                wait_apart(dve, v_step, step.base + step.n, passed)
                flat = cand[:, :, :, :].rearrange("p h a b -> p h (a b)")
                spare = rest[:, :, :].rearrange("p (h q) n -> p h (q n)", q=2)
                best16(lambda i: flat[:, i, :], lambda i: spare[:, i, :], PH, best, pos)
                fpos = pos[:, :, :].rearrange("p h k -> p (h k)")
                step.mark(dve.tensor_scalar(part[:, 0, :], fpos, 4, None, ALU.logical_shift_right))
                step(dve.tensor_scalar(part[:, 1, :], fpos, 15, None, ALU.bitwise_and))
                step(dve.tensor_copy(partf[:, :, :], part[:, :, :]))
                i2 = ixf[:, :, :].rearrange("p (h q) k -> p h q k", q=2)
                for q in range(2):
                    step(dve.tensor_tensor(hit[:, :, :, :].rearrange("p h k j -> p (h k) j"),
                                           partf[:, q, :].unsqueeze(2).to_broadcast([P, HK, PK]),
                                           iota[:, :].unsqueeze(1).to_broadcast([P, HK, PK]), ALU.is_equal))
                    step(dve.tensor_tensor(hit[:, :, :, :], hit[:, :, :, :],
                                           i2[:, :, q, :].unsqueeze(2).to_broadcast([P, PH, PK, PK]), ALU.mult))
                    step(dve.tensor_reduce(name[:, q, :], hit[:, :, :, :].rearrange("p h k j -> p (h k) j"), AX.X, ALU.add))
                step(dve.scalar_tensor_tensor(expert[:, bass.ds(t, 1), :].rearrange("p a k -> p (a k)"), name[:, 0, :],
                                              float(PN), name[:, 1, :], ALU.mult, ALU.add))
                dve.tensor_tensor(ex[:, :, :], best[:, :, :], best[:, :, 0:1].to_broadcast([P, PH, PK]),
                                  ALU.subtract).then_inc(ready, 1)
                dve.wait_ge(expd, t + 1)
                step(dve.tensor_reduce(tot[:, :], ex[:, :, :], AX.X, ALU.add))
                step(dve.reciprocal(tot[:, :], tot[:, :]))
                step(dve.tensor_tensor(weight[:, bass.ds(t, 1), :].rearrange("p a (h k) -> p (a h) k", k=PK), ex[:, :, :],
                                       tot[:, :].unsqueeze(2).to_broadcast([P, PH, PK]), ALU.mult))
                step.leave(TT)


def peer_experts(core, h_tm, expert, weight, y_tm):
    G = 8
    with Stage(core) as st:
        idx = st.sb("idx", [P, 2, G], U32)
        ub = st.sb("ub", [P, 2, G, D])
        vb = st.sb("vb", [P, 2, G, D])
        a = st.sb("a", [P, 2, G])
        ge = st.sb("ge", [P, 2, G])
        wt = st.sb("wt", [P, 2, G])
        diag = st.sb("diag", [P, 2, G, P])
        po = st.ps("po", [P, 2, D])
        u_landed = [[st.sem(f"u_landed{g}{s}") for s in range(G)] for g in range(2)]
        v_landed = [[st.sem(f"v_landed{g}{s}") for s in range(G)] for g in range(2)]
        idx_copied, u_free, v_free, gelu_done, wt_ready, diag_ready, sum_free, zeroed, passed = (st.sem(n) for n in (
            "idx_copied", "u_free", "v_free", "gelu_done", "wt_ready", "diag_ready", "sum_free", "zeroed", "passed"))
        block = st.block()

        @block.gpsimd
        def _(pool):
            with pool.Fori(0, TT) as t:
                with pool.Fori(0, PH) as h:
                    for g in range(2):
                        pool.wait_ge(v_free, t * 128 + h * 16 + (G * g + 8))
                        pool.tensor_copy(idx[:, g, :], expert[:, bass.ds(t, 1), bass.ds(h * PK + g * G, G)]
                                         .rearrange("p a k -> p (a k)")).then_inc(idx_copied, 1)
                        pool.wait_ge(idx_copied, t * 16 + h * 2 + (g + 1))
                        for table, buf, free, landed in (("peer_u", ub, u_free, u_landed), ("peer_v", vb, v_free, v_landed)):
                            for s in range(G):
                                wait_apart(pool, free, t * 128 + h * 16 + (G * g + s + 1), passed)
                                pool.indirect_dma_start(
                                    out=buf[:, g, s, :], out_offset=None, in_=core.dram[table][:, :],
                                    in_offset=bass.IndirectOffsetOnAxis(ap=idx[:, g, s:s + 1], axis=0),
                                ).then_inc(landed[g][s], 16)

        @block.vector
        def _(dve):
            dve.sem_inc(u_free, 2 * G)
            dve.sem_inc(sum_free, 2)
            dve.memset(y_tm[:, :, :], 0.0).then_inc(zeroed, 1)
            dve.wait_ge(zeroed, 1)
            with dve.Fori(0, TT) as t:
                with dve.Fori(0, PH) as h:
                    for g in range(2):
                        for s in range(G):
                            dve.wait_ge(u_landed[g][s], t * 128 + h * 16 + 16)
                            dve.scalar_tensor_tensor(ub[:, g, s, :], ub[:, g, s, :], 1.0,
                                                     h_tm[:, bass.ds(t, 1), :].rearrange("p a d -> p (a d)"),
                                                     ALU.mult, ALU.mult, accum_out=a[:, g, s:s + 1]).then_inc(u_free, 1)
                        dve.wait_ge(gelu_done, t * 16 + h * 2 + (g + 1))
                        dve.tensor_tensor(wt[:, g, :], ge[:, g, :], weight[:, bass.ds(t, 1), bass.ds(h * PK + g * G, G)]
                                          .rearrange("p a k -> p (a k)"), ALU.mult).then_inc(wt_ready, 1)
                        dve.wait_ge(v_free, t * 128 + h * 16 + (G * g + 24))
                        y = y_tm[:, bass.ds(t, 1), :].rearrange("p a d -> p (a d)")
                        dve.tensor_tensor(y, po[:, g, :], y, ALU.add).then_inc(sum_free, 1)
                        dve.wait_ge(sum_free, t * 16 + h * 2 + (g + 3))

        @block.scalar
        def _(act):
            with act.Fori(0, TT) as t:
                with act.Fori(0, PH) as h:
                    for g in range(2):
                        act.wait_ge(u_free, t * 128 + h * 16 + (G * g + 24))
                        act.activation(ge[:, g, :], a[:, g, :], ACT.Gelu_apprx_tanh).then_inc(gelu_done, 1)
                        act.wait_ge(wt_ready, t * 16 + h * 2 + (g + 1))
                        for s in range(G):
                            act.wait_ge(v_free, t * 128 + h * 16 + (G * g + s + 1))
                            act.activation(diag[:, g, s, :], core.mats["ident"][:, :], ACT.Copy,
                                           scale=wt[:, g, s:s + 1]).then_inc(diag_ready, 1)

        @block.tensor
        def _(pe):
            pe.sem_inc(v_free, 2 * G)
            with pe.Fori(0, TT) as t:
                with pe.Fori(0, PH) as h:
                    for g in range(2):
                        pe.wait_ge(sum_free, t * 16 + h * 2 + (g + 1))
                        for s in range(G):
                            pe.wait_ge(diag_ready, t * 128 + h * 16 + (G * g + s + 1))
                            pe.wait_ge(v_landed[g][s], t * 128 + h * 16 + 16)
                            for n in range(2):
                                last = pe.matmul(po[:, g, n * 512:(n + 1) * 512], diag[:, g, s, :],
                                                 vb[:, g, s, n * 512:(n + 1) * 512], start=(s == 0), stop=(s == G - 1))
                            last.then_inc(v_free, 1)


def add_tokens(core, y_tm):
    with Stage(core) as st:
        pt = st.ps("pt", [P, KT, S])
        transposed = st.sem("transposed")
        block = st.block()

        @block.tensor
        def _(pe):
            for k in range(KT):
                for t in range(TT):
                    last = pe.transpose(pt[:, k, t * P:(t + 1) * P], y_tm[:, t, k * P:(k + 1) * P], core.mats["ident"][:, :])
                last.then_inc(transposed, 1)

        @block.vector
        def _(dve):
            for k in range(KT):
                dve.wait_ge(transposed, k + 1)
                dve.tensor_tensor(core.xT[:, k, :], pt[:, k, :], core.xT[:, k, :], ALU.add)


def peer(core):
    norm(core, core.col("norm_ffn"))
    with Stage(core) as st:
        h_tm = st.sb("h_tm", [P, TT, D])
        expert = st.sb("expert", [P, TT, PH * PK], U32)
        weight = st.sb("weight", [P, TT, PH * PK])
        with Stage(core) as st2:
            scores = st2.sb("scores", [P, TT, 2 * PH, PN])
            with Stage(core) as st3:
                qT = st3.sb("qT", [P, 2 * PH, S])
                linear(core, core.dram["w_peer"], KT, 512, 4, core.hT, tiles_to(qT, 4))
                peer_scores(core, qT, h_tm, scores)
            peer_pick(core, scores, expert, weight)
        y_tm = core.hT[:, :, :].rearrange("p k s -> p (k s)").rearrange("p (t d) -> p t d", t=TT)
        peer_experts(core, h_tm, expert, weight, y_tm)
        add_tokens(core, y_tm)


def ple(core):
    norm(core, core.col("norm_ple"))
    with Stage(core) as st:
        pT = st.sb("pT", [P, 2, S])
        gate = st.sb("gate", [P, KT, S])
        proj = st.sb("proj", [P, KT, S])
        with Stage(core) as st2:
            landed = st2.sem("landed")
            block = st2.block()

            @block.sync
            def _(sp):
                sp.dma_start(pT[:, :, :], core.dram["pT"].rearrange("p (k s) -> p k s", k=2)).then_inc(landed, 16)
                sp.wait_ge(landed, 16)
        linear(core, core.dram["w_ple_gate"], KT, 512, 2, core.hT, tiles_to(gate, 4, ACT.Sigmoid))
        linear(core, core.dram["w_ple_proj"], 2, 512, 2, pT, tiles_to(proj, 4))
        with Stage(core) as st2:
            v_step = st2.sem("v_step")
            block = st2.block()

            @block.vector
            def _(dve):
                step = Steps(dve, v_step)
                step(dve.tensor_tensor(gate[:, :, :], gate[:, :, :], proj[:, :, :], ALU.mult))
                dve.tensor_tensor(core.xT[:, :, :], core.xT[:, :, :], gate[:, :, :], ALU.add)


def modulation(core):
    W, N = 512, 2 * 6 * D // 512
    with Stage(core) as st:
        ca = st.sb("ca", [P, KT])
        ring = st.sb("ring", [P, 4, KT * W])
        row = st.sb("row", [1, N * W])
        pv = st.ps("pv", [1, 4, 512])
        pc = st.ps("pc", [P, 512])
        landed = [st.sem(f"landed{s}") for s in range(4)]
        activated, multiplied, copied, turned, v_step = (st.sem(n) for n in (
            "activated", "multiplied", "copied", "turned", "v_step"))
        block = st.block()
        w = core.dram["ada_w"]

        @block.sync
        def _(sp):
            for s in range(4):
                sp.dma_start(ring[:, s, :], w[s * P:(s + 1) * P, :]).then_inc(landed[s], 16)
            with sp.Fori(1, N // 4) as i:
                for s in range(4):
                    sp.wait_ge(multiplied, i * 4 - 3 + s)
                    sp.dma_start(ring[:, s, :], w[bass.ds((i * 4 + s) * P, P), :]).then_inc(landed[s], 16)

        @block.scalar
        def _(act):
            act.activation(ca[:, :], core.col("c"), ACT.Silu).then_inc(activated, 1)
            with act.Fori(0, N // 4) as i:
                for s in range(4):
                    act.wait_ge(multiplied, i * 4 + 1 + s)
                    act.activation(row[0:1, bass.ds((i * 4 + s) * W, W)], pv[0:1, s, :], ACT.Copy).then_inc(copied, 1)

        @block.tensor
        def _(pe):
            pe.wait_ge(activated, 1)
            pe.sem_inc(copied, 4)
            with pe.Fori(0, N // 4) as i:
                for s in range(4):
                    pe.wait_ge(landed[s], i * 16 + 16)
                    pe.wait_ge(copied, i * 4 + 1 + s)
                    for k in range(KT):
                        last = pe.matmul(pv[0:1, s, :], ca[:, k:k + 1], ring[:, s, k * W:(k + 1) * W],
                                         start=(k == 0), stop=(k == KT - 1))
                    last.then_inc(multiplied, 1)
            pe.wait_ge(copied, N + 4)
            for i in range(N * W // P):
                last = pe.matmul(pc[:, i:i + 1], row[0:1, i * P:(i + 1) * P], core.mats["ones"][0:1, 0:1],
                                 start=True, stop=True)
            last.then_inc(turned, 1)

        @block.vector
        def _(dve):
            step = Steps(dve, v_step)
            dve.wait_ge(turned, 1)
            step(dve.tensor_tensor(core.mod[:, :], pc[:, 0:12 * KT], core.col("ada_b"), ALU.add))
            scale = core.mod[:, :].rearrange("p (n c k) -> p n c k", c=3, k=KT)[:, :, 1, :]
            gain = core.gain[:, :].rearrange("p (n k) -> p n k", k=KT)
            dve.scalar_tensor_tensor(gain, scale, 1.0, core.col("norm_g").rearrange("p (n k) -> p n k", k=KT),
                                     ALU.add, ALU.mult)


def modulated_norm(core, which):
    norm(core, core.gain[:, which * KT:(which + 1) * KT], bias=core.mod[:, 3 * KT * which:3 * KT * which + KT])


def gate_col(which):
    return 3 * KT * which + 2 * KT


def feed_forward(core, layer):
    modulated_norm(core, 2 * layer + 1)
    with Stage(core) as st:
        a = st.sb("a", [P, FF // P, S])

        def square(dve, c):
            x = a[:, bass.ds(c * 4, 4), :]
            return dve.tensor_tensor(x, x, x, ALU.mult)

        linear(core, core.dram[f"w_fc1_{layer}"], KT, 512, 8, core.hT, tiles_to(a, 4, ACT.Relu), after=square)
        deep_linear(core, core.dram[f"w_fc2_{layer}"], a, core.mod, gate_col(2 * layer + 1))


def deep_linear(core, w, src, gate, gate_at):
    slices = FF // D
    with Stage(core) as st:
        ring = st.sb("ring", [P, 2, KT * 512])
        acc = st.ps("acc", [P, 4, S])
        landed = [st.sem("landed0"), st.sem("landed1")]
        multiplied, added = st.sem("multiplied"), st.sem("added")
        block = st.block()

        @block.sync
        def _(sp):
            for s in range(2):
                sp.dma_start(ring[:, s, :], w[s * P:(s + 1) * P, :]).then_inc(landed[s], 16)
            with sp.Fori(1, slices) as i:
                for s in range(2):
                    sp.wait_ge(multiplied, i * 2 - 1 + s)
                    sp.dma_start(ring[:, s, :], w[bass.ds((i * 2 + s) * P, P), :]).then_inc(landed[s], 16)

        @block.tensor
        def _(pe):
            pe.sem_inc(added, 1)
            with pe.Fori(0, 2) as half:
                pe.wait_ge(added, half + 1)
                for n in range(slices):
                    s = n % 2
                    pe.wait_ge(landed[s], half * 32 + (n // 2 + 1) * 16)
                    for j in range(4):
                        for k in range(KT):
                            last = pe.matmul(acc[:, j, :], ring[:, s, k * 512 + j * P:k * 512 + (j + 1) * P],
                                             src[:, n * KT + k, :], start=(n == 0 and k == 0),
                                             stop=(n == slices - 1 and k == KT - 1))
                    last.then_inc(multiplied, 1)

        @block.vector
        def _(dve):
            take = add_to_x(core, 4, gate, gate_at)
            with dve.Fori(0, 2) as half:
                dve.wait_ge(multiplied, half * 4 + 4)
                for j in range(4):
                    last = take(dve, half, j, acc[:, j, :])
                last.then_inc(added, 1)


def conv_and_retention(core, apad, gate, qk, v, conv, o):
    pad = CW // 2
    with Stage(core) as st:
        cs = st.sb("cs", [P, 2, S])
        rot = st.sb("rot", [P, P])
        turned_ = st.sb("turned_", [P, 8, S])
        decay = st.sb("decay", [P, RH, TT, S])
        w = st.sb("w", [P, 4, S])
        pr = st.ps("pr", [P, 2, S])
        sc = st.ps("sc", [P, 2, S])
        po = st.ps("po", [P, 2, S])
        landed, v_step, turned, copied, p_step, scored, taken, weighted, mixed, out_done = (st.sem(n) for n in (
            "landed", "v_step", "turned", "copied", "p_step", "scored", "taken", "weighted", "mixed", "out_done"))
        block = st.block()

        @block.sync
        def _(sp):
            for dst, name in ((rot[:, :], "rot_ret"), (cs[:, 0, :], "cos_ret"), (cs[:, 1, :], "sin_ret")):
                sp.dma_start(dst, core.const(name)).then_inc(landed, 16)
            sp.dma_start(decay[:, :, :, :], core.const("decay").rearrange("p (h t s) -> p h t s", h=RH, t=TT)).then_inc(landed, 16)

        @block.vector
        def _(dve):
            step = Steps(dve, v_step)
            a = apad[:, :, pad:pad + S]
            step.mark(dve.memset(apad[:, :, 0:pad], 0.0))
            step.mark(dve.memset(apad[:, :, pad + S:], 0.0))
            step(dve.tensor_tensor(a, a, gate[:, :, :], ALU.mult))
            taps = core.col("conv_w").rearrange("p (j w) -> p j w", w=CW)
            for j in range(4):
                step.mark(dve.tensor_scalar(conv[:, j, :], apad[:, j, 0:S], taps[:, j, 0:1],
                                            core.col("conv_b", j, 1), ALU.mult, ALU.add))
            with dve.Fori(1, CW) as tap:
                step.enter(tap - 1, 4)
                for j in range(4):
                    step.wait(lag=3)
                    step.mark(dve.scalar_tensor_tensor(
                        conv[:, j, :], apad[:, j, bass.ds(tap, S)], taps[:, j, bass.ds(tap, 1)], conv[:, j, :],
                        ALU.mult, ALU.add))
                step.leave(CW - 1)

        @block.tensor
        def _(pe):
            pe.wait_ge(landed, 64)
            for i in range(8):
                if i >= 2:
                    pe.wait_ge(copied, i - 1)
                pe.matmul(pr[:, i % 2, :], rot[:, :], qk[:, i, :], start=True, stop=True).then_inc(turned, 1)
            pe.wait_ge(p_step, 3)
            for u in range(RH * TT + 2):
                if u < RH * TT:
                    h, m = divmod(u, TT)
                    if u >= 2:
                        pe.wait_ge(taken, u - 1)
                    pe.matmul(sc[:, u % 2, :], qk[:, 4 + h, m * P:(m + 1) * P], qk[:, h, :],
                              start=True, stop=True).then_inc(scored, 1)
                if u >= 2:
                    h, m = divmod(u - 2, TT)
                    pe.wait_ge(weighted, u - 1)
                    if m == 0 and h >= 2:
                        pe.wait_ge(out_done, h - 1)
                    pe.matmul(po[:, h % 2, :], v[:, m, h * P:(h + 1) * P], w[:, m, :], start=(m == 0),
                              stop=(m == TT - 1)).then_inc(mixed, 1)

        @block.scalar
        def _(act):
            for i in range(8):
                act.wait_ge(turned, i + 1)
                act.activation(turned_[:, i, :], pr[:, i % 2, :], ACT.Copy).then_inc(copied, 1)
            for u in range(RH * TT + 4):
                if u < RH * TT:
                    act.wait_ge(scored, u + 1)
                    if u >= 4:
                        act.wait_ge(mixed, u - 3)
                    act.activation(w[:, u % 4, :], sc[:, u % 2, :], ACT.Copy, scale=P ** -0.5).then_inc(taken, 1)
                if u >= 7 and u % TT == 3:
                    h = u // TT - 1
                    act.wait_ge(mixed, TT * (h + 1))
                    act.activation(o[:, h, :], po[:, h % 2, :], ACT.Copy).then_inc(out_done, 1)

        @block.gpsimd
        def _(pool):
            step = Steps(pool, p_step)
            pool.wait_ge(landed, 64)
            pool.wait_ge(copied, 8)
            step.mark(pool.tensor_tensor(qk[:, :, :], qk[:, :, :], cs[:, 0, :].unsqueeze(1).to_broadcast([P, 8, S]), ALU.mult))
            step(pool.tensor_tensor(turned_[:, :, :], turned_[:, :, :], cs[:, 1, :].unsqueeze(1).to_broadcast([P, 8, S]), ALU.mult))
            step(pool.tensor_tensor(qk[:, :, :], qk[:, :, :], turned_[:, :, :], ALU.add))
            for u in range(RH * TT):
                h, m = divmod(u, TT)
                pool.wait_ge(taken, u + 1)
                pool.tensor_tensor(w[:, m, :], w[:, m, :], decay[:, h, m, :], ALU.mult).then_inc(weighted, 1)


def conv_and_retention_norms(core, conv, o, gate, cat):
    with Stage(core) as st:
        sq = st.sb("sq", [P, 8, S])
        mu = st.sb("mu", [P, S])
        rstd = st.sb("rstd", [P, S])
        rh = st.sb("rh", [P, RH, S])
        pm = st.ps("pm", [P, 2, S])
        ph = st.ps("ph", [P, RH, S])
        v_step, squared, summed, rooted = (st.sem(n) for n in ("v_step", "squared", "summed", "rooted"))
        block = st.block()
        ones = core.mats["ones"]

        @block.tensor
        def _(pe):
            for j in range(4):
                last = pe.matmul(pm[:, 0, :], ones[:, :], conv[:, j, :], start=(j == 0), stop=(j == 3))
            last.then_inc(summed, 1)
            pe.wait_ge(squared, 1)
            for h in range(RH):
                last = pe.matmul(ph[:, h, :], ones[:, :], sq[:, 4 + h, :], start=True, stop=True)
            last.then_inc(summed, 1)
            pe.wait_ge(squared, 2)
            for j in range(4):
                last = pe.matmul(pm[:, 1, :], ones[:, :], sq[:, j, :], start=(j == 0), stop=(j == 3))
            last.then_inc(summed, 1)

        @block.scalar
        def _(act):
            act.activation(sq[:, 4:8, :], o[:, :, :], ACT.Square).then_inc(squared, 1)
            act.wait_ge(v_step, 2)
            act.activation(sq[:, 0:4, :], conv[:, :, :], ACT.Square).then_inc(squared, 1)
            act.wait_ge(v_step, 3)
            act.activation(rh[:, :, :], rh[:, :, :], ACT.Sqrt).then_inc(rooted, 1)
            act.wait_ge(v_step, 4)
            act.activation(rstd[:, :], rstd[:, :], ACT.Sqrt).then_inc(rooted, 1)
            act.wait_ge(v_step, 5 + 1 + 2 + 4)
            for j in range(4):
                act.activation(cat[:, j, :], conv[:, j, :], ACT.Silu, bias=core.col("cln_b", j, 1))

        @block.vector
        def _(dve):
            step = Steps(dve, v_step)
            dve.wait_ge(summed, 1)
            step(dve.tensor_scalar(mu[:, :], pm[:, 0, :], 1.0 / MA, None, ALU.mult))
            step(dve.tensor_tensor(conv[:, :, :], conv[:, :, :], mu[:, :].unsqueeze(1).to_broadcast([P, 4, S]), ALU.subtract))
            dve.wait_ge(summed, 2)
            step(dve.tensor_scalar(rh[:, :, :], ph[:, :, :], 1.0 / P, EPS, ALU.mult, ALU.add))
            dve.wait_ge(summed, 3)
            step(dve.tensor_scalar(rstd[:, :], pm[:, 1, :], 1.0 / MA, EPS, ALU.mult, ALU.add))
            dve.wait_ge(rooted, 1)
            step(dve.reciprocal(rh[:, :, :], rh[:, :, :]))
            step(dve.tensor_tensor(o[:, :, :], o[:, :, :], rh[:, :, :], ALU.mult))
            step(dve.tensor_tensor(cat[:, 4:8, :], o[:, :, :], gate[:, :, :], ALU.mult))
            dve.wait_ge(rooted, 2)
            step(dve.reciprocal(rstd[:, :], rstd[:, :]))
            for j in range(4):
                step.mark(dve.scalar_tensor_tensor(conv[:, j, :], conv[:, j, :], core.col("cln_g", j, 1), rstd[:, :],
                                                   ALU.mult, ALU.mult))


def second_mixer0(core):
    modulation(core)
    modulated_norm(core, 0)
    d = core.dram
    with Stage(core) as st:
        apad = st.sb("apad", [P, 4, S + CW - 1])
        agate = st.sb("agate", [P, 4, S])
        qk = st.sb("qk", [P, 8, S])
        v = st.sb("v", [P, TT, RH * P])
        g = st.sb("g", [P, 4, S])
        conv = st.sb("conv", [P, 4, S])
        o = st.sb("o", [P, RH, S])
        linear(core, d["w2_val"], KT, 256, 2, core.hT, tiles_to(apad[:, :, CW // 2:CW // 2 + S], 2))
        linear(core, d["w2_gate"], KT, 256, 2, core.hT, tiles_to(agate, 2, ACT.Sigmoid))
        linear(core, d["w2_qk"], KT, 512, 2, core.hT, tiles_to(qk, 4))
        linear(core, d["w2_v"], KT, 256, 2, core.hT, tokens_to(v, 256), token_major=True)
        linear(core, d["w2_g"], KT, 256, 2, core.hT, tiles_to(g, 2, ACT.Silu))
        conv_and_retention(core, apad, agate, qk, v, conv, o)
        conv_and_retention_norms(core, conv, o, g, core.hT)
    linear(core, d["w2_out"], KT, 512, 2, core.hT, add_to_x(core, 4, core.mod, gate_col(0)), engine="vector")


def feed_forward0(core):
    feed_forward(core, 0)


def feed_forward1(core):
    feed_forward(core, 1)


TWO_PI = 2.0 * np.pi
PI_SAFE = 3.1415925
TURN_HI = 6.28125
TURN_MID = float(np.float32(TWO_PI - TURN_HI))
TURN_LO = TWO_PI - TURN_HI - TURN_MID


def reduced(dve, step, x, turns, exact=True):
    step(dve.tensor_scalar(turns, x, 1.0 / TWO_PI, ROUND, ALU.mult, ALU.add))
    step(dve.tensor_scalar(turns, turns, ROUND, None, ALU.subtract))
    for part in (TURN_HI, TURN_MID, TURN_LO) if exact else (TURN_HI, TURN_MID):
        step(dve.scalar_tensor_tensor(x, turns, -part, x, ALU.mult, ALU.add))


def angles(dve, step, sin_of, cos_of):
    step(dve.tensor_scalar(sin_of, sin_of, PI_SAFE, -PI_SAFE, ALU.min, ALU.max))
    step(dve.tensor_scalar(cos_of, sin_of, -1.0, None, ALU.mult))
    step(dve.tensor_tensor(cos_of, cos_of, sin_of, ALU.max))
    step(dve.tensor_scalar(cos_of, cos_of, -1.0, np.pi / 2, ALU.mult, ALU.add))


def s5_powers(core, pb, pc, r8, th8):
    N, M = 2 * SG, 2 * SG * ST
    with Stage(core) as st:
        sign = st.sb("sign", [P, 2])
        lr, dt, ld, th, tmp = (st.sb(n, [P, N]) for n in ("lr", "dt", "ld", "th", "tmp"))
        u, w, q = (st.sb(n, [P, N]) for n in ("u", "w", "q"))
        fr, fi = st.sb("fr", [P, N]), st.sb("fi", [P, N])
        cs = st.sb("cs", [P, 2, N])
        k = st.sb("k", [P, 2, N, ST])
        mag, s, c = (st.sb(n, [P, N, ST]) for n in ("mag", "s", "c"))
        spare = st.sb("spare", [P, N, ST])
        landed, v_step, ready, done = (st.sem(n) for n in ("landed", "v_step", "ready", "done"))
        block = st.block()
        li = core.col("s5_li")

        @block.sync
        def _(sp):
            sp.dma_start(sign[:, :], core.const("sign")).then_inc(landed, 16)
            for i, name in enumerate(("power_b", "power_c")):
                sp.dma_start(k[:, i, :, :], core.const(name).rearrange("p (n t) -> p n t", t=ST)).then_inc(landed, 16)

        @block.scalar
        def _(act):
            act.activation(dt[:, :], core.col("s5_step"), ACT.Exp).then_inc(done, 1)
            act.wait_ge(ready, 1)
            act.activation(q[:, :], ld[:, :], ACT.Exp).then_inc(done, 1)
            act.wait_ge(ready, 2)
            act.activation(cs[:, :, :], cs[:, :, :], ACT.Sin).then_inc(done, 1)
            for i in range(2):
                act.wait_ge(ready, 3 + i)
                act.activation(mag[:, :, :], mag[:, :, :], ACT.Exp)
                act.activation(s[:, :, :], s[:, :, :], ACT.Sin)
                act.activation(c[:, :, :], c[:, :, :], ACT.Sin).then_inc(done, 1)
            act.activation(r8[:, :], ld[:, :], ACT.Exp, scale=float(ST))

        @block.vector
        def _(dve):
            step = Steps(dve, v_step)
            TTm = lambda out, a, b, op=ALU.mult: step(dve.tensor_tensor(out, a, b, op))
            step(dve.tensor_scalar(lr[:, :], core.col("s5_lr"), -1e-4, None, ALU.min))
            dve.wait_ge(done, 1)
            dve.tensor_tensor(ld[:, :], lr[:, :], dt[:, :], ALU.mult).then_inc(ready, 1)
            TTm(th[:, :], li, dt[:, :])
            reduced(dve, step, th[:, :], tmp[:, :])
            step(dve.tensor_copy(cs[:, 1, :], th[:, :]))
            angles(dve, step, cs[:, 1, :], cs[:, 0, :])
            dve.tensor_copy(tmp[:, :], th[:, :]).then_inc(ready, 1)
            dve.wait_ge(done, 3)
            TTm(u[:, :], q[:, :], cs[:, 0, :])
            TTm(w[:, :], q[:, :], cs[:, 1, :])
            step(dve.tensor_scalar(u[:, :], u[:, :], -1.0, None, ALU.add))
            TTm(q[:, :], lr[:, :], lr[:, :])
            TTm(tmp[:, :], li, li)
            TTm(q[:, :], q[:, :], tmp[:, :], ALU.add)
            step(dve.reciprocal(q[:, :], q[:, :]))
            TTm(fr[:, :], u[:, :], lr[:, :])
            TTm(tmp[:, :], w[:, :], li)
            TTm(fr[:, :], fr[:, :], tmp[:, :], ALU.add)
            TTm(fr[:, :], fr[:, :], q[:, :])
            TTm(fi[:, :], w[:, :], lr[:, :])
            TTm(tmp[:, :], u[:, :], li)
            TTm(fi[:, :], fi[:, :], tmp[:, :], ALU.subtract)
            TTm(fi[:, :], fi[:, :], q[:, :])
            step(dve.tensor_scalar(th8[:, :], th[:, :], float(ST), None, ALU.mult))
            reduced(dve, step, th8[:, :], tmp[:, :])
            dve.wait_ge(landed, 48)
            for i in range(2):
                many = lambda x: x[:, :].unsqueeze(2).to_broadcast([P, N, ST])
                TTm(mag[:, :, :], k[:, i, :, :], many(ld))
                TTm(s[:, :, :], k[:, i, :, :], many(th))
                reduced(dve, step, s[:, :, :], spare[:, :, :])
                angles(dve, step, s[:, :, :], c[:, :, :])
                dve.tensor_copy(spare[:, :, :], c[:, :, :]).then_inc(ready, 1)
                dve.wait_ge(done, 4 + i)
                TTm(c[:, :, :], c[:, :, :], mag[:, :, :])
                TTm(s[:, :, :], s[:, :, :], mag[:, :, :])
                if i == 0:
                    TTm(pb[:, 0, :, :], c[:, :, :], many(fr))
                    TTm(spare[:, :, :], s[:, :, :], many(fi))
                    TTm(pb[:, 0, :, :], pb[:, 0, :, :], spare[:, :, :], ALU.subtract)
                    TTm(pb[:, 1, :, :], c[:, :, :], many(fi))
                    TTm(spare[:, :, :], s[:, :, :], many(fr))
                    TTm(pb[:, 1, :, :], pb[:, 1, :, :], spare[:, :, :], ALU.add)
                    step(dve.tensor_scalar(pb[:, 1, :, :], pb[:, 1, :, :], sign[:, 0:1], None, ALU.mult))
                else:
                    step(dve.tensor_scalar(pc[:, 0, :, :], c[:, :, :], sign[:, 1:2], None, ALU.mult))
                    step(dve.tensor_copy(pc[:, 1, :, :], s[:, :, :]))


def s5_to_chunks(core, h2, u):
    with Stage(core) as st:
        p1 = st.ps("p1", [P, 4, 512])
        p2 = st.ps("p2", [P, 4, 512])
        turned, copied, turned2, copied2 = (st.sem(n) for n in ("turned", "copied", "turned2", "copied2"))
        block = st.block()
        ident = core.mats["ident"]

        @block.tensor
        def _(pe):
            for n in range(2 * ST):
                t, half = divmod(n, 2)
                if n >= 4:
                    pe.wait_ge(copied, n - 3)
                for k in range(4):
                    last = pe.transpose(p1[0:SN, n % 4, k * P:(k + 1) * P], core.hT[:, half * 4 + k, t::ST], ident[:, :])
                last.then_inc(turned, 1)
            pe.wait_ge(copied, 2 * ST)
            for n in range(SG // 8):
                if n >= 4:
                    pe.wait_ge(copied2, n - 3)
                for g in range(8):
                    last = pe.transpose(p2[:, n % 4, g * SN:(g + 1) * SN], h2[0:SN, n * 8 + g, :], ident[0:SN, 0:SN])
                last.then_inc(turned2, 1)

        @block.scalar
        def _(act):
            for n in range(2 * ST):
                t, half = divmod(n, 2)
                act.wait_ge(turned, n + 1)
                act.activation(h2[0:SN, half * 32:(half + 1) * 32, t * SC:(t + 1) * SC],
                               p1[0:SN, n % 4, :].rearrange("p (g c) -> p g c", c=SC), ACT.Copy).then_inc(copied, 1)
            for n in range(SG // 8):
                act.wait_ge(turned2, n + 1)
                act.activation(u[:, n * 8:(n + 1) * 8, :], p2[:, n % 4, :].rearrange("p (g c) -> p g c", c=SN),
                               ACT.Copy).then_inc(copied2, 1)


def s5_scan(core, h2, u, pb, pc, r8, th8):
    GDN = 2 * SB
    TAPS = 2 * ST - 1
    with Stage(core) as st:
        no = st.sb("no", [P, GDN, SN])
        keep = st.sb("keep", [P, GDN, SN])
        swap = st.sb("swap", [P, P])
        drow = st.sb("drow", [SN, D])
        bc = st.sb("bc", [P, 4, GDN, SC])
        th, th2, cosT, sinT, decay = (st.sb(n, [P, GDN, SN]) for n in ("th", "th2", "cosT", "sinT", "decay"))
        pw = st.sb("pw", [P, 4, GDN, ST])
        tp = st.sb("tp", [P, GDN, TAPS, SC])
        x1 = st.sb("x1", [P, GDN, SC])
        w2 = st.sb("w2", [P, GDN, ST, SC])
        s1, s2 = st.sb("s1", [P, GDN, ST, SC]), st.sb("s2", [P, GDN, ST, SC])
        w1 = st.sb("w1", [P, GDN, P])
        dm = st.sb("dm", [P, SB, P])
        ub = st.sb("ub", [P, SB, SN])
        e = st.sb("e", [P, GDN, SN])
        gg = st.sb("gg", [P, GDN, SN])
        hs = st.sb("hs", [P, GDN, SN + 1])
        rt = st.sb("rt", [P, 2, GDN])
        sign = st.sb("sign", [P, 2])
        pA = st.ps("pA", [P, 2, 512])
        pE = st.ps("pE", [P, 2, 512])
        pS = st.ps("pS", [P, 2, 512])
        pY = st.ps("pY", [P, 2, 512])
        names = ("landed", "fixed", "v_step", "tabled", "sined", "powers", "w1_turned", "w1_copied", "ub_copied", "ended",
                 "e_copied", "swapped", "scanned", "swapped2", "d_made", "d_copied", "h_ready", "w2_ready", "y_done", "z_done",
                 "bc_free")
        sm = {n: st.sem(n) for n in names}
        block = st.block()
        dram = core.dram

        @block.sync
        def _(sp):
            for dst, src in ((no[:, :, :], core.const("chunk_no").rearrange("p (g c) -> p g c", c=SN)),
                             (keep[:, :, :], core.const("chunk_keep").rearrange("p (g c) -> p g c", c=SN)),
                             (swap[:, :], core.const("swap_s5")), (sign[:, :], core.const("sign")),
                             (drow[:, :], dram["s5_d"][:, :].partition_broadcast(SN))):
                sp.dma_start(dst, src).then_inc(sm["fixed"], 16)
            sp.dma_start(bc[:, :, :, :].rearrange("p a g c -> p (a g c)"), dram["s5_bc"][0:P, :]).then_inc(sm["landed"], 16)
            with sp.Fori(1, SG // SB) as i:
                sp.wait_ge(sm["bc_free"], i)
                sp.dma_start(bc[:, :, :, :].rearrange("p a g c -> p (a g c)"),
                             dram["s5_bc"][bass.ds(i * P, P), :]).then_inc(sm["landed"], 16)

        @block.vector
        def _(dve):
            step = Steps(dve, sm["v_step"])
            dve.wait_ge(sm["fixed"], 80)
            step.mark(dve.memset(tp[:, :, :, :], 0.0))
            step(dve.memset(hs[:, :, :], 0.0))
            skip = h2[0:SN, :, :].rearrange("p g (t c) -> p g t c", c=SC)
            step(dve.tensor_tensor(skip, skip, drow[0:SN, :].rearrange("p (g c) -> p g c", c=SC).unsqueeze(2)
                                   .to_broadcast([SN, SG, ST, SC]), ALU.mult))
            with dve.Fori(0, SG // SB) as i:
                step.enter(i, 28)
                for n, x in enumerate((r8, th8)):
                    step.mark(dve.tensor_copy(rt[:, n, :].rearrange("p (d g) -> p d g", d=2),
                                              x[:, :].rearrange("p (d g) -> p d g", d=2)[:, :, bass.ds(i * SB, SB)]))
                for n, x in enumerate((pb, pc)):
                    for q in range(2):
                        step.mark(dve.tensor_copy(pw[:, 2 * n + q, :, :].rearrange("p (d g) k -> p d g k", d=2),
                                                  x[:, q, :, :].rearrange("p (d g) k -> p d g k", d=2)[:, :, bass.ds(i * SB, SB), :]))
                step.wait()
                step(dve.tensor_tensor(th[:, :, :], no[:, :, :], rt[:, 1, :].unsqueeze(2).to_broadcast([P, GDN, SN]), ALU.mult))
                reduced(dve, step, th[:, :, :], th2[:, :, :])
                angles(dve, step, th[:, :, :], th2[:, :, :])
                dve.tensor_tensor(decay[:, :, :], keep[:, :, :], rt[:, 0, :].unsqueeze(2).to_broadcast([P, GDN, SN]),
                                  ALU.mult).then_inc(sm["tabled"], 1)
                dve.wait_ge(sm["landed"], i * 16 + 16)
                big = lambda x: x.unsqueeze(2).to_broadcast([P, GDN, ST, SC])
                pwb = lambda n: pw[:, n, :, :].unsqueeze(3).to_broadcast([P, GDN, ST, SC])
                step.mark(dve.tensor_tensor(s1[:, :, :, :], pwb(0), big(bc[:, 0, :, :]), ALU.mult))
                step(dve.tensor_tensor(s2[:, :, :, :], pwb(1), big(bc[:, 1, :, :]), ALU.mult))
                step.mark(dve.tensor_tensor(tp[:, 0:SB, 0:ST, :], s1[:, 0:SB, :, :], s2[:, 0:SB, :, :], ALU.add))
                step(dve.tensor_tensor(tp[:, SB:GDN, ST - 1:TAPS, :], s1[:, SB:GDN, :, :], s2[:, SB:GDN, :, :], ALU.add))
                dve.tensor_scalar(x1[:, :, :], bc[:, 2, :, :], sign[:, 1:2], None, ALU.mult).then_inc(sm["powers"], 1)
                step.mark(dve.tensor_tensor(s1[:, :, :, :], pwb(2), big(bc[:, 2, :, :]), ALU.mult))
                step(dve.tensor_tensor(s2[:, :, :, :], pwb(3), big(bc[:, 3, :, :]), ALU.mult))
                dve.tensor_tensor(w2[:, :, :, :], s1[:, :, :, :], s2[:, :, :, :], ALU.subtract).then_inc(sm["w2_ready"], 1)
                dve.wait_ge(sm["w2_ready"], i + 1)
                dve.sem_inc(sm["bc_free"], 1)
                dve.wait_ge(sm["sined"], i + 1)
                dve.wait_ge(sm["swapped"], i + 1)
                flat = lambda x: x[:, :, :].rearrange("p g c -> p (g c)")
                wide = lambda x: x[:, :, :].rearrange("p a c -> p (a c)")
                step.mark(dve.tensor_tensor(flat(th), flat(cosT), flat(e), ALU.mult))
                step(dve.tensor_tensor(flat(th2), flat(sinT), wide(pS), ALU.mult))
                step(dve.tensor_tensor(flat(th), flat(th), flat(th2), ALU.add))
                N = SB * SN
                for d in range(2):
                    way = slice(0, N) if d == 0 else slice(2 * N - 1, N - 1, -1)
                    x = dve.tensor_tensor_scan(flat(gg)[:, way], flat(decay)[:, way], flat(th)[:, way], 0.0, ALU.mult, ALU.add)
                    x.then_inc(sm["scanned"], 1)
                dve.wait_ge(sm["scanned"], i * 2 + 2)
                step(dve.tensor_tensor(flat(th), flat(cosT), flat(gg), ALU.mult))
                dve.wait_ge(sm["swapped2"], i + 1)
                step(dve.tensor_tensor(flat(th2), flat(sinT), wide(pS), ALU.mult))
                step.mark(dve.tensor_tensor(hs[:, 0:SB, 1:SN + 1], th[:, 0:SB, :], th2[:, 0:SB, :], ALU.subtract))
                dve.tensor_tensor(hs[:, SB:GDN, 0:SN], th[:, SB:GDN, :], th2[:, SB:GDN, :], ALU.subtract).then_inc(sm["h_ready"], 1)
                dve.wait_ge(sm["y_done"], i + 1)
                here = bass.ds(i * SB, SB)
                dve.tensor_tensor(h2[0:SN, here, :], pY[0:SN, :, :].rearrange("p a (g x) -> p (a g) x", x=P),
                                  h2[0:SN, here, :], ALU.add).then_inc(sm["z_done"], 1)
                step.leave(SG // SB)

        @block.scalar
        def _(act):
            with act.Fori(0, SG // SB) as i:
                act.activation(ub[:, :, :], u[:, bass.ds(i * SB, SB), :], ACT.Copy).then_inc(sm["ub_copied"], 1)
                act.wait_ge(sm["tabled"], i + 1)
                act.activation(sinT[:, :, :], th[:, :, :], ACT.Sin)
                act.activation(cosT[:, :, :], th2[:, :, :], ACT.Sin).then_inc(sm["sined"], 1)
                for n in range(4):
                    act.wait_ge(sm["w1_turned"], i * 4 + (n + 1))
                    act.activation(w1[:, n * 4:(n + 1) * 4, :], pA[:, n % 2, :].rearrange("p (g s) -> p g s", s=P),
                                   ACT.Copy).then_inc(sm["w1_copied"], 1)
                for n in range(2):
                    act.wait_ge(sm["ended"], i * 2 + (n + 1))
                    act.activation(e[:, n * SB:(n + 1) * SB, :], pE[:, n, :].rearrange("p (g c) -> p g c", c=SN),
                                   ACT.Copy).then_inc(sm["e_copied"], 1)
                for n in range(2):
                    act.wait_ge(sm["d_made"], i * 2 + (n + 1))
                    act.activation(dm[:, n * 4:(n + 1) * 4, :], pA[:, n, :].rearrange("p (g s) -> p g s", s=P),
                                   ACT.Copy).then_inc(sm["d_copied"], 1)
                act.wait_ge(sm["z_done"], i + 1)

        @block.tensor
        def _(pe):
            ident = core.mats["ident"]
            with pe.Fori(0, SG // SB) as i:
                pe.wait_ge(sm["powers"], i + 1)
                for n in range(4):
                    if n >= 2:
                        pe.wait_ge(sm["w1_copied"], i * 4 + (n - 1))
                    for q in range(4):
                        gd = n * 4 + q
                        t0 = 0 if gd < SB else ST - 1
                        last = pe.transpose(pA[:, n % 2, q * P:(q + 1) * P], tp[:, gd, t0:t0 + ST, :], ident[:, :])
                    last.then_inc(sm["w1_turned"], 1)
                pe.wait_ge(sm["ub_copied"], i + 1)
                for d in range(2):
                    pe.wait_ge(sm["w1_copied"], i * 4 + (2 * d + 2))
                    for g in range(SB):
                        last = pe.matmul(pE[:, d, g * SN:(g + 1) * SN], w1[:, d * SB + g, :], ub[:, g, :], start=True, stop=True)
                    last.then_inc(sm["ended"], 1)
                for d in range(2):
                    pe.wait_ge(sm["e_copied"], i * 2 + (d + 1))
                    last = pe.matmul(pS[:, d, :], swap[:, :], e[:, d * SB:(d + 1) * SB, :], start=True, stop=True)
                last.then_inc(sm["swapped"], 1)
                for g in range(SB):
                    for t in range(ST):
                        for d in range(2):
                            last = pe.matmul(pA[:, g // 4, (g % 4) * P + t * SC:(g % 4) * P + (t + 1) * SC],
                                             tp[:, d * SB + g, ST - 1 - t:TAPS - t, :], x1[:, d * SB + g, :],
                                             start=(d == 0), stop=(d == 1))
                    if g % 4 == 3:
                        last.then_inc(sm["d_made"], 1)
                pe.wait_ge(sm["scanned"], i * 2 + 2)
                for d in range(2):
                    last = pe.matmul(pS[:, d, :], swap[:, :], gg[:, d * SB:(d + 1) * SB, :], start=True, stop=True)
                last.then_inc(sm["swapped2"], 1)
                pe.wait_ge(sm["h_ready"], i + 1)
                pe.wait_ge(sm["d_copied"], i * 2 + 2)
                pe.wait_ge(sm["w2_ready"], i + 1)
                for g in range(SB):
                    y = pY[0:SN, g // 4, (g % 4) * P:(g % 4 + 1) * P]
                    pe.matmul(y, ub[:, g, :], dm[:, g, :], start=True, stop=False)
                    for d in range(2):
                        last = pe.matmul(y, hs[:, d * SB + g, d:d + SN], w2[:, d * SB + g, :, :], start=False, stop=(d == 1))
                last.then_inc(sm["y_done"], 1)


def s5_from_chunks(core, z, zT):
    with Stage(core) as st:
        zt = st.sb("zt", [SN, ST, D])
        pt = st.ps("pt", [P, 4, 512])
        turned, copied, activated = (st.sem(n) for n in ("turned", "copied", "activated"))
        block = st.block()

        @block.scalar
        def _(act):
            for t in range(ST):
                act.activation(zt[0:SN, t, :].rearrange("p (g c) -> p g c", c=SC), z[0:SN, :, t * SC:(t + 1) * SC],
                               ACT.Gelu_apprx_tanh).then_inc(activated, 1)

        @block.tensor
        def _(pe):
            pe.wait_ge(activated, ST)
            for k in range(KT):
                if k >= 4:
                    pe.wait_ge(copied, k - 3)
                for t in range(ST):
                    last = pe.transpose(pt[:, k % 4, t * SN:(t + 1) * SN], zt[0:SN, t, k * P:(k + 1) * P],
                                        core.mats["ident"][0:SN, 0:SN])
                last.then_inc(turned, 1)

        @block.vector
        def _(dve):
            for k in range(KT):
                dve.wait_ge(turned, k + 1)
                dve.tensor_copy(zT[:, k, :].rearrange("p (c t) -> p t c", t=ST),
                                pt[:, k % 4, :].rearrange("p (t c) -> p t c", c=SN)).then_inc(copied, 1)


def second_mixer1(core):
    modulated_norm(core, 2)
    with Stage(core) as st:
        h2 = st.sb("h2", [SN, SG, P])
        with Stage(core) as st2:
            u = st2.sb("u", [P, SG, SN])
            s5_to_chunks(core, h2, u)
            flat = core.hT[:, :, :].rearrange("p k s -> p (k s)")
            pb = flat[:, 0:4 * SG * ST].rearrange("p (q n k) -> p q n k", q=2, k=ST)
            pc = flat[:, 4 * SG * ST:8 * SG * ST].rearrange("p (q n k) -> p q n k", q=2, k=ST)
            r8, th8 = st2.sb("r8", [P, 2 * SG]), st2.sb("th8", [P, 2 * SG])
            s5_powers(core, pb, pc, r8, th8)
            s5_scan(core, h2, u, pb, pc, r8, th8)
        s5_from_chunks(core, h2, core.hT)
    with Stage(core) as st:
        gate = st.sb("gate", [P, KT, S])
        lin = st.sb("lin", [P, KT, S])
        linear(core, core.dram["w_glu_b"], KT, 512, 2, core.hT, tiles_to(gate, 4, ACT.Sigmoid))
        linear(core, core.dram["w_glu_a"], KT, 512, 2, core.hT, tiles_to(lin, 4))
        with Stage(core) as st2:
            v_step = st2.sem("v_step")
            block = st2.block()

            @block.vector
            def _(dve):
                step = Steps(dve, v_step)
                step(dve.tensor_tensor(gate[:, :, :], gate[:, :, :], lin[:, :, :], ALU.mult))
                at = gate_col(2)
                for k in range(KT):
                    dve.scalar_tensor_tensor(core.xT[:, k, :], gate[:, k, :], core.mod[:, at + k:at + k + 1],
                                             core.xT[:, k, :], ALU.mult, ALU.add)


def final_norm(core):
    norm(core, core.col("norm_f"), out=core.xT)


def lay_out_more(f, d):
    d["w_peer"] = by_chunks(f["peer_wq"][0], 512)
    d["sub_keys"] = f["peer_subkeys"][0].reshape(2 * PH, PN, P).transpose(2, 0, 1).reshape(P, -1)
    d["peer_u"], d["peer_v"] = f["peer_u"][0], f["peer_v"][0]
    d["pT"] = by_chunks(f["p"][0, 0].T, S)
    d["w_ple_gate"] = by_chunks(f["ple_gate"][0], 512)
    d["w_ple_proj"] = by_chunks(f["ple_proj"][0], 512)
    d["ada_w"] = np.concatenate([by_chunks(f["ada_w_2"][i], 512) for i in range(2)])
    w = f["w_in_2"][0]
    for i, name in enumerate(("w2_val", "w2_gate")):
        d[name] = by_chunks(w[:, i * MA:(i + 1) * MA], 256)
    d["w2_qk"] = by_chunks(w[:, 2 * MA:4 * MA], 512)
    d["w2_v"] = by_chunks(w[:, 4 * MA:5 * MA], 256)
    d["w2_g"] = by_chunks(w[:, 5 * MA:], 256)
    d["w2_out"] = by_chunks(f["w_out_2"][0], 512)
    for i in range(2):
        d[f"w_fc1_{i}"] = by_chunks(f["w_fc1_2"][i], 512)
        w = f["w_fc2_2"][i].reshape(FF // D, D, 2, 512)
        d[f"w_fc2_{i}"] = np.concatenate([by_chunks(w[k, :, n], 512) for n in range(2) for k in range(FF // D)])
    d["w_glu_a"], d["w_glu_b"] = (by_chunks(f[n][0], 512) for n in ("w_glu_a_2", "w_glu_b_2"))
    d["s5_d"] = f["s5_d_2"]
    b = [f[n][0].transpose(2, 0, 1, 3) for n in ("s5_b_re_2", "s5_b_im_2")]
    c = [f[n][0].transpose(3, 0, 1, 2) for n in ("s5_c_re_2", "s5_c_im_2")]
    four = np.stack([np.concatenate(p, 0) for p in (b, b[::-1], c, c[::-1])], 1)
    d["s5_bc"] = (four.reshape(P, 4, 2, SG // SB, SB, SC).transpose(3, 0, 1, 2, 4, 5).reshape(SG // SB * P, -1))


def build(nc, dram, out):
    core = Core(nc, dram)
    with ExitStack() as ctx:
        def sb(name, shape):
            return ctx.enter_context(nc.sbuf_tensor(name, shape, F32))

        core.xT = sb("xT", [P, KT, S])
        core.hT = sb("hT", [P, KT, S])
        core.cols = sb("cols", [P, N_COLS])
        core.mats = {n: sb(n, [P, P]) for n in ("ident", "ones", "ones64", "rot_att")}
        core.mod, core.gain = sb("mod", [P, 12 * KT]), sb("gain", [P, 4 * KT])
        load_stage(core)
        for stage in STAGES:
            stage(core)
        with Stage(core) as st:
            written = st.sem("written")
            block = st.block()

            @block.sync
            def _(sp):
                sp.dma_start(out.rearrange("p (k s) -> p k s", k=KT), core.xT[:, :, :]).then_inc(written, 16)
                sp.wait_ge(written, 16)


def by_chunks(w, width):
    k, n = w.shape
    return np.ascontiguousarray(
        w.reshape(k // P, P, n // width, width).transpose(2, 1, 0, 3).reshape(-1, k // P * width))


def columns(v):
    return v.reshape(-1, P).T


def lay_out(a):
    f = {n: np.asarray(v) for n, v in a.items()}
    w_in, d = f["w_in"][0], {}
    d["xT"] = by_chunks(f["x"][0].T, S)
    o = np.cumsum([0, AH * AD, AKV * AD, AKV * AD, 512, 512, 512, 512, 512, 2048])
    part = [w_in[:, o[i]:o[i + 1]] for i in range(9)]
    pair = np.arange(AH).reshape(2, 4).T.reshape(-1)
    d["w_qk"] = by_chunks(np.concatenate([part[0].reshape(D, AH, AD)[:, pair].reshape(D, -1), part[1], part[2]], 1), 384)
    d["w_v"] = by_chunks(part[2], 64)
    d["w_hg_silu"] = by_chunks(np.concatenate([part[3], part[7]], 1), 512)
    d["w_hg_f"] = by_chunks(np.concatenate([part[4], part[5]], 1), 512)
    d["w_hg_v"] = by_chunks(part[6], 256)
    d["w_gates"] = by_chunks(part[8], 512)
    d["w_up_att"] = by_chunks(f["w_up_att"][0].reshape(AH, AD, D)[pair].reshape(-1, D), 512)
    d["w_up_hg"] = by_chunks(f["w_up_hg"][0], 512)
    d["w_out"] = by_chunks(f["w_out"][0], 512)
    twice = lambda v: np.concatenate([v, v], 0)
    state_cols = lambda v: twice(v[0].reshape(2 * SG, SP).T)
    cols = {
        "norm_mix": columns(f["norm_mix"]), "norm_ffn": columns(f["norm_ffn"]), "norm_ple": columns(f["norm_ple"]),
        "q_norm": twice(f["q_norm"].T), "k_norm": twice(f["k_norm"].T), "hg_out_norm": f["hg_out_norm"].T,
        "lb_raw": columns(f["hg_lb_raw"]), "norm_g": columns(f["norm_g_2"]), "ada_b": columns(f["ada_b_2"]),
        "conv_b": columns(f["conv_b_2"]), "cln_g": columns(f["cln_g_2"]), "cln_b": columns(f["cln_b_2"]),
        "conv_w": f["conv_w_2"][0].reshape(CW, 4, P).transpose(2, 1, 0).reshape(P, -1),
        "norm_f": columns(f["norm_f_2"]), "c": columns(f["c_2"]),
        "s5_lr": state_cols(f["s5_lam_re_2"]), "s5_li": state_cols(f["s5_lam_im_2"]),
        "s5_step": np.broadcast_to(f["s5_log_step_2"].reshape(1, -1), (P, 2 * SG)),
    }
    d["cols"] = np.ascontiguousarray(np.concatenate([cols[n] for n, _ in COLS], 1))
    lay_out_more(f, d)
    d["consts"] = constants()
    return {n: np.ascontiguousarray(v) for n, v in d.items()}


def kernel(**inputs):
    import concourse.bacc as bacc
    from concourse.bass_utils import run_bass_kernel_spmd

    nc = bacc.Bacc("TRN2", target_bir_lowering=False, num_devices=1)
    arrays = lay_out(inputs)
    dram = {n: nc.dram_tensor("in_" + n, v.shape, F32, kind="ExternalInput").ap() for n, v in arrays.items()}
    out = nc.dram_tensor("out", (P, KT * S), F32, kind="ExternalOutput").ap()
    build(nc, dram, out)
    r = run_bass_kernel_spmd(nc, [{"in_" + n: v for n, v in arrays.items()}], core_ids=[0])
    y = np.asarray(r.results[0]["out"]).reshape(P, KT, S)
    return np.ascontiguousarray(y.transpose(2, 1, 0).reshape(1, S, D))


STAGES = [first_mixer,peer,ple,second_mixer0,feed_forward0,second_mixer1,feed_forward1,final_norm]
```

```python
from contextlib import ExitStack

import numpy as np

import concourse.bass as bass
from concourse import mybir

F32 = mybir.dt.float32
U32 = mybir.dt.uint32
ALU = mybir.AluOpType
ACT = mybir.ActivationFunctionType
AX = mybir.AxisListType

P = 128
S = 512
D = 1024
KT = D // P
TT = S // P
EPS = 1e-6

AH, AKV, AD = 8, 2, 64
GH, GD = 4, 128
GC, GB = 64, 16
NCH, NBL = S // GC, GC // GB
PH, PK, PN, PX = 8, 16, 128, 128 * 128
RH = 4
MA = D // 2
CW = 31
FF = 4 * D
SG, SC, SP = 64, 16, 64
ST = 8
SN = S // ST
SB = 4
NEG = -3.0e38
ROUND = 12582912.0

COLS = [("norm_mix", KT), ("norm_ffn", KT), ("norm_ple", KT), ("q_norm", 1), ("k_norm", 1),
        ("hg_out_norm", 1), ("lb_raw", 16), ("norm_g", 4 * KT), ("ada_b", 12 * KT), ("conv_b", 4),
        ("cln_g", 4), ("cln_b", 4), ("conv_w", 4 * CW), ("norm_f", KT), ("c", KT),
        ("s5_lr", 2 * SG), ("s5_li", 2 * SG), ("s5_step", 2 * SG)]
COL_AT = {}
_n = 0
for _name, _k in COLS:
    COL_AT[_name] = (_n, _k)
    _n += _k
N_COLS = _n

CONSTS = [("ident", P), ("ones", P), ("ones64", P), ("rot_att", P), ("rot_ret", P), ("swap_s5", P),
          ("sign", 2), ("reset", 2 * S), ("causal", 2 * TT * GC), ("cos_att", S), ("sin_att", S),
          ("cos_ret", S), ("sin_ret", S), ("decay", RH * TT * S), ("iota16", PK),
          ("chunk_no", 2 * SB * SN), ("chunk_keep", 2 * SB * SN), ("power_b", 2 * SG * ST),
          ("power_c", 2 * SG * ST)]
CONST_AT = {}
_n = 0
for _name, _k in CONSTS:
    CONST_AT[_name] = (_n, _k)
    _n += _k
N_CONSTS = _n


def constants():
    t = {}
    t["ident"] = np.eye(P)
    t["ones"] = np.ones((P, P))
    t["ones64"] = np.kron(np.eye(2), np.ones((64, 64)))
    pos = np.arange(S)
    inv = (np.float32(10000.0) ** (-np.arange(16, dtype=np.float32) / np.float32(16))).astype(np.float32)
    axis = np.stack([pos // 64, pos % 64]).astype(np.float32)
    ang = (axis[:, None, :] * inv[None, :, None]).astype(np.float32).astype(np.float64)
    ang = np.broadcast_to(ang[:, None], (2, 2, 16, S)).reshape(64, S)
    t["cos_att"], t["sin_att"] = (np.tile(f(ang), (2, 1)) for f in (np.cos, np.sin))
    rot = np.zeros((P, P))
    for c in range(P):
        if (c // 16) % 2 == 0:
            rot[c + 16, c] = -1.0
        else:
            rot[c - 16, c] = 1.0
    t["rot_att"] = rot
    inv = (np.float32(10000.0) ** (-np.arange(0, P, 2, dtype=np.float32) / np.float32(P))).astype(np.float32)
    ang = (pos[None, :].astype(np.float32) * inv[:, None]).astype(np.float32).astype(np.float64)
    t["cos_ret"], t["sin_ret"] = (np.tile(f(ang), (2, 1)) for f in (np.cos, np.sin))
    rot = np.zeros((P, P))
    swap = np.zeros((P, P))
    for c in range(64):
        rot[c + 64, c], rot[c, c + 64] = -1.0, 1.0
        swap[c + 64, c], swap[c, c + 64] = 1.0, -1.0
    t["rot_ret"], t["swap_s5"] = rot, swap
    sign = np.ones((P, 2))
    sign[:64, 0] = -1.0
    sign[64:, 1] = -1.0
    t["sign"] = sign
    reset = np.ones((2, S))
    reset[0, 0::GC] = 0.0
    reset[1, GC - 1::GC] = 0.0
    t["reset"] = np.broadcast_to(reset.reshape(-1), (P, 2 * S))
    s = np.arange(P) % GC
    c = np.arange(GC)
    mask = np.stack([s[:, None] <= c[None], s[:, None] >= c[None]], 1).astype(float)
    t["causal"] = np.broadcast_to(mask[:, :, None], (P, 2, TT, GC)).reshape(P, -1)
    lg = np.log1p(-np.exp2(-5.0 - np.arange(RH)))
    m = np.arange(P)[:, None] + P * np.arange(TT)[None]
    t["decay"] = np.exp(lg[None, :, None, None] * np.abs(m[:, None, :, None] - pos)).reshape(P, -1)
    t["iota16"] = np.broadcast_to(np.arange(PK), (P, PK))
    no = np.arange(SN)
    t["chunk_no"] = np.broadcast_to(np.stack([no, SN - 1 - no])[:, None], (2, SB, SN)).reshape(1, -1)
    keep = np.ones((2, SN))
    keep[0, 0] = keep[1, -1] = 0.0
    t["chunk_keep"] = np.broadcast_to(keep[:, None], (2, SB, SN)).reshape(1, -1)
    d = np.arange(ST)
    t["power_b"] = np.broadcast_to(np.stack([ST - 1 - d, d])[:, None], (SG // SB, 2, SB, ST)).reshape(1, -1)
    t["power_c"] = np.broadcast_to(np.stack([d + 1, ST - d])[:, None], (SG // SB, 2, SB, ST)).reshape(1, -1)
    out = np.concatenate([np.broadcast_to(t[n], (P, k)) for n, k in CONSTS], 1)
    return np.ascontiguousarray(out, dtype=np.float32)


def wait_apart(eng, sem, value, passed):
    eng.wait_ge(sem, value)
    eng.sem_inc(passed, 1)


class Steps:

    def __init__(self, eng, sem):
        self.eng, self.sem, self.base, self.n = eng, sem, 0, 0

    def mark(self, ins):
        self.n += 1
        ins.then_inc(self.sem, 1)

    def wait(self, lag=0):
        self.eng.wait_ge(self.sem, self.base + (self.n - lag))

    def __call__(self, ins):
        self.mark(ins)
        self.wait()

    def enter(self, i, per):
        self.start, self.per = self.base + self.n, per
        self.base, self.n = i * per + self.start, 0

    def leave(self, count):
        assert self.n == self.per, (self.n, self.per)
        self.base, self.n = self.start + count * self.per, 0


class Core:

    def __init__(self, nc, dram):
        self.nc, self.dram, self.stages, self.spent = nc, dram, 0, []

    def const(self, name):
        at, n = CONST_AT[name]
        return self.dram["consts"][:, at:at + n]

    def col(self, name, at=0, n=None):
        a, k = COL_AT[name]
        return self.cols[:, a + at:a + at + (k - at if n is None else n)]


class Stage:

    def __init__(self, core):
        core.stages += 1
        self.nc, self.ctx, self.tag = core.nc, ExitStack(), f"_{core.stages}"
        self.sems, self.core = [], core

    def __enter__(self):
        if len(self.nc.free_semaphores) < 60 and self.core.spent:
            self.nc.clear_and_free_semaphores(self.core.spent)
            self.nc.all_engine_barrier()
            self.core.spent = []
        self.ctx.__enter__()
        return self

    def __exit__(self, *a):
        self.ctx.__exit__(*a)
        self.core.spent += self.sems

    def sb(self, name, shape, dt=F32):
        return self.ctx.enter_context(self.nc.sbuf_tensor(name + self.tag, shape, dt))

    def ps(self, name, shape):
        return self.ctx.enter_context(self.nc.psum_tensor(name + self.tag, shape, F32))

    def sem(self, name):
        self.sems.append(self.nc.alloc_semaphore(name + self.tag))
        return self.sems[-1]

    def block(self):
        return self.ctx.enter_context(self.nc.Block())


def load_stage(core):
    with Stage(core) as st:
        landed = st.sem("landed")
        block = st.block()

        @block.sync
        def _(sp):
            loads = [(core.xT[:, :, :], core.dram["xT"].rearrange("p (k s) -> p k s", k=KT)),
                     (core.cols[:, :], core.dram["cols"][:, :])]
            for name, tile in core.mats.items():
                loads.append((tile[:, :], core.const(name)))
            for dst, src in loads:
                sp.dma_start(dst, src).then_inc(landed, 16)
            sp.wait_ge(landed, 16 * len(loads))


class Modulation:
    RING, PER, PARTS = 4, 2, 3

    def __init__(self, core, st, part):
        self.core, self.part, R = core, part, self.RING
        self.c = st.sb("c_row", [P, D])
        self.ring = st.sb("ada_ring", [P, R, self.PER, D])
        self.c_landed, self.silu, self.multiplied, self.added = (st.sem(n) for n in ("c_landed", "silu", "ada_multiplied", "added"))
        self.landed = [st.sem(f"ada_landed{s}") for s in range(R)]
        self.loads = 12 * KT // self.PARTS // self.PER

    def gpsimd(self, pool):
        at = self.part * self.loads * P
        w = self.core.dram["ada_w"][at:at + self.loads * P, :]

        def load(s, rows):
            pool.dma_start(self.ring[:, s, :, :].rearrange("p a d -> p (a d)"), rows).then_inc(self.landed[s], 16)

        pool.dma_start(self.c[:, :], self.core.dram["c_row"][:, :].partition_broadcast(P)).then_inc(self.c_landed, 16)
        for s in range(self.RING):
            load(s, w[s * P:(s + 1) * P, :])
        with pool.Fori(1, self.loads // self.RING) as i:
            for s in range(self.RING):
                pool.wait_ge(self.multiplied, (i * self.RING + (s + 1 - self.RING)) * self.PER)
                load(s, w[bass.ds((i * self.RING + s) * P, P), :])

    def scalar(self, act):
        act.wait_ge(self.c_landed, 16)
        act.activation(self.c[:, :], self.c[:, :], ACT.Silu).then_inc(self.silu, 1)

    def vector(self, dve):
        mod = self.core.mod
        dve.wait_ge(self.silu, 1)
        with dve.Fori(0, self.loads // self.RING) as i:
            for s in range(self.RING):
                dve.wait_ge(self.landed[s], i * 16 + 16)
                for j in range(self.PER):
                    dve.scalar_tensor_tensor(
                        self.ring[:, s, j, :], self.ring[:, s, j, :], 1.0, self.c[:, :], ALU.mult, ALU.mult,
                        accum_out=mod[:, bass.ds(i * (self.RING * self.PER) + (self.part * self.loads * self.PER + s * self.PER + j), 1)],
                    ).then_inc(self.multiplied, 1)
        if self.part < self.PARTS - 1:
            return
        dve.wait_ge(self.multiplied, self.loads * self.PER)
        dve.tensor_tensor(mod[:, :], mod[:, :], self.core.col("ada_b"), ALU.add).then_inc(self.added, 1)
        dve.wait_ge(self.added, 1)
        scale = mod[:, :].rearrange("p (n c k) -> p n c k", c=3, k=KT)[:, :, 1, :]
        gain = self.core.gain[:, :].rearrange("p (n k) -> p n k", k=KT)
        norm_g = self.core.col("norm_g").rearrange("p (n k) -> p n k", k=KT)
        dve.tensor_tensor(gain, scale, norm_g, ALU.mult).then_inc(self.added, 1)
        dve.wait_ge(self.added, 2)
        dve.tensor_tensor(gain, gain, norm_g, ALU.add)


def linear(core, w, kt, width, chunks, src, evac, token_major=False, engine="scalar", after=None, beside=None):
    banks = TT if token_major else width // P
    n = width if token_major else S
    with Stage(core) as st:
        ring = st.sb("ring", [P, 2, kt * width])
        acc = st.ps("acc", [P, 2, 4, 512])
        landed = [st.sem("landed0"), st.sem("landed1")]
        some = min(2, kt)
        part_landed = [st.sem(f"part_landed{i}") for i in range(kt // some)]
        multiplied, slot_free = st.sem("multiplied"), st.sem("slot_free")
        side = beside(core, st) if beside else None
        block = st.block()

        @block.sync
        def _(sp):
            for i, sem in enumerate(part_landed):
                part = slice(i * some * width, (i + 1) * some * width)
                sp.dma_start(ring[:, 0, part], w[0:P, part]).then_inc(sem, 16)
            sp.dma_start(ring[:, 1, :], w[P:2 * P, :]).then_inc(landed[1], 16)
            if chunks > 2:
                with sp.Fori(1, chunks // 2) as i:
                    for s in range(2):
                        sp.wait_ge(multiplied, i * 2 - 1 + s)
                        sp.dma_start(ring[:, s, :], w[bass.ds((i * 2 + s) * P, P), :]).then_inc(landed[s], 16)

        def product(pe, s, j, k):
            wk = ring[:, s, k * width:(k + 1) * width]
            if token_major:
                lhsT, rhs = src[:, k, j * P:(j + 1) * P], wk
            else:
                lhsT, rhs = wk[:, j * P:(j + 1) * P], src[:, k, :]
            return pe.matmul(acc[:, s, j, 0:n], lhsT, rhs, start=(k == 0), stop=(k == kt - 1))

        def multiply(pe, s):
            for j in range(banks):
                for k in range(kt):
                    last = product(pe, s, j, k)
            last.then_inc(multiplied, 1)

        @block.tensor
        def _(pe):
            for i, sem in enumerate(part_landed):
                pe.wait_ge(sem, 16)
                for j in range(banks):
                    for k in range(i * some, (i + 1) * some):
                        last = product(pe, 0, j, k)
            last.then_inc(multiplied, 1)
            pe.wait_ge(landed[1], 16)
            multiply(pe, 1)
            if chunks > 2:
                with pe.Fori(1, chunks // 2) as i:
                    for s in range(2):
                        pe.wait_ge(landed[s], i * 16 + (16 if s else 0))
                        pe.wait_ge(slot_free, i * 2 - 1 + s)
                        multiply(pe, s)

        def take_out(eng):
            with eng.Fori(0, chunks // 2) as i:
                for s in range(2):
                    eng.wait_ge(multiplied, i * 2 + 1 + s)
                    for j in range(banks):
                        last = evac(eng, i * 2 + s, j, acc[:, s, j, 0:n])
                    last.then_inc(slot_free, 1)

        if after is not None:
            @block.vector
            def _(dve):
                with dve.Fori(0, chunks // 2) as i:
                    for s in range(2):
                        dve.wait_ge(slot_free, i * 2 + 1 + s)
                        after(dve, i * 2 + s)

        if side:
            block.gpsimd(side.gpsimd)
            block.vector(side.vector)

        if engine == "scalar":
            @block.scalar
            def _(act):
                if side:
                    side.scalar(act)
                take_out(act)
        else:
            @block.vector
            def _(dve):
                take_out(dve)


def tiles_to(dst, per, func=None, scale=1.0):
    def evac(act, c, j, bank):
        out = dst[:, bass.ds(c * per + j, 1), :].rearrange("p a s -> p (a s)")
        return act.activation(out, bank, func or ACT.Copy, scale=scale)
    return evac


def tokens_to(dst, width):
    def evac(act, c, j, bank):
        return act.activation(dst[:, j, bass.ds(c * width, width)], bank, ACT.Copy)
    return evac


def add_to_x(core, per, gate=None, gate_at=0):
    def evac(dve, c, j, bank):
        x = core.xT[:, bass.ds(c * per + j, 1), :].rearrange("p a s -> p (a s)")
        if gate is None:
            return dve.tensor_tensor(x, bank, x, ALU.add)
        return dve.scalar_tensor_tensor(x, bank, gate[:, bass.ds(c * per + j + gate_at, 1)], x,
                                        ALU.mult, ALU.add)
    return evac


def norm(core, gain, bias=None, out=None):
    out = core.hT if out is None else out
    HALF, MINE = KT // 2, 5
    with Stage(core) as st:
        sq = st.sb("sq", [P, KT, S])
        rstd = st.sb("rstd", [P, S])
        ms = st.ps("ms", [P, S])
        squared, squared2, summed, v_step, rooted, scaled, scaled2 = (st.sem(n) for n in (
            "squared", "squared2", "summed", "v_step", "rooted", "scaled", "scaled2"))
        block = st.block()

        @block.scalar
        def _(act):
            for k in range(HALF):
                act.activation(sq[:, k, :], core.xT[:, k, :], ACT.Square).then_inc(squared, 1)
            act.wait_ge(v_step, 1)
            act.activation(rstd[:, :], rstd[:, :], ACT.Sqrt).then_inc(rooted, 1)
            if bias is not None:
                for k in range(MINE):
                    act.wait_ge(scaled, k + 1)
                    act.activation(out[:, k, :], out[:, k, :], ACT.Identity, bias=bias[:, k:k + 1])
            for k in range(MINE, KT):
                act.wait_ge(scaled2, k - MINE + 1)
                if bias is None:
                    act.activation(out[:, k, :], out[:, k, :], ACT.Copy, scale=gain[:, k:k + 1])
                else:
                    act.activation(out[:, k, :], out[:, k, :], ACT.Identity, scale=gain[:, k:k + 1], bias=bias[:, k:k + 1])

        @block.tensor
        def _(pe):
            for n in range(KT):
                k = n // 2 + HALF * (n % 2)
                pe.wait_ge(squared2 if n % 2 else squared, n // 2 + 1)
                last = pe.matmul(ms[:, :], core.mats["ones"][:, :], sq[:, k, :], start=(n == 0), stop=(n == KT - 1))
            last.then_inc(summed, 1)

        @block.vector
        def _(dve):
            for k in range(HALF, KT):
                dve.tensor_tensor(sq[:, k, :], core.xT[:, k, :], core.xT[:, k, :], ALU.mult).then_inc(squared2, 1)
            step = Steps(dve, v_step)
            dve.wait_ge(summed, 1)
            step(dve.tensor_scalar(rstd[:, :], ms[:, :], 1.0 / D, EPS, ALU.mult, ALU.add))
            dve.wait_ge(rooted, 1)
            step(dve.reciprocal(rstd[:, :], rstd[:, :]))
            for k in range(MINE):
                dve.scalar_tensor_tensor(out[:, k, :], core.xT[:, k, :], gain[:, k:k + 1], rstd[:, :],
                                         ALU.mult, ALU.mult).then_inc(scaled, 1)

        @block.gpsimd
        def _(pool):
            pool.wait_ge(v_step, 2)
            for k in range(MINE, KT):
                pool.tensor_tensor(out[:, k, :], core.xT[:, k, :], rstd[:, :], ALU.mult).then_inc(scaled2, 1)


def attention(core, qT, kT, v, yT):
    UNITS = [(a, t) for a in range(2) for t in range(TT)]
    with Stage(core) as st:
        cs = st.sb("cs", [P, 2, S])
        kr = st.sb("kr", [P, S])
        qr = st.sb("qr", [P, S])
        sq, xn, a1, a2, rstd = (st.sb(n, [P, S]) for n in ("sq", "xn", "a1", "a2", "rstd"))
        prob = st.sb("prob", [P, 4, S])
        probT = st.sb("probT", [P, TT, 2, S])
        stat = st.sb("stat", [P, 3, 8])
        sc = st.ps("sc", [P, 4, S])
        pt = st.ps("pt", [P, 2, S])
        po = st.ps("po", [P, 2, S])
        pn, pr = po[:, 0, :], po[:, 1, :]
        landed, squared, summed, v_step, rooted, normed, turned, rotated = (
            st.sem(n) for n in ("landed", "squared", "summed", "v_step", "rooted", "normed", "turned", "rotated"))
        st_unit = st.sem("unit_step")
        scored, maxed, expd, scaled, transposed, copied, mixed, out_done = (
            st.sem(n) for n in ("scored", "maxed", "expd", "scaled", "transposed", "copied", "mixed", "out_done"))
        block = st.block()

        @block.sync
        def _(sp):
            sp.dma_start(cs[:, 0, :], core.const("cos_att")).then_inc(landed, 16)
            sp.dma_start(cs[:, 1, :], core.const("sin_att")).then_inc(landed, 16)

        def turn_tensor(pe, n):
            pe.wait_ge(squared, n)
            pe.matmul(pn, core.mats["ones64"][:, :], sq[:, :], start=True, stop=True).then_inc(summed, 1)
            pe.wait_ge(normed, n)
            pe.matmul(pr, core.mats["rot_att"][:, :], xn[:, :], start=True, stop=True).then_inc(turned, 1)

        def turn_scalar(act, n, src):
            act.activation(sq[:, :], src, ACT.Square).then_inc(squared, 1)
            act.wait_ge(v_step, (n - 1) * 4 + 1)
            act.activation(rstd[:, :], rstd[:, :], ACT.Sqrt).then_inc(rooted, 1)

        def turn_vector(dve, step, n, src, gain, dst):
            dve.wait_ge(summed, n)
            step(dve.tensor_scalar(rstd[:, :], pn, 1.0 / AD, EPS, ALU.mult, ALU.add))
            dve.wait_ge(rooted, n)
            step(dve.reciprocal(rstd[:, :], rstd[:, :]))
            dve.scalar_tensor_tensor(xn[:, :], src, gain, rstd[:, :], ALU.mult, ALU.mult).then_inc(normed, 1)
            dve.wait_ge(normed, n)
            step(dve.tensor_tensor(a1[:, :], xn[:, :], cs[:, 0, :], ALU.mult))
            dve.wait_ge(turned, n)
            step(dve.tensor_tensor(a2[:, :], pr, cs[:, 1, :], ALU.mult))
            dve.tensor_tensor(dst, a1[:, :], a2[:, :], ALU.add).then_inc(rotated, 1)

        def q_tile(j):
            return qT[:, bass.ds(j, 1), :].rearrange("p a s -> p (a s)")

        @block.tensor
        def _(pe):
            turn_tensor(pe, 1)
            with pe.Fori(0, 4) as j:
                turn_tensor(pe, j + 2)
                pe.wait_ge(rotated, j + 2)

                def transposes(u):
                    a, t = UNITS[u]
                    pe.wait_ge(scaled, j * 8 + (u + 1))
                    if u >= 2:
                        pe.wait_ge(copied, j * 8 + (u - 1))
                    for b in range(TT):
                        last = pe.transpose(pt[:, u % 2, b * P:(b + 1) * P], prob[:, u % 4, b * P:(b + 1) * P],
                                            core.mats["ident"][:, :])
                    last.then_inc(transposed, 1)

                def mix(a):
                    pe.wait_ge(copied, j * 8 + (4 * a + 4))
                    for b in range(TT):
                        last = pe.matmul(po[64 * a:64 * a + 64, a, :], v[:, b, 64 * a:64 * a + 64],
                                         probT[:, b, a, :], start=(b == 0), stop=(b == TT - 1))
                    last.then_inc(mixed, 1)

                for u, (a, t) in enumerate(UNITS):
                    if u >= 4:
                        pe.wait_ge(expd, j * 8 + (u - 3))
                    pe.matmul(sc[:, u % 4, :], qr[64 * a:64 * a + 64, t * P:(t + 1) * P],
                              kr[64 * a:64 * a + 64, :], start=True, stop=True).then_inc(scored, 1)
                    if u >= 2:
                        transposes(u - 2)
                    if u == 6:
                        mix(0)
                transposes(6)
                transposes(7)
                mix(1)
                pe.wait_ge(out_done, j * 2 + 2)

        @block.scalar
        def _(act):
            turn_scalar(act, 1, kT[:, 0, :])
            with act.Fori(0, 4) as j:
                act.wait_ge(rotated, j + 1)
                turn_scalar(act, j + 2, q_tile(j))

                def copy(u):
                    a, t = UNITS[u]
                    act.wait_ge(transposed, j * 8 + (u + 1))
                    act.activation(probT[:, :, a, t * P:(t + 1) * P],
                                   pt[:, u % 2, :].rearrange("p (b q) -> p b q", b=TT),
                                   ACT.Copy).then_inc(copied, 1)

                for u in range(8):
                    act.wait_ge(maxed, j * 8 + (u + 1))
                    if u >= 4:
                        act.wait_ge(transposed, j * 8 + (u - 3))
                    act.activation(prob[:, u % 4, :], sc[:, u % 4, :], ACT.Exp, bias=stat[:, 0, u:u + 1],
                                   scale=AD ** -0.5, accum_out=stat[:, 1, u:u + 1]).then_inc(expd, 1)
                    if u >= 2:
                        copy(u - 2)
                copy(6)
                copy(7)
                for a in range(2):
                    act.wait_ge(mixed, j * 2 + (a + 1))
                    act.activation(yT[64 * a:64 * a + 64, bass.ds(j, 1), :].rearrange("p a s -> p (a s)"),
                                   po[64 * a:64 * a + 64, a, :], ACT.Copy).then_inc(out_done, 1)

        @block.vector
        def _(dve):
            step = Steps(dve, v_step)
            dve.wait_ge(landed, 32)
            turn_vector(dve, step, 1, kT[:, 0, :], core.col("k_norm"), kr[:, :])
            unit = Steps(dve, st_unit)
            with dve.Fori(0, 4) as j:
                step.enter(j, 4)
                unit.enter(j, 16)
                turn_vector(dve, step, j + 2, q_tile(j), core.col("q_norm"), qr[:, :])

                def scale(u):
                    dve.wait_ge(expd, j * 8 + (u + 1))
                    unit(dve.reciprocal(stat[:, 2, u:u + 1], stat[:, 1, u:u + 1]))
                    dve.tensor_scalar(prob[:, u % 4, :], prob[:, u % 4, :], stat[:, 2, u:u + 1], None,
                                      ALU.mult).then_inc(scaled, 1)

                for u in range(8):
                    dve.wait_ge(scored, j * 8 + (u + 1))
                    unit(dve.tensor_reduce(stat[:, 0, u:u + 1], sc[:, u % 4, :], AX.X, ALU.max))
                    dve.tensor_scalar(stat[:, 0, u:u + 1], stat[:, 0, u:u + 1], -AD ** -0.5, None,
                                      ALU.mult).then_inc(maxed, 1)
                    if u >= 1:
                        scale(u - 1)
                scale(7)
                unit.leave(4)
                step.leave(4)


def hgrn_gates(core, qT, fT, kT, lT):
    n = 2 * GH
    with Stage(core) as st:
        r = st.sb("r", [P, 6, n])
        v_step, maxed, expd, sig, kept, gated = (st.sem(x) for x in ("v_step", "maxed", "expd", "sig", "kept", "gated"))
        block = st.block()

        @block.scalar
        def _(act):
            act.wait_ge(maxed, 2)
            act.activation(r[:, 0:2, :], r[:, 0:2, :], ACT.Exp).then_inc(expd, 1)
            for d in range(2):
                act.activation(kT[:, d, :, :], fT[:, d, :, :], ACT.Sigmoid).then_inc(sig, 1)
            for d in range(2):
                act.wait_ge(kept, d + 1)
                act.activation(lT[:, d, :, :], lT[:, d, :, :], ACT.Ln)

        @block.vector
        def _(dve):
            step = Steps(dve, v_step)
            raw = [core.col("lb_raw", i * n, n) for i in range(2)]
            step(dve.tensor_tensor(r[:, 2, :], raw[0], raw[1], ALU.max))
            for i in range(2):
                dve.tensor_tensor(r[:, i, :], raw[i], r[:, 2, :], ALU.subtract).then_inc(maxed, 1)
            dve.wait_ge(expd, 1)
            step(dve.tensor_tensor(r[:, 3, :], r[:, 0, :], r[:, 1, :], ALU.add))
            step(dve.reciprocal(r[:, 3, :], r[:, 3, :]))
            step(dve.tensor_tensor(r[:, 4, :], r[:, 0, :], r[:, 3, :], ALU.mult))
            step(dve.tensor_scalar(r[:, 5, :], r[:, 4, :], -1.0, 1.0, ALU.mult, ALU.add))
            for d in range(2):
                dve.wait_ge(sig, d + 1)
                for h in range(GH):
                    i = d * GH + h
                    dve.tensor_scalar(lT[:, d, h, :], kT[:, d, h, :], r[:, 5, i:i + 1], r[:, 4, i:i + 1],
                                      ALU.mult, ALU.add).then_inc(gated, 1)
            for d in range(2):
                dve.wait_ge(gated, GH * (d + 1))
                dve.tensor_scalar(fT[:, d, :, :], lT[:, d, :, :], -1.0, 1.0, ALU.mult, ALU.add).then_inc(kept, 1)


def hgrn(core, qT, kT, lT, v, gT, oT):
    W = NCH * NBL
    with Stage(core) as st:
        reset = st.sb("reset", [P, 2, S])
        causal = st.sb("causal", [P, 2, TT, GC])
        ql, vl, gl = (st.sb(n, [P, S]) for n in ("ql", "vl", "gl"))
        kl, b = (st.sb(n, [P, 2, S]) for n in ("kl", "b"))
        qd, qe, kd = (st.sb(n, [P, 2, S]) for n in ("qd", "qe", "kd"))
        kk = st.sb("kk", [P, 2, NCH, NBL, GC])
        ebl = st.sb("ebl", [P, 2, NCH])
        kdT = st.sb("kdT", [P, 2, TT, P])
        at = st.sb("at", [P, 2, TT, GC])
        state = st.sb("state", [P, 2, P])
        sq, rstd, on = (st.sb(n, [P, S]) for n in ("sq", "rstd", "on"))
        pa = st.ps("pa", [P, 2, TT, GC])
        pk = st.ps("pk", [P, 2, TT, P])
        pst = st.ps("pst", [P, 2, 512])
        po = st.ps("po", [P, 2, 512])
        pn = st.ps("pn", [P, S])
        (landed, v_step, a_step, a_ready, k_ready, kdT_ready, a_scores, a_masked, state_add, state_new,
         o_done, squared, summed, rooted, kdt_p) = (st.sem(n) for n in (
             "landed", "v_step", "a_step", "a_ready", "k_ready", "kdT_ready", "a_scores", "a_masked",
             "state_add", "state_new", "o_done", "squared", "summed", "rooted", "kdt_p"))
        block = st.block()
        ident = core.mats["ident"]

        @block.sync
        def _(sp):
            sp.dma_start(reset[:, :, :], core.const("reset").rearrange("p (d s) -> p d s", d=2)).then_inc(landed, 16)
            sp.dma_start(causal[:, :, :, :], core.const("causal").rearrange("p (d t c) -> p d t c", d=2, t=TT)).then_inc(landed, 16)

        def one(x, h):
            return x[:, bass.ds(h, 1), :].rearrange("p a s -> p (a s)")

        def rows(d, i):
            return (0, GB * (i + 1)) if d == 0 else (GB * i, GC)

        @block.vector
        def _(dve):
            step = Steps(dve, v_step)
            dve.wait_ge(landed, 32)
            step(dve.memset(kk[:, :, :, :, :], 0.0))
            with dve.Fori(0, GH) as h:
                step.enter(h, 26)
                step.mark(dve.tensor_copy(ql[:, :], one(qT, h)))
                for d in range(2):
                    step.mark(dve.tensor_copy(kl[:, d, :], kT[:, d, bass.ds(h, 1), :].rearrange("p a s -> p (a s)")))
                step.mark(dve.tensor_copy(vl[:, :].rearrange("p (t e) -> p t e", t=TT), v[:, :, bass.ds(h * P, P)]))
                step.mark(dve.memset(state[:, :, :], 0.0))
                for d in range(2):
                    way = slice(None, None, 1) if d == 0 else slice(None, None, -1)
                    lg = lT[:, d, bass.ds(h, 1), :].rearrange("p a s -> p (a s)")
                    if d == 1:
                        step(dve.tensor_copy(qe[:, 1, :], lg))
                        lg = qe[:, 1, :]
                    step(dve.tensor_tensor_scan(b[:, d, way], reset[:, d, way], lg[:, way], 0.0, ALU.mult, ALU.add))
                bb = [b[:, d, :].rearrange("p (w g) -> p w g", g=GB) for d in range(2)]
                bc = [b[:, d, :].rearrange("p (n c) -> p n c", c=GC) for d in range(2)]
                mid = [GB // 2 - 1, GB // 2]
                last = [GC - 1, 0]
                for d in range(2):
                    m = bb[d][:, :, mid[d]:mid[d] + 1].to_broadcast([P, W, GB])
                    step.mark(dve.tensor_tensor(qd[:, d, :].rearrange("p (w g) -> p w g", g=GB), bb[d], m, ALU.subtract))
                    e = bc[d][:, :, last[d]:last[d] + 1].to_broadcast([P, NCH, GC])
                    step.mark(dve.tensor_tensor(kd[:, d, :].rearrange("p (n c) -> p n c", c=GC), e, bc[d], ALU.subtract))
                step.wait()
                dve.tensor_scalar(qd[:, :, :], qd[:, :, :], 80.0, None, ALU.min).then_inc(a_ready, 1)
                for d in range(2):
                    for i in range(NBL):
                        lo, hi = rows(d, i)
                        m = bc[d][:, :, GB * i + mid[d]:GB * i + mid[d] + 1].to_broadcast([P, NCH, hi - lo])
                        step.mark(dve.tensor_tensor(kk[:, d, :, i, lo:hi], m, bc[d][:, :, lo:hi], ALU.subtract))
                step.wait()
                for d in range(2):
                    for i in range(NBL):
                        own = kk[:, d, :, i, GB * i:GB * (i + 1)]
                        last_ = dve.tensor_scalar(own, own, 80.0, None, ALU.min)
                last_.then_inc(a_ready, 1)
                dve.wait_ge(a_step, h * 2 + 1)
                step.mark(dve.tensor_tensor(qd[:, :, :], qd[:, :, :], ql[:, :].unsqueeze(1).to_broadcast([P, 2, S]), ALU.mult))
                step.mark(dve.tensor_tensor(qe[:, :, :], qe[:, :, :], ql[:, :].unsqueeze(1).to_broadcast([P, 2, S]), ALU.mult))
                dve.tensor_tensor(kd[:, :, :], kd[:, :, :], kl[:, :, :], ALU.mult).then_inc(k_ready, 1)
                dve.wait_ge(a_step, h * 2 + 2)
                for d in range(2):
                    kc = kl[:, d, :].rearrange("p (n c) -> p n c", c=GC)
                    for i in range(NBL):
                        lo, hi = rows(d, i)
                        x = kk[:, d, :, i, lo:hi]
                        last_ = dve.tensor_tensor(x, x, kc[:, :, lo:hi], ALU.mult)
                last_.then_inc(k_ready, 1)
                dve.wait_ge(a_scores, h + 1)
                dve.tensor_tensor(at[:, :, :, :], pa[:, :, :, :], causal[:, :, :, :], ALU.mult).then_inc(a_masked, 1)
                for n in range(NCH):
                    for d in range(2):
                        c = n if d == 0 else NCH - 1 - n
                        dve.wait_ge(state_add, h * 16 + (2 * n + d + 1))
                        dve.scalar_tensor_tensor(state[:, d, :], state[:, d, :], ebl[:, d, c:c + 1],
                                                 pst[:, d, 0:P], ALU.mult, ALU.add).then_inc(state_new, 1)
                dve.wait_ge(summed, h + 1)
                step(dve.tensor_scalar(rstd[:, :], pn[:, :], 1.0 / GD, EPS, ALU.mult, ALU.add))
                dve.wait_ge(rooted, h + 1)
                step(dve.reciprocal(rstd[:, :], rstd[:, :]))
                step(dve.scalar_tensor_tensor(on[:, :], on[:, :], core.col("hg_out_norm"), rstd[:, :], ALU.mult, ALU.mult))
                step(dve.tensor_tensor(one(oT, h), on[:, :], one(gT, h), ALU.mult))
                step.leave(GH)

        @block.scalar
        def _(act):
            with act.Fori(0, GH) as h:
                act.wait_ge(a_ready, h * 2 + 1)
                act.activation(qd[:, :, :], qd[:, :, :], ACT.Exp)
                act.activation(kd[:, :, :], kd[:, :, :], ACT.Exp)
                act.activation(qe[:, :, :], b[:, :, :], ACT.Exp)
                act.activation(ebl[:, 0, :], b[:, 0, GC - 1::GC], ACT.Exp)
                act.activation(ebl[:, 1, :], b[:, 1, 0::GC], ACT.Exp).then_inc(a_step, 1)
                act.wait_ge(a_ready, h * 2 + 2)
                for d in range(2):
                    for i in range(NBL):
                        lo, hi = rows(d, i)
                        x = kk[:, d, :, i, lo:hi]
                        last_ = act.activation(x, x, ACT.Exp)
                last_.then_inc(a_step, 1)
                for d in range(2):
                    act.wait_ge(kdt_p, h * 2 + (d + 1))
                    act.activation(kdT[:, d, :, :], pk[:, d, :, :], ACT.Copy).then_inc(kdT_ready, 1)
                act.wait_ge(o_done, h + 1)
                o = po[:, :, 0:S // 2].rearrange("p a (t c) -> p a t c", c=GC)
                for dst, func in ((sq, ACT.Square), (on, ACT.Copy)):
                    act.activation(dst[:, :].rearrange("p (t a c) -> p a t c", a=2, c=GC), o, func).then_inc(squared, 1)
                act.wait_ge(v_step, h * 26 + 24)
                act.activation(rstd[:, :], rstd[:, :], ACT.Sqrt).then_inc(rooted, 1)

        @block.tensor
        def _(pe):
            with pe.Fori(0, GH) as h:
                pe.wait_ge(k_ready, h * 2 + 1)
                for d in range(2):
                    for t in range(TT):
                        last = pe.transpose(pk[:, d, t, :], kd[:, d, t * P:(t + 1) * P], ident[:, :])
                    last.then_inc(kdt_p, 1)
                pe.wait_ge(k_ready, h * 2 + 2)
                for d in range(2):
                    for c in range(NCH):
                        r = GC * (c % 2)
                        for i in range(NBL):
                            last = pe.matmul(pa[r:r + GC, d, c // 2, GB * i:GB * (i + 1)], kk[:, d, c, i, :],
                                             qd[:, d, c * GC + GB * i:c * GC + GB * (i + 1)], start=True, stop=True,
                                             skip_group_check=True)
                last.then_inc(a_scores, 1)
                pe.wait_ge(a_masked, h + 1)
                for n in range(NCH):
                    for d in range(2):
                        c = n if d == 0 else NCH - 1 - n
                        r = GC * (c % 2)
                        vc = vl[r:r + GC, (c // 2) * P:(c // 2 + 1) * P]
                        o = po[:, c % 2, GC * (c // 2):GC * (c // 2 + 1)]
                        pe.matmul(o, vc, at[r:r + GC, d, c // 2, :], start=(n == 0), stop=False, skip_group_check=True)
                        if n == 0 and d == 0:
                            pe.wait_ge(kdT_ready, h * 2 + 2)
                        if n >= 1:
                            pe.wait_ge(state_new, h * 16 + (2 * (n - 1) + d + 1))
                        last = pe.matmul(o, state[:, d, :], qe[:, d, c * GC:(c + 1) * GC], start=False, stop=False,
                                         skip_group_check=True)
                        pe.matmul(pst[:, d, 0:P], kdT[r:r + GC, d, c // 2, :], vc, start=True, stop=True).then_inc(state_add, 1)
                last.then_inc(o_done, 1)
                pe.wait_ge(squared, h * 2 + 2)
                pe.matmul(pn[:, :], core.mats["ones"][:, :], sq[:, :], start=True, stop=True).then_inc(summed, 1)


def merge(core, gates, y_att, y_hg, m):
    with Stage(core) as st:
        v_step = st.sem("v_step")
        block = st.block()

        @block.vector
        def _(dve):
            step = Steps(dve, v_step)
            step(dve.tensor_tensor(y_att[:, :, :], y_att[:, :, :], gates[:, 0:KT, :], ALU.mult))
            step(dve.tensor_tensor(y_hg[:, :, :], y_hg[:, :, :], gates[:, KT:2 * KT, :], ALU.mult))
            dve.tensor_tensor(m[:, :, :], y_att[:, :, :], y_hg[:, :, :], ALU.add)


def first_mixer(core):
    norm(core, core.col("norm_mix"))
    d = core.dram
    with Stage(core) as st:
        ya = st.sb("ya", [P, 4, S])
        yh = st.sb("yh", [P, GH, S])
        with Stage(core) as st2:
            qkT = st2.sb("qkT", [P, 6, S])
            v = st2.sb("v", [P, TT, AKV * AD])
            linear(core, d["w_qk"], KT, 384, 2, core.hT, tiles_to(qkT, 3))
            linear(core, d["w_v"], KT, 64, 2, core.hT, tokens_to(v, 64), token_major=True)
            attention(core, qkT, qkT[:, 4:5, :], v, ya)
        with Stage(core) as st2:
            pT = st2.sb("pT", [P, 4, GH, S])
            hv = st2.sb("hv", [P, TT, GH * GD])
            kT = st2.sb("kT", [P, 2, GH, S])
            flat = pT[:, :, :, :].rearrange("p a h s -> p (a h) s")
            linear(core, d["w_hg_silu"], KT, 512, 2, core.hT, tiles_to(flat[:, 0:8, :], 4, ACT.Silu),
                   beside=lambda core, st: Modulation(core, st, 0))
            linear(core, d["w_hg_f"], KT, 512, 2, core.hT, tiles_to(flat[:, 8:16, :], 4),
                   beside=lambda core, st: Modulation(core, st, 1))
            linear(core, d["w_hg_v"], KT, 256, 2, core.hT, tokens_to(hv, 256), token_major=True)
            fT = pT[:, 2:4, :, :]
            lT = kT
            hgrn_gates(core, pT, fT, kT, lT)
            hgrn(core, pT[:, 0, :, :], fT, lT, hv, pT[:, 1, :, :], yh)
        with Stage(core) as st2:
            y_att, y_hg = st2.sb("y_att", [P, KT, S]), st2.sb("y_hg", [P, KT, S])
            gates = st2.sb("gates", [P, 2 * KT, S])
            linear(core, d["w_up_att"], 4, 512, 2, ya, tiles_to(y_att, 4))
            linear(core, d["w_up_hg"], 4, 512, 2, yh, tiles_to(y_hg, 4))
            linear(core, d["w_gates"], KT, 512, 4, core.hT, tiles_to(gates, 4, ACT.Sigmoid))
            merge(core, gates, y_att, y_hg, core.hT)
            linear(core, d["w_out"], KT, 512, 2, core.hT, add_to_x(core, 4), engine="vector")


UNITS = TT * PH
PER = 22


def peer_scores(core, qT, h_tm, scores):
    with Stage(core) as st:
        keys = st.sb("keys", [P, 2 * PH, PN])
        pt = st.ps("pt", [P, 4, 512])
        pq = st.ps("pq", [P, 4, 512])
        landed, transposed, copied, scored, taken = (st.sem(n) for n in ("landed", "transposed", "copied", "scored", "taken"))
        block = st.block()

        @block.sync
        def _(sp):
            sp.dma_start(keys[:, :, :], core.dram["sub_keys"].rearrange("p (h n) -> p h n", n=PN)).then_inc(landed, 16)

        @block.tensor
        def _(pe):
            n = 0
            for t in range(TT):
                for half in range(2):
                    if n >= 4:
                        pe.wait_ge(copied, n - 3)
                    for k in range(4):
                        last = pe.transpose(pt[:, n % 4, k * P:(k + 1) * P],
                                            core.hT[:, half * 4 + k, t * P:(t + 1) * P], core.mats["ident"][:, :])
                    last.then_inc(transposed, 1)
                    n += 1
            pe.wait_ge(landed, 16)
            n = 0
            for t in range(TT):
                for quarter in range(4):
                    if n >= 4:
                        pe.wait_ge(taken, n - 3)
                    for k in range(4):
                        i = quarter * 4 + k
                        last = pe.matmul(pq[:, n % 4, k * PN:(k + 1) * PN], qT[:, i, t * P:(t + 1) * P],
                                         keys[:, i, :], start=True, stop=True)
                    last.then_inc(scored, 1)
                    n += 1

        @block.scalar
        def _(act):
            for n in range(2 * TT):
                act.wait_ge(transposed, n + 1)
                act.activation(h_tm[:, n // 2, (n % 2) * 512:(n % 2 + 1) * 512], pt[:, n % 4, :], ACT.Copy).then_inc(copied, 1)

        @block.vector
        def _(dve):
            for n in range(4 * TT):
                dve.wait_ge(scored, n + 1)
                dve.tensor_copy(scores[:, 2 * n:2 * n + 2, :, :],
                                pq[:, n % 4, :].rearrange("p (h q n) -> p h q n", q=2, n=PN)).then_inc(taken, 1)
            dve.memset(scores[:, UNITS:UNITS + 1, :, :], 0.0)


def peer_experts(core, h_tm, scores, y_tm):
    G = PK // 2
    with Stage(core) as st:
        iota = st.sb("iota", [P, PK])
        sc, rest = st.sb("sc", [P, 2, PN]), st.sb("rest", [P, 2, PN])
        v, ixf = st.sb("v", [P, 2, PK]), st.sb("ixf", [P, 2, PK])
        ix = st.sb("ix", [P, 2, PK], U32)
        cand, left, hit = (st.sb(n, [P, PK, PK]) for n in ("cand", "left", "hit"))
        best = st.sb("best", [P, PK])
        pos = st.sb("pos", [P, PK], U32)
        part = st.sb("part", [P, 2, PK], U32)
        partf, name = st.sb("partf", [P, 2, PK]), st.sb("name", [P, 2, PK])
        ex = st.sb("ex", [P, PK])
        tot = st.sb("tot", [P, 2])
        idx = st.sb("idx", [P, 2, PK], U32)
        weight = st.sb("weight", [P, 2, PK])
        ub = st.sb("ub", [P, G, D])
        vb = st.sb("vb", [P, 2, G, D])
        a, ge, wt = (st.sb(n, [P, 2, G]) for n in ("a", "ge", "wt"))
        diag = st.sb("diag", [P, 2, G, P])
        zeros = st.sb("zeros", [P, 512])
        po = st.ps("po", [P, D])
        u_landed = [st.sem(f"u_landed{s}") for s in range(G)]
        v_landed = [[st.sem(f"v_landed{g}{s}") for s in range(G)] for g in range(2)]
        (landed, v_step, picked, summing, expd, u_free, v_free, gelu_done, wt_ready, diag_ready, tile_out, zeroed,
         passed, pool_passed) = (st.sem(n) for n in (
             "landed", "v_step", "picked", "summing", "expd", "u_free", "v_free", "gelu_done", "wt_ready", "diag_ready",
             "tile_out", "zeroed", "passed", "pool_passed"))
        block = st.block()

        @block.sync
        def _(sp):
            sp.dma_start(iota[:, :], core.const("iota16")).then_inc(landed, 16)

        @block.gpsimd
        def _(pool):
            with pool.Fori(0, TT) as t:
                with pool.Fori(0, PH // 2) as hh:
                    for par in range(2):
                        unit = t * PH + hh * 2 + par
                        for g in range(2):
                            if g == 0:
                                wait_apart(pool, picked, unit + 1, pool_passed)
                            for table, buf, free, landed_ in (("peer_u", ub, u_free, u_landed),
                                                              ("peer_v", vb[:, g, :, :], v_free, v_landed[g])):
                                for s in range(G):
                                    wait_apart(pool, free, unit * PK + (G * g + s + 1), pool_passed)
                                    pool.indirect_dma_start(
                                        out=buf[:, s, :], out_offset=None, in_=core.dram[table][:, :],
                                        in_offset=bass.IndirectOffsetOnAxis(ap=idx[:, par, G * g + s:G * g + s + 1], axis=0),
                                    ).then_inc(landed_[s], 16)

        @block.vector
        def _(dve):
            step = Steps(dve, v_step)

            def settle(ins):
                step.mark(ins)
                wait_apart(dve, v_step, step.base + step.n, passed)

            def best16(rows, top, where):
                for values, _, i in rows:
                    last = dve.max(top(i)[:, 0:8], values)
                settle(last)
                for values, spare, i in rows:
                    dve.max_index(where(i)[:, 0:8], top(i)[:, 0:8], values)
                    last = dve.match_replace(spare, top(i)[:, 0:8], values, NEG)
                settle(last)
                for _, spare, i in rows:
                    last = dve.max(top(i)[:, 8:16], spare)
                settle(last)
                for _, spare, i in rows:
                    last = dve.max_index(where(i)[:, 8:16], top(i)[:, 8:16], spare)
                step(last)

            def pick_keys(unit):
                settle(dve.tensor_copy(sc[:, :, :], scores[:, bass.ds(unit, 1), :, :].rearrange("p a q n -> p (a q) n")))
                best16([(sc[:, q, :], rest[:, q, :], q) for q in range(2)], lambda q: v[:, q, :], lambda q: ix[:, q, :])
                step.mark(dve.tensor_copy(ixf[:, :, :], ix[:, :, :]))
                settle(dve.tensor_tensor(cand[:, :, :], v[:, 0, :].unsqueeze(2).to_broadcast([P, PK, PK]),
                                         v[:, 1, :].unsqueeze(1).to_broadcast([P, PK, PK]), ALU.add))

            def pick_experts(unit, par):
                flat = lambda x: x[:, :, :].rearrange("p a b -> p (a b)")
                best16([(flat(cand), flat(left), 0)], lambda q: best[:, :], lambda q: pos[:, :])
                dve.tensor_scalar(ex[:, :], best[:, :], best[:, 0:1], None, ALU.subtract).then_inc(summing, 1)
                step.mark(dve.tensor_scalar(part[:, 0, :], pos[:, :], 4, None, ALU.logical_shift_right))
                step(dve.tensor_scalar(part[:, 1, :], pos[:, :], 15, None, ALU.bitwise_and))
                step(dve.tensor_copy(partf[:, :, :], part[:, :, :]))
                for q in range(2):
                    step(dve.tensor_tensor(hit[:, :, :], partf[:, q, :].unsqueeze(2).to_broadcast([P, PK, PK]),
                                           iota[:, :].unsqueeze(1).to_broadcast([P, PK, PK]), ALU.is_equal))
                    step(dve.tensor_tensor(hit[:, :, :], hit[:, :, :], ixf[:, q, :].unsqueeze(1).to_broadcast([P, PK, PK]), ALU.mult))
                    step(dve.tensor_reduce(name[:, q, :], hit[:, :, :], AX.X, ALU.add))
                dve.wait_ge(expd, unit + 1)
                step(dve.reciprocal(tot[:, 1:2], tot[:, 0:1]))
                step(dve.tensor_scalar(weight[:, par, :], ex[:, :], tot[:, 1:2], None, ALU.mult))
                dve.scalar_tensor_tensor(idx[:, par, :], name[:, 0, :], float(PN), name[:, 1, :],
                                         ALU.mult, ALU.add).then_inc(picked, 1)

            dve.sem_inc(u_free, G)
            dve.memset(zeros[:, :], 0.0).then_inc(zeroed, 1)
            dve.wait_ge(landed, 16)
            pick_keys(0)
            pick_experts(0, 0)
            with dve.Fori(0, TT) as t:
                with dve.Fori(0, PH // 2) as hh:
                    step.enter(t * (PH // 2) + hh, 2 * PER)
                    for par in range(2):
                        unit = t * PH + hh * 2 + par
                        for g in range(2):
                            for s in range(G):
                                dve.wait_ge(u_landed[s], unit * 32 + (16 * g + 16))
                                dve.scalar_tensor_tensor(ub[:, s, :], ub[:, s, :], 1.0,
                                                         h_tm[:, bass.ds(t, 1), :].rearrange("p a d -> p (a d)"),
                                                         ALU.mult, ALU.mult, accum_out=a[:, g, s:s + 1]).then_inc(u_free, 1)
                            dve.wait_ge(gelu_done, unit * 2 + (g + 1))
                            dve.tensor_tensor(wt[:, g, :], ge[:, g, :], weight[:, par, G * g:G * g + G],
                                              ALU.mult).then_inc(wt_ready, 1)
                            if g == 0:
                                pick_keys(unit + 1)
                            else:
                                wait_apart(dve, v_free, unit * PK + PK, passed)
                                pick_experts(unit + 1, 1 - par)
                    step.leave(TT * PH // 2)

        @block.scalar
        def _(act):
            def exponentials(unit):
                act.wait_ge(summing, unit + 1)
                act.activation(ex[:, :], ex[:, :], ACT.Exp, accum_out=tot[:, 0:1]).then_inc(expd, 1)

            exponentials(0)
            with act.Fori(0, TT) as t:
                with act.Fori(0, PH // 2) as hh:
                    for par in range(2):
                        unit = t * PH + hh * 2 + par
                        for g in range(2):
                            act.wait_ge(u_free, unit * PK + (G * g + 16))
                            act.activation(ge[:, g, :], a[:, g, :], ACT.Gelu_apprx_tanh).then_inc(gelu_done, 1)
                            act.wait_ge(wt_ready, unit * 2 + (g + 1))
                            for s in range(G):
                                act.wait_ge(v_free, unit * PK + (G * g + s + 1))
                                act.activation(diag[:, g, s, :], core.mats["ident"][:, :], ACT.Copy,
                                               scale=wt[:, g, s:s + 1]).then_inc(diag_ready, 1)
                        exponentials(unit + 1)
                act.wait_ge(v_free, t * 128 + 144)
                act.activation(y_tm[:, bass.ds(t, 1), :].rearrange("p a d -> p (a d)"), po[:, :], ACT.Copy).then_inc(tile_out, 1)

        @block.tensor
        def _(pe):
            pe.sem_inc(v_free, PK)
            pe.wait_ge(zeroed, 1)
            pe.sem_inc(tile_out, 1)
            with pe.Fori(0, TT) as t:
                pe.wait_ge(tile_out, t + 1)
                for n in range(2):
                    pe.matmul(po[:, n * 512:(n + 1) * 512], zeros[:, 0:P], zeros[:, :], start=True, stop=False,
                              skip_group_check=True)
                with pe.Fori(0, PH) as h:
                    for g in range(2):
                        for s in range(G):
                            pe.wait_ge(diag_ready, t * 128 + h * PK + (G * g + s + 1))
                            pe.wait_ge(v_landed[g][s], t * 128 + h * PK + 16)
                            for n in range(2):
                                last = pe.matmul(po[:, n * 512:(n + 1) * 512], diag[:, g, s, :],
                                                 vb[:, g, s, n * 512:(n + 1) * 512], start=False, stop=False,
                                                 skip_group_check=True)
                            last.then_inc(v_free, 1)


def add_tokens(core, y_tm):
    with Stage(core) as st:
        pt = st.ps("pt", [P, KT, S])
        transposed = st.sem("transposed")
        block = st.block()

        @block.tensor
        def _(pe):
            for k in range(KT):
                for t in range(TT):
                    last = pe.transpose(pt[:, k, t * P:(t + 1) * P], y_tm[:, t, k * P:(k + 1) * P], core.mats["ident"][:, :])
                last.then_inc(transposed, 1)

        @block.vector
        def _(dve):
            for k in range(KT):
                dve.wait_ge(transposed, k + 1)
                dve.tensor_tensor(core.xT[:, k, :], pt[:, k, :], core.xT[:, k, :], ALU.add)


def peer(core):
    norm(core, core.col("norm_ffn"))
    with Stage(core) as st:
        h_tm = st.sb("h_tm", [P, TT, D])
        scores = st.sb("scores", [P, UNITS + 1, 2, PN])
        with Stage(core) as st2:
            qT = st2.sb("qT", [P, 2 * PH, S])
            linear(core, core.dram["w_peer"], KT, 512, 4, core.hT, tiles_to(qT, 4), 
                   beside=lambda core, st: Modulation(core, st, 2))
            peer_scores(core, qT, h_tm, scores)
        y_tm = core.hT[:, :, :].rearrange("p k s -> p (k s)").rearrange("p (t d) -> p t d", t=TT)
        peer_experts(core, h_tm, scores, y_tm)
        add_tokens(core, y_tm)


def ple(core):
    norm(core, core.col("norm_ple"))
    with Stage(core) as st:
        pT = st.sb("pT", [P, 2, S])
        gate = st.sb("gate", [P, KT, S])
        proj = st.sb("proj", [P, KT, S])
        with Stage(core) as st2:
            landed = st2.sem("landed")
            block = st2.block()

            @block.sync
            def _(sp):
                sp.dma_start(pT[:, :, :], core.dram["pT"].rearrange("p (k s) -> p k s", k=2)).then_inc(landed, 16)
                sp.wait_ge(landed, 16)
        linear(core, core.dram["w_ple_gate"], KT, 512, 2, core.hT, tiles_to(gate, 4, ACT.Sigmoid))
        linear(core, core.dram["w_ple_proj"], 2, 512, 2, pT, tiles_to(proj, 4))
        with Stage(core) as st2:
            v_step = st2.sem("v_step")
            block = st2.block()

            @block.vector
            def _(dve):
                step = Steps(dve, v_step)
                step(dve.tensor_tensor(gate[:, :, :], gate[:, :, :], proj[:, :, :], ALU.mult))
                dve.tensor_tensor(core.xT[:, :, :], core.xT[:, :, :], gate[:, :, :], ALU.add)


def modulated_norm(core, which):
    norm(core, core.gain[:, which * KT:(which + 1) * KT], bias=core.mod[:, 3 * KT * which:3 * KT * which + KT])


def gate_col(which):
    return 3 * KT * which + 2 * KT


def feed_forward(core, layer, beside=None):
    modulated_norm(core, 2 * layer + 1)
    with Stage(core) as st:
        a = st.sb("a", [P, FF // P, S])

        def square(dve, c):
            x = a[:, bass.ds(c * 4, 4), :]
            return dve.tensor_tensor(x, x, x, ALU.mult)

        linear(core, core.dram[f"w_fc1_{layer}"], KT, 512, 8, core.hT, tiles_to(a, 4, ACT.Relu), after=square)
        deep_linear(core, core.dram[f"w_fc2_{layer}"], a, core.mod, gate_col(2 * layer + 1), beside)


def deep_linear(core, w, src, gate, gate_at, beside=None):
    slices = FF // D
    with Stage(core) as st:
        ring = st.sb("ring", [P, 2, KT * 512])
        acc = st.ps("acc", [P, 4, S])
        landed = [st.sem("landed0"), st.sem("landed1")]
        part_landed = [st.sem(f"part_landed{i}") for i in range(KT // 2)]
        multiplied, added = st.sem("multiplied"), st.sem("added")
        load, scalar, vector = beside(core, st) if beside else (None, None, None)
        block = st.block()
        if beside:
            block.gpsimd(load)
            block.scalar(scalar)

        @block.sync
        def _(sp):
            for i, sem in enumerate(part_landed):
                part = slice(i * 1024, (i + 1) * 1024)
                sp.dma_start(ring[:, 0, part], w[0:P, part]).then_inc(sem, 16)
            sp.dma_start(ring[:, 1, :], w[P:2 * P, :]).then_inc(landed[1], 16)
            with sp.Fori(1, slices) as i:
                for s in range(2):
                    sp.wait_ge(multiplied, i * 2 - 1 + s)
                    sp.dma_start(ring[:, s, :], w[bass.ds((i * 2 + s) * P, P), :]).then_inc(landed[s], 16)

        @block.tensor
        def _(pe):
            def product(n, j, k):
                return pe.matmul(acc[:, j, :], ring[:, n % 2, k * 512 + j * P:k * 512 + (j + 1) * P],
                                 src[:, n * KT + k, :], start=(n == 0 and k == 0), stop=(n == slices - 1 and k == KT - 1))

            def multiply(n):
                for j in range(4):
                    for k in range(KT):
                        last = product(n, j, k)
                last.then_inc(multiplied, 1)

            for i, sem in enumerate(part_landed):
                pe.wait_ge(sem, 16)
                for j in range(4):
                    for k in (2 * i, 2 * i + 1):
                        last = product(0, j, k)
            last.then_inc(multiplied, 1)
            for half in range(2):
                if half:
                    pe.wait_ge(landed[0], 32)
                    pe.wait_ge(added, 1)
                    multiply(0)
                for n in range(1, slices):
                    pe.wait_ge(landed[n % 2], half * 32 + (n // 2 + n % 2) * 16)
                    multiply(n)

        @block.vector
        def _(dve):
            if beside:
                vector(dve)
            take = add_to_x(core, 4, gate, gate_at)
            with dve.Fori(0, 2) as half:
                dve.wait_ge(multiplied, half * 4 + 4)
                for j in range(4):
                    last = take(dve, half, j, acc[:, j, :])
                last.then_inc(added, 1)


def conv_and_retention(core, apad, gate, qk, v, conv, o):
    pad = CW // 2
    with Stage(core) as st:
        cs = st.sb("cs", [P, 2, S])
        rot = st.sb("rot", [P, P])
        turned_ = st.sb("turned_", [P, 8, S])
        decay = st.sb("decay", [P, RH, TT, S])
        w = st.sb("w", [P, 4, S])
        pr = st.ps("pr", [P, 2, S])
        sc = st.ps("sc", [P, 2, S])
        po = st.ps("po", [P, 2, S])
        landed, v_step, turned, copied, p_step, scored, taken, weighted, mixed, out_done = (st.sem(n) for n in (
            "landed", "v_step", "turned", "copied", "p_step", "scored", "taken", "weighted", "mixed", "out_done"))
        block = st.block()

        @block.sync
        def _(sp):
            for dst, name in ((rot[:, :], "rot_ret"), (cs[:, 0, :], "cos_ret"), (cs[:, 1, :], "sin_ret")):
                sp.dma_start(dst, core.const(name)).then_inc(landed, 16)
            sp.dma_start(decay[:, :, :, :], core.const("decay").rearrange("p (h t s) -> p h t s", h=RH, t=TT)).then_inc(landed, 16)

        @block.vector
        def _(dve):
            step = Steps(dve, v_step)
            a = apad[:, :, pad:pad + S]
            step.mark(dve.memset(apad[:, :, 0:pad], 0.0))
            step.mark(dve.memset(apad[:, :, pad + S:], 0.0))
            step(dve.tensor_tensor(a, a, gate[:, :, :], ALU.mult))
            taps = core.col("conv_w").rearrange("p (j w) -> p j w", w=CW)
            for j in range(4):
                step.mark(dve.tensor_scalar(conv[:, j, :], apad[:, j, 0:S], taps[:, j, 0:1],
                                            core.col("conv_b", j, 1), ALU.mult, ALU.add))
            with dve.Fori(1, CW) as tap:
                step.enter(tap - 1, 4)
                for j in range(4):
                    step.wait(lag=3)
                    step.mark(dve.scalar_tensor_tensor(
                        conv[:, j, :], apad[:, j, bass.ds(tap, S)], taps[:, j, bass.ds(tap, 1)], conv[:, j, :],
                        ALU.mult, ALU.add))
                step.leave(CW - 1)

        @block.tensor
        def _(pe):
            pe.wait_ge(landed, 64)
            for i in range(8):
                if i >= 2:
                    pe.wait_ge(copied, i - 1)
                pe.matmul(pr[:, i % 2, :], rot[:, :], qk[:, i, :], start=True, stop=True).then_inc(turned, 1)
            pe.wait_ge(p_step, 3)
            for u in range(RH * TT + 2):
                if u < RH * TT:
                    h, m = divmod(u, TT)
                    if u >= 2:
                        pe.wait_ge(taken, u - 1)
                    pe.matmul(sc[:, u % 2, :], qk[:, 4 + h, m * P:(m + 1) * P], qk[:, h, :],
                              start=True, stop=True).then_inc(scored, 1)
                if u >= 2:
                    h, m = divmod(u - 2, TT)
                    pe.wait_ge(weighted, u - 1)
                    if m == 0 and h >= 2:
                        pe.wait_ge(out_done, h - 1)
                    pe.matmul(po[:, h % 2, :], v[:, m, h * P:(h + 1) * P], w[:, m, :], start=(m == 0),
                              stop=(m == TT - 1)).then_inc(mixed, 1)

        @block.scalar
        def _(act):
            for i in range(8):
                act.wait_ge(turned, i + 1)
                act.activation(turned_[:, i, :], pr[:, i % 2, :], ACT.Copy).then_inc(copied, 1)
            for u in range(RH * TT + 4):
                if u < RH * TT:
                    act.wait_ge(scored, u + 1)
                    if u >= 4:
                        act.wait_ge(mixed, u - 3)
                    act.activation(w[:, u % 4, :], sc[:, u % 2, :], ACT.Copy, scale=P ** -0.5).then_inc(taken, 1)
                if u >= 7 and u % TT == 3:
                    h = u // TT - 1
                    act.wait_ge(mixed, TT * (h + 1))
                    act.activation(o[:, h, :], po[:, h % 2, :], ACT.Copy).then_inc(out_done, 1)

        @block.gpsimd
        def _(pool):
            step = Steps(pool, p_step)
            pool.wait_ge(landed, 64)
            pool.wait_ge(copied, 8)
            step.mark(pool.tensor_tensor(qk[:, :, :], qk[:, :, :], cs[:, 0, :].unsqueeze(1).to_broadcast([P, 8, S]), ALU.mult))
            step(pool.tensor_tensor(turned_[:, :, :], turned_[:, :, :], cs[:, 1, :].unsqueeze(1).to_broadcast([P, 8, S]), ALU.mult))
            step(pool.tensor_tensor(qk[:, :, :], qk[:, :, :], turned_[:, :, :], ALU.add))
            for u in range(RH * TT):
                h, m = divmod(u, TT)
                pool.wait_ge(taken, u + 1)
                pool.tensor_tensor(w[:, m, :], w[:, m, :], decay[:, h, m, :], ALU.mult).then_inc(weighted, 1)


def conv_and_retention_norms(core, conv, o, gate, cat):
    with Stage(core) as st:
        sq = st.sb("sq", [P, 8, S])
        mu = st.sb("mu", [P, S])
        rstd = st.sb("rstd", [P, S])
        rh = st.sb("rh", [P, RH, S])
        pm = st.ps("pm", [P, 2, S])
        ph = st.ps("ph", [P, RH, S])
        v_step, squared, summed, rooted = (st.sem(n) for n in ("v_step", "squared", "summed", "rooted"))
        block = st.block()
        ones = core.mats["ones"]

        @block.tensor
        def _(pe):
            for j in range(4):
                last = pe.matmul(pm[:, 0, :], ones[:, :], conv[:, j, :], start=(j == 0), stop=(j == 3))
            last.then_inc(summed, 1)
            pe.wait_ge(squared, 1)
            for h in range(RH):
                last = pe.matmul(ph[:, h, :], ones[:, :], sq[:, 4 + h, :], start=True, stop=True)
            last.then_inc(summed, 1)
            pe.wait_ge(squared, 2)
            for j in range(4):
                last = pe.matmul(pm[:, 1, :], ones[:, :], sq[:, j, :], start=(j == 0), stop=(j == 3))
            last.then_inc(summed, 1)

        @block.scalar
        def _(act):
            act.activation(sq[:, 4:8, :], o[:, :, :], ACT.Square).then_inc(squared, 1)
            act.wait_ge(v_step, 2)
            act.activation(sq[:, 0:4, :], conv[:, :, :], ACT.Square).then_inc(squared, 1)
            act.wait_ge(v_step, 3)
            act.activation(rh[:, :, :], rh[:, :, :], ACT.Sqrt).then_inc(rooted, 1)
            act.wait_ge(v_step, 4)
            act.activation(rstd[:, :], rstd[:, :], ACT.Sqrt).then_inc(rooted, 1)
            act.wait_ge(v_step, 5 + 1 + 2 + 4)
            for j in range(4):
                act.activation(cat[:, j, :], conv[:, j, :], ACT.Silu, bias=core.col("cln_b", j, 1))

        @block.vector
        def _(dve):
            step = Steps(dve, v_step)
            dve.wait_ge(summed, 1)
            step(dve.tensor_scalar(mu[:, :], pm[:, 0, :], 1.0 / MA, None, ALU.mult))
            step(dve.tensor_tensor(conv[:, :, :], conv[:, :, :], mu[:, :].unsqueeze(1).to_broadcast([P, 4, S]), ALU.subtract))
            dve.wait_ge(summed, 2)
            step(dve.tensor_scalar(rh[:, :, :], ph[:, :, :], 1.0 / P, EPS, ALU.mult, ALU.add))
            dve.wait_ge(summed, 3)
            step(dve.tensor_scalar(rstd[:, :], pm[:, 1, :], 1.0 / MA, EPS, ALU.mult, ALU.add))
            dve.wait_ge(rooted, 1)
            step(dve.reciprocal(rh[:, :, :], rh[:, :, :]))
            step(dve.tensor_tensor(o[:, :, :], o[:, :, :], rh[:, :, :], ALU.mult))
            step(dve.tensor_tensor(cat[:, 4:8, :], o[:, :, :], gate[:, :, :], ALU.mult))
            dve.wait_ge(rooted, 2)
            step(dve.reciprocal(rstd[:, :], rstd[:, :]))
            for j in range(4):
                step.mark(dve.scalar_tensor_tensor(conv[:, j, :], conv[:, j, :], core.col("cln_g", j, 1), rstd[:, :],
                                                   ALU.mult, ALU.mult))


def second_mixer0(core):
    modulated_norm(core, 0)
    d = core.dram
    with Stage(core) as st:
        apad = st.sb("apad", [P, 4, S + CW - 1])
        agate = st.sb("agate", [P, 4, S])
        qk = st.sb("qk", [P, 8, S])
        v = st.sb("v", [P, TT, RH * P])
        g = st.sb("g", [P, 4, S])
        conv = st.sb("conv", [P, 4, S])
        o = st.sb("o", [P, RH, S])
        linear(core, d["w2_val"], KT, 256, 2, core.hT, tiles_to(apad[:, :, CW // 2:CW // 2 + S], 2))
        linear(core, d["w2_gate"], KT, 256, 2, core.hT, tiles_to(agate, 2, ACT.Sigmoid))
        linear(core, d["w2_qk"], KT, 512, 2, core.hT, tiles_to(qk, 4))
        linear(core, d["w2_v"], KT, 256, 2, core.hT, tokens_to(v, 256), token_major=True)
        linear(core, d["w2_g"], KT, 256, 2, core.hT, tiles_to(g, 2, ACT.Silu))
        conv_and_retention(core, apad, agate, qk, v, conv, o)
        conv_and_retention_norms(core, conv, o, g, core.hT)
    linear(core, d["w2_out"], KT, 512, 2, core.hT, add_to_x(core, 4, core.mod, gate_col(0)), engine="vector")


def feed_forward1(core):
    feed_forward(core, 1)


TWO_PI = 2.0 * np.pi
PI_SAFE = 3.1415925
TURN_HI = 6.28125
TURN_MID = float(np.float32(TWO_PI - TURN_HI))
TURN_LO = TWO_PI - TURN_HI - TURN_MID


def reduced(dve, step, x, turns, exact=True):
    step(dve.tensor_scalar(turns, x, 1.0 / TWO_PI, ROUND, ALU.mult, ALU.add))
    step(dve.tensor_scalar(turns, turns, ROUND, None, ALU.subtract))
    for part in (TURN_HI, TURN_MID, TURN_LO) if exact else (TURN_HI, TURN_MID):
        step(dve.scalar_tensor_tensor(x, turns, -part, x, ALU.mult, ALU.add))


def angles(dve, step, sin_of, cos_of):
    step(dve.tensor_scalar(sin_of, sin_of, PI_SAFE, -PI_SAFE, ALU.min, ALU.max))
    step(dve.tensor_scalar(cos_of, sin_of, -1.0, None, ALU.mult))
    step(dve.tensor_tensor(cos_of, cos_of, sin_of, ALU.max))
    step(dve.tensor_scalar(cos_of, cos_of, -1.0, np.pi / 2, ALU.mult, ALU.add))


def s5_powers(core, st, p):
    N = 2 * SG
    pb, pc, r8, th8 = p.b, p.c, p.r8, p.th8
    sign = st.sb("sign", [P, 2])
    lr, dt, ld, th, tmp = (st.sb(n, [P, N]) for n in ("lr", "dt", "ld", "th", "tmp"))
    u, w, q = (st.sb(n, [P, N]) for n in ("u", "w", "q"))
    fr, fi = st.sb("fr", [P, N]), st.sb("fi", [P, N])
    cs = st.sb("cs", [P, 2, N])
    k = st.sb("k", [P, 2, N, ST])
    mag, s, c = (st.sb(n, [P, N, ST]) for n in ("mag", "s", "c"))
    spare = st.sb("spare", [P, N, ST])
    landed, v_step, ready, done = (st.sem(n) for n in ("k_landed", "powers_step", "powers_ready", "powers_done"))
    li = core.col("s5_li")

    def load(pool):
        pool.dma_start(sign[:, :], core.const("sign")).then_inc(landed, 16)
        for i, name in enumerate(("power_b", "power_c")):
            pool.dma_start(k[:, i, :, :], core.const(name).rearrange("p (n t) -> p n t", t=ST)).then_inc(landed, 16)

    def scalar(act):
        act.activation(dt[:, :], core.col("s5_step"), ACT.Exp).then_inc(done, 1)
        act.wait_ge(ready, 1)
        act.activation(q[:, :], ld[:, :], ACT.Exp).then_inc(done, 1)
        act.wait_ge(ready, 2)
        act.activation(cs[:, :, :], cs[:, :, :], ACT.Sin).then_inc(done, 1)
        for i in range(2):
            act.wait_ge(ready, 3 + i)
            act.activation(mag[:, :, :], mag[:, :, :], ACT.Exp)
            act.activation(s[:, :, :], s[:, :, :], ACT.Sin)
            act.activation(c[:, :, :], c[:, :, :], ACT.Sin).then_inc(done, 1)
        act.activation(r8[:, :], ld[:, :], ACT.Exp, scale=float(ST))

    def vector(dve):
        step = Steps(dve, v_step)
        TTm = lambda out, a, b, op=ALU.mult: step(dve.tensor_tensor(out, a, b, op))
        step(dve.tensor_scalar(lr[:, :], core.col("s5_lr"), -1e-4, None, ALU.min))
        dve.wait_ge(done, 1)
        dve.tensor_tensor(ld[:, :], lr[:, :], dt[:, :], ALU.mult).then_inc(ready, 1)
        TTm(th[:, :], li, dt[:, :])
        reduced(dve, step, th[:, :], tmp[:, :])
        step(dve.tensor_copy(cs[:, 1, :], th[:, :]))
        angles(dve, step, cs[:, 1, :], cs[:, 0, :])
        dve.tensor_copy(tmp[:, :], th[:, :]).then_inc(ready, 1)
        dve.wait_ge(done, 3)
        TTm(u[:, :], q[:, :], cs[:, 0, :])
        TTm(w[:, :], q[:, :], cs[:, 1, :])
        step(dve.tensor_scalar(u[:, :], u[:, :], -1.0, None, ALU.add))
        TTm(q[:, :], lr[:, :], lr[:, :])
        TTm(tmp[:, :], li, li)
        TTm(q[:, :], q[:, :], tmp[:, :], ALU.add)
        step(dve.reciprocal(q[:, :], q[:, :]))
        TTm(fr[:, :], u[:, :], lr[:, :])
        TTm(tmp[:, :], w[:, :], li)
        TTm(fr[:, :], fr[:, :], tmp[:, :], ALU.add)
        TTm(fr[:, :], fr[:, :], q[:, :])
        TTm(fi[:, :], w[:, :], lr[:, :])
        TTm(tmp[:, :], u[:, :], li)
        TTm(fi[:, :], fi[:, :], tmp[:, :], ALU.subtract)
        TTm(fi[:, :], fi[:, :], q[:, :])
        step(dve.tensor_scalar(th8[:, :], th[:, :], float(ST), None, ALU.mult))
        reduced(dve, step, th8[:, :], tmp[:, :])
        dve.wait_ge(landed, 48)
        for i in range(2):
            many = lambda x: x[:, :].unsqueeze(2).to_broadcast([P, N, ST])
            TTm(mag[:, :, :], k[:, i, :, :], many(ld))
            TTm(s[:, :, :], k[:, i, :, :], many(th))
            reduced(dve, step, s[:, :, :], spare[:, :, :])
            angles(dve, step, s[:, :, :], c[:, :, :])
            dve.tensor_copy(spare[:, :, :], c[:, :, :]).then_inc(ready, 1)
            dve.wait_ge(done, 4 + i)
            TTm(c[:, :, :], c[:, :, :], mag[:, :, :])
            TTm(s[:, :, :], s[:, :, :], mag[:, :, :])
            if i == 0:
                TTm(pb[:, 0, :, :], c[:, :, :], many(fr))
                TTm(spare[:, :, :], s[:, :, :], many(fi))
                TTm(pb[:, 0, :, :], pb[:, 0, :, :], spare[:, :, :], ALU.subtract)
                TTm(pb[:, 1, :, :], c[:, :, :], many(fi))
                TTm(spare[:, :, :], s[:, :, :], many(fr))
                TTm(pb[:, 1, :, :], pb[:, 1, :, :], spare[:, :, :], ALU.add)
                step(dve.tensor_scalar(pb[:, 1, :, :], pb[:, 1, :, :], sign[:, 0:1], None, ALU.mult))
            else:
                step(dve.tensor_scalar(pc[:, 0, :, :], c[:, :, :], sign[:, 1:2], None, ALU.mult))
                step(dve.tensor_copy(pc[:, 1, :, :], s[:, :, :]))

    return load, scalar, vector


class Powers:

    def __init__(self, st):
        self.b, self.c = (st.sb(n, [P, 2, 2 * SG, ST]) for n in ("power_b", "power_c"))
        self.r8, self.th8 = (st.sb(n, [P, 2 * SG]) for n in ("r8", "th8"))


def s5_to_chunks(core, h2, u):
    with Stage(core) as st:
        p1 = st.ps("p1", [P, 4, 512])
        p2 = st.ps("p2", [P, 4, 512])
        turned, copied, turned2, copied2 = (st.sem(n) for n in ("turned", "copied", "turned2", "copied2"))
        block = st.block()
        ident = core.mats["ident"]

        @block.tensor
        def _(pe):
            for n in range(2 * ST):
                t, half = divmod(n, 2)
                if n >= 4:
                    pe.wait_ge(copied, n - 3)
                for k in range(4):
                    last = pe.transpose(p1[0:SN, n % 4, k * P:(k + 1) * P], core.hT[:, half * 4 + k, t::ST], ident[:, :])
                last.then_inc(turned, 1)
            pe.wait_ge(copied, 2 * ST)
            for n in range(SG // 8):
                if n >= 4:
                    pe.wait_ge(copied2, n - 3)
                for g in range(8):
                    last = pe.transpose(p2[:, n % 4, g * SN:(g + 1) * SN], h2[0:SN, n * 8 + g, :], ident[0:SN, 0:SN])
                last.then_inc(turned2, 1)

        @block.scalar
        def _(act):
            for n in range(2 * ST):
                t, half = divmod(n, 2)
                act.wait_ge(turned, n + 1)
                act.activation(h2[0:SN, half * 32:(half + 1) * 32, t * SC:(t + 1) * SC],
                               p1[0:SN, n % 4, :].rearrange("p (g c) -> p g c", c=SC), ACT.Copy).then_inc(copied, 1)
            for n in range(SG // 8):
                act.wait_ge(turned2, n + 1)
                act.activation(u[:, n * 8:(n + 1) * 8, :], p2[:, n % 4, :].rearrange("p (g c) -> p g c", c=SN),
                               ACT.Copy).then_inc(copied2, 1)


def s5_scan(core, h2, u, pb, pc, r8, th8):
    GDN = 2 * SB
    ROUNDS = SG // SB
    TAPS = 2 * ST - 1
    N = SB * SN
    with Stage(core) as st:
        no = st.sb("no", [P, GDN, SN])
        keep = st.sb("keep", [P, GDN, SN])
        swap = st.sb("swap", [P, P])
        sign = st.sb("sign", [P, 2])
        quarter = st.sb("quarter", [P, 1])
        drow = st.sb("drow", [SN, D])
        bc = st.sb("bc", [P, 2, 4, GDN, SC])
        w2 = st.sb("w2", [P, 2, GDN, ST, SC])
        dm = st.sb("dm", [P, 2, SB, P])
        ub = st.sb("ub", [P, 2, SB, SN])
        th, turns, cosT, sinT, decay = (st.sb(n, [P, GDN, SN]) for n in ("th", "turns", "cosT", "sinT", "decay"))
        tp = st.sb("tp", [P, GDN, TAPS, SC])
        x1 = st.sb("x1", [P, 2, SB * (SB + 1) * SC])
        taps = st.sb("taps", [SB * SC, TAPS * SC])
        s1, s2 = st.sb("s1", [P, GDN, ST, SC]), st.sb("s2", [P, GDN, ST, SC])
        c1, c2 = st.sb("c1", [P, GDN, ST, SC]), st.sb("c2", [P, GDN, ST, SC])
        w1 = st.sb("w1", [P, GDN, P])
        e, gg, t1, t2 = (st.sb(n, [P, GDN, SN]) for n in ("e", "gg", "t1", "t2"))
        hs = st.sb("hs", [P, GDN, SN + 1])
        pA = st.ps("pA", [P, 2, 512])
        pK = st.ps("pK", [SB * SC, 512])
        pD = st.ps("pD", [P, 512])
        pE = st.ps("pE", [P, 512])
        pS = st.ps("pS", [P, 2, 512])
        pY = st.ps("pY", [P, 512])
        (fixed, v_step, a_step, p_step, powers, tabled, sined, decayed, w2_ready, x1_made, tapped, taps_copied, passed, ub_copied, w1_turned, w1_copied,
         d_made, d_copied, ended, e_copied, swapped, scanned, swapped2, h_ready, y_done, z_done) = (st.sem(n) for n in (
             "fixed", "v_step", "a_step", "p_step", "powers", "tabled", "sined", "decayed", "w2_ready", "x1_made", "tapped", "taps_copied", "passed",
             "ub_copied", "w1_turned", "w1_copied", "d_made", "d_copied", "ended", "e_copied", "swapped", "scanned",
             "swapped2", "h_ready", "y_done", "z_done"))
        landed = [st.sem(f"landed{par}") for par in range(2)]
        block = st.block()
        dram = core.dram
        flat = lambda x: x[:, :, :].rearrange("p g c -> p (g c)")
        big = lambda x: x.unsqueeze(2).to_broadcast([P, GDN, ST, SC])

        def of_round(x, q, n):
            return x[:, q, bass.ds(n * GDN, GDN), :].unsqueeze(3).to_broadcast([P, GDN, ST, SC])

        def prepare_all(eng, prepare):
            prepare(0, 0, True)
            with eng.Fori(0, ROUNDS // 2 - 1) as i:
                for k in range(2):
                    prepare(i * 2 + (k + 1), 1 - k)
            prepare(ROUNDS - 1, 1)

        @block.sync
        def _(sp):
            for dst, src in ((no[:, :, :], core.const("chunk_no").rearrange("p (g c) -> p g c", c=SN)),
                             (keep[:, :, :], core.const("chunk_keep").rearrange("p (g c) -> p g c", c=SN)),
                             (swap[:, :], core.const("swap_s5")), (sign[:, :], core.const("sign")),
                             (drow[:, :], dram["s5_d"][:, :].partition_broadcast(SN))):
                sp.dma_start(dst, src).then_inc(fixed, 16)

            def load(par, rows):
                sp.dma_start(bc[:, par, :, :, :].rearrange("p a g c -> p (a g c)"), rows).then_inc(landed[par], 16)

            for par in range(2):
                load(par, dram["s5_bc"][par * P:(par + 1) * P, :])
            with sp.Fori(1, ROUNDS // 2) as i:
                for par in range(2):
                    sp.wait_ge(powers, i * 4 + (2 * par - 2))
                    sp.wait_ge(x1_made, i * 2 + (par - 1))
                    sp.wait_ge(w2_ready, i * 2 + (par - 1))
                    load(par, dram["s5_bc"][bass.ds((i * 2 + par) * P, P), :])

        @block.gpsimd
        def _(pool):
            def prepare(n, par, first=False):
                if not first:
                    pool.wait_ge(scanned, n * 2)
                pool.tensor_tensor(decay[:, :, :], keep[:, :, :],
                                   r8[:, bass.ds(n * GDN, GDN)].unsqueeze(2).to_broadcast([P, GDN, SN]),
                                   ALU.mult).then_inc(decayed, 1)
                pool.wait_ge(landed[par], (n - par) * 8 + 16)
                if not first:
                    pool.wait_ge(w2_ready, n)
                pool.tensor_tensor(c1[:, :, :, :], of_round(pc, 0, n), big(bc[:, par, 2, :, :]), ALU.mult).then_inc(p_step, 1)
                pool.tensor_tensor(c2[:, :, :, :], of_round(pc, 1, n), big(bc[:, par, 3, :, :]), ALU.mult).then_inc(p_step, 1)
                pool.wait_ge(p_step, n * 2 + 2)
                pool.tensor_tensor(w2[:, par, :, :, :], c1[:, :, :, :], c2[:, :, :, :], ALU.subtract).then_inc(w2_ready, 1)

            pool.wait_ge(fixed, 80)
            prepare_all(pool, prepare)

        @block.vector
        def _(dve):
            step = Steps(dve, v_step)
            mult = lambda out, a, b: dve.tensor_tensor(out, a, b, ALU.mult)

            def powers_by_b(n, par, first=False):
                if not first:
                    dve.wait_ge(tapped, n)
                dve.wait_ge(landed[par], (n - par) * 8 + 16)
                step.mark(mult(s1[:, :, :, :], of_round(pb, 0, n), big(bc[:, par, 0, :, :])))
                step(mult(s2[:, :, :, :], of_round(pb, 1, n), big(bc[:, par, 1, :, :])))
                dve.tensor_tensor(tp[:, 0:SB, 0:ST, :], s1[:, 0:SB, :, :], s2[:, 0:SB, :, :], ALU.add).then_inc(powers, 1)
                dve.tensor_tensor(tp[:, SB:GDN, ST - 1:TAPS, :], s1[:, SB:GDN, :, :], s2[:, SB:GDN, :, :],
                                  ALU.add).then_inc(powers, 1)

            def table(n):
                step(dve.tensor_tensor(th[:, :, :], no[:, :, :],
                                       th8[:, bass.ds(n * GDN, GDN)].unsqueeze(2).to_broadcast([P, GDN, SN]), ALU.mult))
                reduced(dve, step, th[:, :, :], turns[:, :, :], exact=False)
                dve.tensor_scalar(th[:, :, :], th[:, :, :], PI_SAFE, -PI_SAFE, ALU.min, ALU.max).then_inc(tabled, 1)

            def into_frame(n):
                dve.wait_ge(sined, n + 1)
                dve.wait_ge(e_copied, n + 1)
                step.mark(mult(flat(t1), flat(cosT), flat(e)))
                dve.wait_ge(swapped, n + 1)
                step(mult(flat(t2), flat(sinT), pS[:, 0, :]))
                step(dve.tensor_tensor(flat(t1), flat(t1), flat(t2), ALU.add))
                dve.wait_ge(decayed, n + 1)
                for d in range(2):
                    way = slice(0, N) if d == 0 else slice(2 * N - 1, N - 1, -1)
                    dve.tensor_tensor_scan(flat(gg)[:, way], flat(decay)[:, way], flat(t1)[:, way], 0.0,
                                           ALU.mult, ALU.add).then_inc(scanned, 1)

            def out_of_frame(n):
                dve.wait_ge(scanned, n * 2 + 2)
                step.mark(mult(flat(t1), flat(cosT), flat(gg)))
                dve.wait_ge(swapped2, n + 1)
                step(mult(flat(t2), flat(sinT), pS[:, 1, :]))
                dve.tensor_tensor(hs[:, 0:SB, 1:SN + 1], t1[:, 0:SB, :], t2[:, 0:SB, :], ALU.subtract).then_inc(h_ready, 1)
                dve.tensor_tensor(hs[:, SB:GDN, 0:SN], t1[:, SB:GDN, :], t2[:, SB:GDN, :], ALU.subtract).then_inc(h_ready, 1)

            def run(n, par, nxt):
                if nxt:
                    powers_by_b(*nxt)
                into_frame(n)
                out_of_frame(n)
                if nxt:
                    table(nxt[0])
                dve.wait_ge(y_done, n + 1)
                here = bass.ds(n * SB, SB)
                dve.tensor_tensor(h2[0:SN, here, :], pY[0:SN, :].rearrange("p (g x) -> p g x", x=P),
                                  h2[0:SN, here, :], ALU.add).then_inc(z_done, 1)

            dve.wait_ge(fixed, 80)
            step.mark(dve.memset(tp[:, :, :, :], 0.0))
            step.mark(dve.memset(x1[:, :, :], 0.0))
            step.mark(dve.memset(quarter[:, :], np.pi / 2))
            step(dve.memset(hs[:, :, :], 0.0))
            powers_by_b(0, 0, True)
            table(0)
            skip = h2[0:SN, :, :].rearrange("p g (t c) -> p g t c", c=SC)
            step(dve.tensor_tensor(skip, skip, drow[0:SN, :].rearrange("p (g c) -> p g c", c=SC).unsqueeze(2)
                                   .to_broadcast([SN, SG, ST, SC]), ALU.mult))
            PER = 2 + 5 + 3 + 2
            with dve.Fori(0, ROUNDS // 2 - 1) as i:
                step.enter(i, 2 * PER)
                for k in range(2):
                    run(i * 2 + k, k, (i * 2 + (k + 1), 1 - k))
                step.leave(ROUNDS // 2 - 1)
            run(ROUNDS - 2, 0, (ROUNDS - 1, 1))
            run(ROUNDS - 1, 1, None)

        @block.scalar
        def _(act):
            def prepare(n, par, first=False):
                if not first:
                    act.wait_ge(ended, n)
                act.activation(ub[:, par, :, :], u[:, bass.ds(n * SB, SB), :], ACT.Copy).then_inc(ub_copied, 1)
                act.wait_ge(landed[par], (n - par) * 8 + 16)
                act.activation(x1[:, :, :].rearrange("p d (g c) -> p d g c", c=(SB + 1) * SC)[:, :, :, 0:SC],
                               bc[:, par, 2, :, :].rearrange("p (d g) c -> p d g c", d=2), ACT.Copy,
                               scale=sign[:, 1:2]).then_inc(x1_made, 1)
                for half in range(2):
                    act.wait_ge(w1_turned, n * 2 + (half + 1))
                    act.activation(w1[:, half * SB:(half + 1) * SB, :], pA[:, half, :].rearrange("p (g s) -> p g s", s=P),
                                   ACT.Copy).then_inc(w1_copied, 1)
                act.wait_ge(tapped, n + 1)
                act.activation(taps[:, :], pK[:, 0:TAPS * SC], ACT.Copy).then_inc(taps_copied, 1)
                act.wait_ge(d_made, n + 1)
                act.activation(dm[:, par, :, :].rearrange("p g (t c) -> p t g c", c=SC),
                               pD[:, :].rearrange("p (t g c) -> p t g c", t=ST, c=SC), ACT.Copy).then_inc(d_copied, 1)
                act.wait_ge(ended, n + 1)
                act.activation(e[:, :, :], pE[:, :].rearrange("p (g c) -> p g c", c=SN), ACT.Copy).then_inc(e_copied, 1)
                act.wait_ge(tabled, n + 1)
                act.activation(sinT[:, :, :], th[:, :, :], ACT.Sin)
                act.activation(turns[:, :, :], th[:, :, :], ACT.Abs).then_inc(a_step, 1)
                act.wait_ge(a_step, n + 1)
                act.activation(cosT[:, :, :], turns[:, :, :], ACT.Sin, scale=-1.0, bias=quarter[:, 0:1]).then_inc(sined, 1)

            act.wait_ge(fixed, 80)
            act.wait_ge(v_step, 4)
            prepare_all(act, prepare)

        @block.tensor
        def _(pe):
            ident = core.mats["ident"]

            def turn(n):
                pe.wait_ge(powers, n * 2 + 2)
                for half in range(2):
                    t0 = 0 if half == 0 else ST - 1
                    for q in range(SB):
                        last = pe.transpose(pA[:, half, q * P:(q + 1) * P], tp[:, half * SB + q, t0:t0 + ST, :], ident[:, :])
                    last.then_inc(w1_turned, 1)

            def own(n, first=False):
                pe.wait_ge(x1_made, n + 1)
                for gd in range(GDN):
                    d, g = divmod(gd, SB)
                    last = pe.matmul(pK[:, 0:TAPS * SC], x1[:, d, g * SB * SC:(g + 1) * SB * SC], tp[:, gd, :, :],
                                     start=(gd == 0), stop=(gd == GDN - 1))
                last.then_inc(tapped, 1)
                if not first:
                    pe.wait_ge(d_copied, n)
                wait_apart(pe, taps_copied, n + 1, passed)
                for t in range(ST):
                    last = pe.transpose(pD[:, t * SB * SC:(t + 1) * SB * SC], taps[:, (ST - 1 - t) * SC:(TAPS - t) * SC],
                                        ident[0:SB * SC, 0:SB * SC])
                last.then_inc(d_made, 1)

            def ends(n, par):
                pe.wait_ge(ub_copied, n + 1)
                pe.wait_ge(w1_copied, n * 2 + 2)
                for d in range(2):
                    for g in range(SB):
                        last = pe.matmul(pE[:, (d * SB + g) * SN:(d * SB + g + 1) * SN], w1[:, d * SB + g, :],
                                         ub[:, par, g, :], start=True, stop=True)
                last.then_inc(ended, 1)

            def run(n, par, nxt):
                pe.wait_ge(e_copied, n + 1)
                pe.matmul(pS[:, 0, :], swap[:, :], e[:, :, :], start=True, stop=True).then_inc(swapped, 1)
                if nxt:
                    turn(nxt[0])
                pe.wait_ge(scanned, n * 2 + 2)
                pe.matmul(pS[:, 1, :], swap[:, :], gg[:, :, :], start=True, stop=True).then_inc(swapped2, 1)
                if nxt:
                    own(nxt[0])
                pe.wait_ge(h_ready, n * 2 + 2)
                pe.wait_ge(d_copied, n + 1)
                pe.wait_ge(w2_ready, n + 1)
                for g in range(SB):
                    y = pY[0:SN, g * P:(g + 1) * P]
                    pe.matmul(y, ub[:, par, g, :], dm[:, par, g, :], start=True, stop=False)
                    for d in range(2):
                        last = pe.matmul(y, hs[:, d * SB + g, d:d + SN], w2[:, par, d * SB + g, :, :],
                                         start=False, stop=(d == 1))
                last.then_inc(y_done, 1)
                if nxt:
                    ends(*nxt)

            turn(0)
            own(0, True)
            ends(0, 0)
            with pe.Fori(0, ROUNDS // 2 - 1) as i:
                for k in range(2):
                    run(i * 2 + k, k, (i * 2 + (k + 1), 1 - k))
            run(ROUNDS - 2, 0, (ROUNDS - 1, 1))
            run(ROUNDS - 1, 1, None)


def s5_from_chunks(core, z, zT):
    with Stage(core) as st:
        zt = st.sb("zt", [SN, ST, D])
        pt = st.ps("pt", [P, 4, 512])
        turned, copied, activated = (st.sem(n) for n in ("turned", "copied", "activated"))
        block = st.block()

        @block.scalar
        def _(act):
            for t in range(ST):
                act.activation(zt[0:SN, t, :].rearrange("p (g c) -> p g c", c=SC), z[0:SN, :, t * SC:(t + 1) * SC],
                               ACT.Gelu_apprx_tanh).then_inc(activated, 1)

        @block.tensor
        def _(pe):
            pe.wait_ge(activated, ST)
            for k in range(KT):
                if k >= 4:
                    pe.wait_ge(copied, k - 3)
                for t in range(ST):
                    last = pe.transpose(pt[:, k % 4, t * SN:(t + 1) * SN], zt[0:SN, t, k * P:(k + 1) * P],
                                        core.mats["ident"][0:SN, 0:SN])
                last.then_inc(turned, 1)

        @block.vector
        def _(dve):
            for k in range(KT):
                dve.wait_ge(turned, k + 1)
                dve.tensor_copy(zT[:, k, :].rearrange("p (c t) -> p t c", t=ST),
                                pt[:, k % 4, :].rearrange("p (t c) -> p t c", c=SN)).then_inc(copied, 1)


def second_mixer1(core, p):
    modulated_norm(core, 2)
    with Stage(core) as st:
        h2 = st.sb("h2", [SN, SG, P])
        with Stage(core) as st2:
            u = st2.sb("u", [P, SG, SN])
            s5_to_chunks(core, h2, u)
            s5_scan(core, h2, u, p.b, p.c, p.r8, p.th8)
        s5_from_chunks(core, h2, core.hT)
    with Stage(core) as st:
        gate = st.sb("gate", [P, KT, S])
        lin = st.sb("lin", [P, KT, S])
        linear(core, core.dram["w_glu_b"], KT, 512, 2, core.hT, tiles_to(gate, 4, ACT.Sigmoid))
        linear(core, core.dram["w_glu_a"], KT, 512, 2, core.hT, tiles_to(lin, 4))
        with Stage(core) as st2:
            v_step = st2.sem("v_step")
            block = st2.block()

            @block.vector
            def _(dve):
                step = Steps(dve, v_step)
                step(dve.tensor_tensor(gate[:, :, :], gate[:, :, :], lin[:, :, :], ALU.mult))
                at = gate_col(2)
                for k in range(KT):
                    dve.scalar_tensor_tensor(core.xT[:, k, :], gate[:, k, :], core.mod[:, at + k:at + k + 1],
                                             core.xT[:, k, :], ALU.mult, ALU.add)


def feed_forward_and_s5(core):
    with Stage(core) as st:
        p = Powers(st)
        feed_forward(core, 0, lambda core, st: s5_powers(core, st, p))
        second_mixer1(core, p)


def final_norm(core):
    norm(core, core.col("norm_f"), out=core.xT)


def lay_out_more(f, d):
    d["w_peer"] = by_chunks(f["peer_wq"][0], 512)
    d["sub_keys"] = f["peer_subkeys"][0].reshape(2 * PH, PN, P).transpose(2, 0, 1).reshape(P, -1)
    d["peer_u"], d["peer_v"] = f["peer_u"][0], f["peer_v"][0]
    d["pT"] = by_chunks(f["p"][0, 0].T, S)
    d["w_ple_gate"] = by_chunks(f["ple_gate"][0], 512)
    d["w_ple_proj"] = by_chunks(f["ple_proj"][0], 512)
    d["ada_w"] = f["ada_w_2"].transpose(0, 2, 1).reshape(-1, 2, P, D).transpose(0, 2, 1, 3).reshape(-1, 2 * D)
    d["c_row"] = f["c_2"].reshape(1, D)
    w = f["w_in_2"][0]
    for i, name in enumerate(("w2_val", "w2_gate")):
        d[name] = by_chunks(w[:, i * MA:(i + 1) * MA], 256)
    d["w2_qk"] = by_chunks(w[:, 2 * MA:4 * MA], 512)
    d["w2_v"] = by_chunks(w[:, 4 * MA:5 * MA], 256)
    d["w2_g"] = by_chunks(w[:, 5 * MA:], 256)
    d["w2_out"] = by_chunks(f["w_out_2"][0], 512)
    for i in range(2):
        d[f"w_fc1_{i}"] = by_chunks(f["w_fc1_2"][i], 512)
        w = f["w_fc2_2"][i].reshape(FF // D, D, 2, 512)
        d[f"w_fc2_{i}"] = np.concatenate([by_chunks(w[k, :, n], 512) for n in range(2) for k in range(FF // D)])
    d["w_glu_a"], d["w_glu_b"] = (by_chunks(f[n][0], 512) for n in ("w_glu_a_2", "w_glu_b_2"))
    d["s5_d"] = f["s5_d_2"]
    b = [f[n][0].transpose(2, 0, 1, 3) for n in ("s5_b_re_2", "s5_b_im_2")]
    c = [f[n][0].transpose(3, 0, 1, 2) for n in ("s5_c_re_2", "s5_c_im_2")]
    four = np.stack([np.concatenate(p, 0) for p in (b, b[::-1], c, c[::-1])], 1)
    d["s5_bc"] = (four.reshape(P, 4, 2, SG // SB, SB, SC).transpose(3, 0, 1, 2, 4, 5).reshape(SG // SB * P, -1))


def build(nc, dram, out):
    core = Core(nc, dram)
    with ExitStack() as ctx:
        def sb(name, shape):
            return ctx.enter_context(nc.sbuf_tensor(name, shape, F32))

        core.xT = sb("xT", [P, KT, S])
        core.hT = sb("hT", [P, KT, S])
        core.cols = sb("cols", [P, N_COLS])
        core.mats = {n: sb(n, [P, P]) for n in ("ident", "ones", "ones64", "rot_att")}
        core.mod, core.gain = sb("mod", [P, 12 * KT]), sb("gain", [P, 4 * KT])
        load_stage(core)
        for stage in STAGES:
            stage(core)
        with Stage(core) as st:
            written = st.sem("written")
            block = st.block()

            @block.sync
            def _(sp):
                sp.dma_start(out.rearrange("p (k s) -> p k s", k=KT), core.xT[:, :, :]).then_inc(written, 16)
                sp.wait_ge(written, 16)


def by_chunks(w, width):
    k, n = w.shape
    return np.ascontiguousarray(
        w.reshape(k // P, P, n // width, width).transpose(2, 1, 0, 3).reshape(-1, k // P * width))


def columns(v):
    return v.reshape(-1, P).T


def lay_out(a):
    f = {n: np.asarray(v) for n, v in a.items()}
    w_in, d = f["w_in"][0], {}
    d["xT"] = by_chunks(f["x"][0].T, S)
    o = np.cumsum([0, AH * AD, AKV * AD, AKV * AD, 512, 512, 512, 512, 512, 2048])
    part = [w_in[:, o[i]:o[i + 1]] for i in range(9)]
    pair = np.arange(AH).reshape(2, 4).T.reshape(-1)
    d["w_qk"] = by_chunks(np.concatenate([part[0].reshape(D, AH, AD)[:, pair].reshape(D, -1), part[1], part[2]], 1), 384)
    d["w_v"] = by_chunks(part[2], 64)
    d["w_hg_silu"] = by_chunks(np.concatenate([part[3], part[7]], 1), 512)
    d["w_hg_f"] = by_chunks(np.concatenate([part[4], part[5]], 1), 512)
    d["w_hg_v"] = by_chunks(part[6], 256)
    d["w_gates"] = by_chunks(part[8], 512)
    d["w_up_att"] = by_chunks(f["w_up_att"][0].reshape(AH, AD, D)[pair].reshape(-1, D), 512)
    d["w_up_hg"] = by_chunks(f["w_up_hg"][0], 512)
    d["w_out"] = by_chunks(f["w_out"][0], 512)
    twice = lambda v: np.concatenate([v, v], 0)
    by_rounds = lambda v: v.reshape(2, SG // SB, SB, -1).transpose(1, 0, 2, 3).reshape(2 * SG, -1)
    state_cols = lambda v: twice(by_rounds(v).T)
    cols = {
        "norm_mix": columns(f["norm_mix"]), "norm_ffn": columns(f["norm_ffn"]), "norm_ple": columns(f["norm_ple"]),
        "q_norm": twice(f["q_norm"].T), "k_norm": twice(f["k_norm"].T), "hg_out_norm": f["hg_out_norm"].T,
        "lb_raw": columns(f["hg_lb_raw"]), "norm_g": columns(f["norm_g_2"]), "ada_b": columns(f["ada_b_2"]),
        "conv_b": columns(f["conv_b_2"]), "cln_g": columns(f["cln_g_2"]), "cln_b": columns(f["cln_b_2"]),
        "conv_w": f["conv_w_2"][0].reshape(CW, 4, P).transpose(2, 1, 0).reshape(P, -1),
        "norm_f": columns(f["norm_f_2"]), "c": columns(f["c_2"]),
        "s5_lr": state_cols(f["s5_lam_re_2"]), "s5_li": state_cols(f["s5_lam_im_2"]),
        "s5_step": np.broadcast_to(by_rounds(f["s5_log_step_2"]).T, (P, 2 * SG)),
    }
    d["cols"] = np.ascontiguousarray(np.concatenate([cols[n] for n, _ in COLS], 1))
    lay_out_more(f, d)
    d["consts"] = constants()
    return {n: np.ascontiguousarray(v) for n, v in d.items()}


def kernel(**inputs):
    import concourse.bacc as bacc
    from concourse.bass_utils import run_bass_kernel_spmd

    nc = bacc.Bacc("TRN2", target_bir_lowering=False, num_devices=1)
    arrays = lay_out(inputs)
    dram = {n: nc.dram_tensor("in_" + n, v.shape, F32, kind="ExternalInput").ap() for n, v in arrays.items()}
    out = nc.dram_tensor("out", (P, KT * S), F32, kind="ExternalOutput").ap()
    build(nc, dram, out)
    r = run_bass_kernel_spmd(nc, [{"in_" + n: v for n, v in arrays.items()}], core_ids=[0])
    y = np.asarray(r.results[0]["out"]).reshape(P, KT, S)
    return np.ascontiguousarray(y.transpose(2, 1, 0).reshape(1, S, D))


STAGES = [first_mixer,peer,ple,second_mixer0,feed_forward_and_s5,feed_forward1,final_norm]
```
